# Optimizing a Trainium2 kernel written in Bass

```python
import math
import jax
import jax.numpy as jnp
from jax import lax
import numpy as np
import jax, jax.numpy as jnp

D_MODEL = 1024
BATCH = 1
SEQ = 512
DEPTH = 1

HEAD_DIM = 64
NSA_HEADS = 8
NSA_GROUPS = 2
NSA_REP = NSA_HEADS // NSA_GROUPS
CMP_BLOCK = 32
CMP_STRIDE = 16
CMP_HIDDEN = 256
SEL_BLOCK = 64
SEL_TOPK = 16
NSA_WINDOW = 512
NSA_QBLOCK = 128
SWA_HEADS = 8
SWA_KV_HEADS = 2
SWA_REP = SWA_HEADS // SWA_KV_HEADS
SWA_WINDOW = 128
SWA_QBLOCK = 128
D_FF = 4 * D_MODEL
NUM_BUCKETS = 32
MAX_DISTANCE = 1024
N_BIAS_HEADS = NSA_HEADS + SWA_HEADS
RMS_EPS = 1e-6

NSA_Q_DIM = NSA_HEADS * HEAD_DIM
NSA_KV_DIM = NSA_GROUPS * HEAD_DIM
SWA_Q_DIM = SWA_HEADS * HEAD_DIM
SWA_KV_DIM = SWA_KV_HEADS * HEAD_DIM
IN_SIZES = (NSA_Q_DIM,) + (NSA_KV_DIM,) * 6 + (3 * NSA_HEADS, SWA_Q_DIM, SWA_KV_DIM, SWA_KV_DIM, D_MODEL, D_MODEL)
IN_DIM = int(sum(IN_SIZES))
IN_OFFSETS = tuple(int(o) for o in np.cumsum(IN_SIZES)[:-1])


def rms_norm(x, g):
    xf = x.astype(jnp.float32)
    y = xf * lax.rsqrt(jnp.mean(xf * xf, axis=-1, keepdims=True) + RMS_EPS)
    return (y * g.astype(jnp.float32)).astype(x.dtype)

def t5_bucket(dist):
    max_exact = NUM_BUCKETS // 2
    d = jnp.maximum(dist, 0)
    df = jnp.maximum(d, 1).astype(jnp.float32)
    large = max_exact + (jnp.log(df / max_exact) / math.log(MAX_DISTANCE / max_exact)
                         * (NUM_BUCKETS - max_exact)).astype(jnp.int32)
    large = jnp.minimum(large, NUM_BUCKETS - 1)
    return jnp.where(d < max_exact, d, large)

def masked_softmax(s, mask):
    s = jnp.where(mask, s.astype(jnp.float32), -jnp.inf)
    m = jnp.max(s, axis=-1, keepdims=True)
    m = jnp.where(jnp.isfinite(m), m, 0.0)
    e = jnp.exp(s - m)
    return e / jnp.maximum(jnp.sum(e, axis=-1, keepdims=True), 1e-30)

def compress_kv(kv, pos, w1, w2):
    b, s, g, d = kv.shape
    n_cmp = (s - CMP_BLOCK) // CMP_STRIDE + 1
    kb = kv.reshape(b, s // CMP_STRIDE, CMP_STRIDE, g, d)
    blocks = jnp.concatenate([kb[:, o:o + n_cmp] for o in range(CMP_BLOCK // CMP_STRIDE)], axis=2)
    blocks = blocks + pos[None, None, :, None, :]
    flat = blocks.transpose(0, 1, 3, 2, 4).reshape(b, n_cmp, g, CMP_BLOCK * d)
    return jax.nn.gelu(flat @ w1) @ w2

def nsa_attention(q, kc, vc, k_slc, v_slc, k_win, v_win, gates, bias_tab):
    b, s, g, r, d = q.shape
    scale = d ** -0.5
    n_cmp = kc.shape[1]
    n_sel = s // SEL_BLOCK
    topk = min(SEL_TOPK, n_sel)
    n_chunks = s // NSA_QBLOCK
    ratio = SEL_BLOCK // CMP_STRIDE
    pad_front = CMP_BLOCK // CMP_STRIDE - 1
    pad_back = n_sel * ratio - n_cmp
    ks_blk = k_slc.reshape(b, n_sel, SEL_BLOCK, g, d).transpose(0, 3, 1, 2, 4)
    vs_blk = v_slc.reshape(b, n_sel, SEL_BLOCK, g, d).transpose(0, 3, 1, 2, 4)
    kw = jnp.pad(k_win, ((0, 0), (NSA_WINDOW, 0), (0, 0), (0, 0)))
    vw = jnp.pad(v_win, ((0, 0), (NSA_WINDOW, 0), (0, 0), (0, 0)))
    cmp_end = jnp.arange(n_cmp) * CMP_STRIDE + CMP_BLOCK - 1
    b_idx = jnp.arange(b)[:, None, None, None]
    g_idx = jnp.arange(g)[None, :, None, None]
    win_off = jnp.arange(NSA_QBLOCK + NSA_WINDOW) - NSA_WINDOW
    sel_off = jnp.arange(SEL_BLOCK)
    blk_ids = jnp.arange(n_sel)

    def chunk(args):
        qc, gc, ci = args
        t = ci * NSA_QBLOCK + jnp.arange(NSA_QBLOCK)
        sc = jnp.einsum('bqgrd,bngd->bgrqn', qc, kc).astype(jnp.float32) * scale
        pc = masked_softmax(sc, cmp_end[None, :] <= t[:, None])
        oc = jnp.einsum('bgrqn,bngd->bqgrd', pc.astype(vc.dtype), vc)
        pg = jnp.pad(pc.sum(axis=2), ((0, 0), (0, 0), (0, 0), (pad_front, pad_back)))
        ps = sum(pg[..., o:o + n_sel * ratio:ratio] for o in range(ratio + pad_front))
        cur = t // SEL_BLOCK
        valid = blk_ids[None, :] <= cur[:, None]
        forced = (blk_ids[None, :] == 0) | (blk_ids[None, :] == cur[:, None]) | (blk_ids[None, :] == cur[:, None] - 1)
        score = jnp.where(valid, jnp.where(forced, jnp.inf, ps), -jnp.inf)
        _, idx = lax.top_k(score, topk)
        kg = ks_blk[b_idx, g_idx, idx]
        vg = vs_blk[b_idx, g_idx, idx]
        pos = idx[..., None] * SEL_BLOCK + sel_off
        tq = t[None, None, :, None, None]
        bias_s = bias_tab[t5_bucket(tq - pos), g_idx[..., None]]
        ss = jnp.einsum('bqgrd,bgqjkd->bgrqjk', qc, kg).astype(jnp.float32) * scale + jnp.moveaxis(bias_s, -1, 2)
        n_keys = topk * SEL_BLOCK
        mask_s = (pos <= tq).reshape(b, g, 1, NSA_QBLOCK, n_keys)
        p_s = masked_softmax(ss.reshape(b, g, r, NSA_QBLOCK, n_keys), mask_s)
        o_s = jnp.einsum('bgrqn,bgqnd->bqgrd', p_s.astype(vg.dtype), vg.reshape(b, g, NSA_QBLOCK, n_keys, d))
        kwc = lax.dynamic_slice_in_dim(kw, ci * NSA_QBLOCK, NSA_QBLOCK + NSA_WINDOW, axis=1)
        vwc = lax.dynamic_slice_in_dim(vw, ci * NSA_QBLOCK, NSA_QBLOCK + NSA_WINDOW, axis=1)
        spos = ci * NSA_QBLOCK + win_off
        dist = t[:, None] - spos[None, :]
        mask_w = (dist >= 0) & (dist < NSA_WINDOW) & (spos[None, :] >= 0)
        bias_w = jnp.transpose(bias_tab[t5_bucket(dist)], (2, 3, 0, 1))
        sw = jnp.einsum('bqgrd,bkgd->bgrqk', qc, kwc).astype(jnp.float32) * scale + bias_w
        p_w = masked_softmax(sw, mask_w)
        o_w = jnp.einsum('bgrqk,bkgd->bqgrd', p_w.astype(vwc.dtype), vwc)
        gs = jax.nn.sigmoid(gc.astype(jnp.float32)).astype(qc.dtype)
        return gs[..., 0:1] * oc + gs[..., 1:2] * o_s + gs[..., 2:3] * o_w

    q_ch = q.reshape(b, n_chunks, NSA_QBLOCK, g, r, d).swapaxes(0, 1)
    g_ch = gates.reshape(b, n_chunks, NSA_QBLOCK, g, r, 3).swapaxes(0, 1)
    out = lax.map(chunk, (q_ch, g_ch, jnp.arange(n_chunks)))
    return out.swapaxes(0, 1).reshape(b, s, g * r * d)

def swa_sink_attention(q, k, v, sinks, bias_tab):
    b, s, g, r, d = q.shape
    scale = d ** -0.5
    nb = s // SWA_QBLOCK
    qb = q.reshape(b, nb, SWA_QBLOCK, g, r, d)
    kb = k.reshape(b, nb, SWA_QBLOCK, g, d)
    vb = v.reshape(b, nb, SWA_QBLOCK, g, d)
    pad = ((0, 0), (1, 0), (0, 0), (0, 0), (0, 0))
    kk = jnp.concatenate([jnp.pad(kb, pad)[:, :-1], kb], axis=2)
    vv = jnp.concatenate([jnp.pad(vb, pad)[:, :-1], vb], axis=2)
    qi = jnp.arange(SWA_QBLOCK)[:, None]
    ki = jnp.arange(2 * SWA_QBLOCK)[None, :]
    dist = qi - ki + SWA_QBLOCK
    band = (dist >= 0) & (dist < SWA_WINDOW)
    first = (jnp.arange(nb) > 0)[:, None, None] | (ki >= SWA_QBLOCK)[None]
    mask = (band[None] & first)[None, :, None, None]
    bias = jnp.transpose(bias_tab[t5_bucket(dist)], (2, 3, 0, 1))
    sc = jnp.einsum('bnqgrd,bnkgd->bngrqk', qb, kk).astype(jnp.float32) * scale + bias
    sc = jnp.where(mask, sc, -jnp.inf)
    sink = sinks.astype(jnp.float32)[None, None, :, :, None, None]
    m = jnp.maximum(jnp.max(sc, axis=-1, keepdims=True), sink)
    e = jnp.exp(sc - m)
    p = e / (jnp.sum(e, axis=-1, keepdims=True) + jnp.exp(sink - m))
    o = jnp.einsum('bngrqk,bnkgd->bnqgrd', p.astype(vv.dtype), vv)
    return o.reshape(b, s, g * r * d)

def first_inputs(seed: int = 0) -> dict:
    key = jax.random.key(seed)
    ks = jax.random.split(key, 20)
    nrm = lambda k, shape, scale: jax.random.normal(k, shape, jnp.float32) * scale
    gain = lambda k: 1.0 + nrm(k, (DEPTH, D_MODEL), 0.05)
    cin = CMP_BLOCK * HEAD_DIM
    return {
        'x': nrm(ks[0], (BATCH, SEQ, D_MODEL), 1.0),
        'norm_mix_pre': gain(ks[1]),
        'norm_mix_post': gain(ks[2]),
        'norm_mlp_pre': gain(ks[3]),
        'norm_mlp_post': gain(ks[4]),
        'w_in': nrm(ks[5], (DEPTH, D_MODEL, IN_DIM), D_MODEL ** -0.5),
        'cmp_pos_k': nrm(ks[6], (DEPTH, CMP_BLOCK, HEAD_DIM), 0.5),
        'cmp_w1_k': nrm(ks[7], (DEPTH, cin, CMP_HIDDEN), cin ** -0.5),
        'cmp_w2_k': nrm(ks[8], (DEPTH, CMP_HIDDEN, HEAD_DIM), CMP_HIDDEN ** -0.5),
        'cmp_pos_v': nrm(ks[9], (DEPTH, CMP_BLOCK, HEAD_DIM), 0.5),
        'cmp_w1_v': nrm(ks[10], (DEPTH, cin, CMP_HIDDEN), cin ** -0.5),
        'cmp_w2_v': nrm(ks[11], (DEPTH, CMP_HIDDEN, HEAD_DIM), CMP_HIDDEN ** -0.5),
        'attn_sinks': nrm(ks[12], (DEPTH, SWA_HEADS), 0.5),
        'rel_bias': nrm(ks[13], (NUM_BUCKETS, N_BIAS_HEADS), 0.5),
        'w_up_nsa': nrm(ks[14], (DEPTH, NSA_Q_DIM, D_MODEL), NSA_Q_DIM ** -0.5),
        'w_up_swa': nrm(ks[15], (DEPTH, SWA_Q_DIM, D_MODEL), SWA_Q_DIM ** -0.5),
        'w_out': nrm(ks[16], (DEPTH, D_MODEL, D_MODEL), D_MODEL ** -0.5),
        'w_mlp_in': nrm(ks[17], (DEPTH, D_MODEL, D_FF), D_MODEL ** -0.5),
        'w_mlp_out': nrm(ks[18], (DEPTH, D_FF, D_MODEL), D_FF ** -0.5),
    }

def first_block(x, norm_mix_pre, norm_mix_post, norm_mlp_pre, norm_mlp_post, w_in,
              cmp_pos_k, cmp_w1_k, cmp_w2_k, cmp_pos_v, cmp_w1_v, cmp_w2_v,
              attn_sinks, rel_bias, w_up_nsa, w_up_swa, w_out, w_mlp_in, w_mlp_out):
    b, s, _ = x.shape
    bias_nsa = rel_bias[:, :NSA_HEADS].reshape(NUM_BUCKETS, NSA_GROUPS, NSA_REP)
    bias_swa = rel_bias[:, NSA_HEADS:].reshape(NUM_BUCKETS, SWA_KV_HEADS, SWA_REP)
    h = x
    for l in range(DEPTH):
        u = rms_norm(h, norm_mix_pre[l])
        (q_n, kc_n, vc_n, ks_n, vs_n, kw_n, vw_n, g_n,
         q_s, k_s, v_s, gate_a, gate_b) = jnp.split(u @ w_in[l], IN_OFFSETS, axis=-1)
        kvr = lambda t_: t_.reshape(b, s, NSA_GROUPS, HEAD_DIM)
        kc = compress_kv(kvr(kc_n), cmp_pos_k[l], cmp_w1_k[l], cmp_w2_k[l])
        vc = compress_kv(kvr(vc_n), cmp_pos_v[l], cmp_w1_v[l], cmp_w2_v[l])
        o_a = nsa_attention(q_n.reshape(b, s, NSA_GROUPS, NSA_REP, HEAD_DIM), kc, vc,
                            kvr(ks_n), kvr(vs_n), kvr(kw_n), kvr(vw_n),
                            g_n.reshape(b, s, NSA_GROUPS, NSA_REP, 3), bias_nsa)
        o_b = swa_sink_attention(q_s.reshape(b, s, SWA_KV_HEADS, SWA_REP, HEAD_DIM),
                                 k_s.reshape(b, s, SWA_KV_HEADS, HEAD_DIM),
                                 v_s.reshape(b, s, SWA_KV_HEADS, HEAD_DIM),
                                 attn_sinks[l].reshape(SWA_KV_HEADS, SWA_REP), bias_swa)
        y = jax.nn.sigmoid(gate_a) * (o_a @ w_up_nsa[l]) + jax.nn.sigmoid(gate_b) * (o_b @ w_up_swa[l])
        h = h + rms_norm(y @ w_out[l], norm_mix_post[l])
        u = rms_norm(h, norm_mlp_pre[l])
        f = jnp.square(jax.nn.relu(u @ w_mlp_in[l])) @ w_mlp_out[l]
        h = h + rms_norm(f, norm_mlp_post[l])
    return h


DEPTH_2 = 2

GRID_W = 64
CTX_LEN = 256
A_HEADS = D_MODEL // (2 * HEAD_DIM)
A_WIDTH = A_HEADS * 2 * HEAD_DIM
A_IN_WIDTH = 4 * A_WIDTH
B_HEADS = D_MODEL // HEAD_DIM
B_KV_HEADS = 4
B_GROUP = B_HEADS // B_KV_HEADS
B_WIDTH = B_HEADS * HEAD_DIM
B_KV_WIDTH = B_KV_HEADS * HEAD_DIM
B_IN_WIDTH = 2 * B_WIDTH + 2 * B_KV_WIDTH
MIX_WIDTH = A_WIDTH
WINDOW = 128
Q_BLOCK = 128
BAND = Q_BLOCK + 2 * WINDOW
ROPE_THETA = 10000.0
NORM_EPS = 1e-6
SUBLN_EPS = 1e-5
NEG_INF = -1e30
ATTN_SCALE = HEAD_DIM ** -0.5
N_A_LAYERS = (DEPTH_2 + 1) // 2
N_B_LAYERS = DEPTH_2 // 2


def rms_norm_2(x, g, eps=NORM_EPS):
    x32 = x.astype(jnp.float32)
    y = x32 * lax.rsqrt(jnp.mean(x32 * x32, axis=-1, keepdims=True) + eps)
    return (y * g.astype(jnp.float32)).astype(x.dtype)

def modulate(h, shift, scale):
    return h * (1.0 + scale) + shift

def axial_angles(rows, rot_dim=HEAD_DIM):
    row = jnp.repeat(jnp.arange(rows, dtype=jnp.int32), GRID_W).astype(jnp.float32)
    col = jnp.tile(jnp.arange(GRID_W, dtype=jnp.int32), rows).astype(jnp.float32)
    axis_dim = rot_dim // 2
    inv_freq = ROPE_THETA ** (-jnp.arange(0, axis_dim, 2, dtype=jnp.float32) / axis_dim)
    return row[:, None] * inv_freq, col[:, None] * inv_freq

def rope_1d(x, ang):
    ang = ang.reshape(ang.shape[:1] + (1,) * (x.ndim - 3) + ang.shape[1:])
    cos, sin = jnp.cos(ang), jnp.sin(ang)
    x1, x2 = jnp.split(x.astype(jnp.float32), 2, axis=-1)
    return jnp.concatenate([x1 * cos - x2 * sin, x2 * cos + x1 * sin], axis=-1).astype(x.dtype)

def rope_axial(x, ang_r, ang_c):
    xr, xc = jnp.split(x, 2, axis=-1)
    return jnp.concatenate([rope_1d(xr, ang_r), rope_1d(xc, ang_c)], axis=-1)

def diff_attention_mixer(hx, hc, w_in, lq1, lk1, lq2, lk2, subln_g, layer_idx, with_ctx_out, ang_r, ang_c):
    B, S, _ = hx.shape
    nblk = S // Q_BLOCK
    lam_init = 0.8 - 0.6 * math.exp(-0.3 * layer_idx)
    f32 = jnp.float32
    lam = (jnp.exp(jnp.sum(lq1.astype(f32) * lk1.astype(f32)))
           - jnp.exp(jnp.sum(lq2.astype(f32) * lk2.astype(f32))) + lam_init)

    def split(p):
        q, k, v, g = jnp.split(p, [A_WIDTH, 2 * A_WIDTH, 3 * A_WIDTH], axis=-1)
        lead = p.shape[:2]
        return (q.reshape(lead + (A_HEADS, 2, HEAD_DIM)),
                k.reshape(lead + (A_HEADS, 2, HEAD_DIM)),
                v.reshape(lead + (A_HEADS, 2 * HEAD_DIM)), g)

    qx, kx, vx, gx = split(hx @ w_in)
    qc, kc, vc, gc = split(hc @ w_in)
    qx = rope_axial(qx, ang_r, ang_c)
    kx = rope_axial(kx, ang_r, ang_c)
    k_all = jnp.concatenate([kc, kx], axis=1)
    v_all = jnp.concatenate([vc, vx], axis=1)

    def attend(qb, keys, vals):
        s = jnp.einsum('bqhmd,bkhmd->bhmqk', qb, keys).astype(f32) * ATTN_SCALE
        p = jax.nn.softmax(s, axis=-1)
        a = p[:, :, 0] - lam * p[:, :, 1]
        return jnp.einsum('bhqk,bkhe->bqhe', a.astype(vals.dtype), vals)

    q_blocks = qx.reshape(B, nblk, Q_BLOCK, A_HEADS, 2, HEAD_DIM).swapaxes(0, 1)
    ox = lax.map(lambda qb: attend(qb, k_all, v_all), q_blocks)
    ox = ox.swapaxes(0, 1).reshape(B, S, A_HEADS, 2 * HEAD_DIM)

    def finish(o, g):
        o = rms_norm_2(o, subln_g, SUBLN_EPS) * (1.0 - lam_init)
        return o.reshape(o.shape[:2] + (A_WIDTH,)) * jax.nn.silu(g)

    out_x = finish(ox, gx)
    out_c = finish(attend(qc, kc, vc), gc) if with_ctx_out else None
    return out_x, out_c

def window_gqa_mixer(hx, hc, w_in, sink, with_ctx_out, ang_r, ang_c):
    B, S, _ = hx.shape
    nblk = S // Q_BLOCK
    f32 = jnp.float32

    def split(p):
        q, k, v, g = jnp.split(p, [B_WIDTH, B_WIDTH + B_KV_WIDTH, B_WIDTH + 2 * B_KV_WIDTH], axis=-1)
        lead = p.shape[:2]
        return (q.reshape(lead + (B_KV_HEADS, B_GROUP, HEAD_DIM)),
                k.reshape(lead + (B_KV_HEADS, HEAD_DIM)),
                v.reshape(lead + (B_KV_HEADS, HEAD_DIM)), g)

    qx, kx, vx, gx = split(hx @ w_in)
    qc, kc, vc, gc = split(hc @ w_in)
    qx = rope_axial(qx, ang_r, ang_c)
    kx = rope_axial(kx, ang_r, ang_c)
    n_ctx = kc.shape[1]
    sink_f = sink.astype(f32).reshape(B_KV_HEADS, B_GROUP)[None, :, :, None, None]

    def sink_softmax(s):
        sb = jnp.broadcast_to(sink_f, s.shape[:-1] + (1,))
        return jax.nn.softmax(jnp.concatenate([s, sb], axis=-1), axis=-1)[..., :-1]

    pad = ((0, 0), (WINDOW, WINDOW), (0, 0), (0, 0))
    kp = jnp.pad(kx, pad)
    vp = jnp.pad(vx, pad)
    q_blocks = qx.reshape(B, nblk, Q_BLOCK, B_KV_HEADS, B_GROUP, HEAD_DIM).swapaxes(0, 1)

    def block(args):
        qb, i = args
        start = i * Q_BLOCK
        kb = lax.dynamic_slice_in_dim(kp, start, BAND, axis=1)
        vb = lax.dynamic_slice_in_dim(vp, start, BAND, axis=1)
        qpos = start + jnp.arange(Q_BLOCK)
        kpos = start - WINDOW + jnp.arange(BAND)
        mask = ((jnp.abs(qpos[:, None] - kpos[None, :]) <= WINDOW)
                & (kpos >= 0)[None, :] & (kpos < S)[None, :])
        s_band = jnp.einsum('bqhgd,bjhd->bhgqj', qb, kb).astype(f32) * ATTN_SCALE
        s_band = jnp.where(mask, s_band, NEG_INF)
        s_ctx = jnp.einsum('bqhgd,bjhd->bhgqj', qb, kc).astype(f32) * ATTN_SCALE
        p = sink_softmax(jnp.concatenate([s_ctx, s_band], axis=-1)).astype(vb.dtype)
        return (jnp.einsum('bhgqj,bjhd->bqhgd', p[..., :n_ctx], vc)
                + jnp.einsum('bhgqj,bjhd->bqhgd', p[..., n_ctx:], vb))

    ox = lax.map(block, (q_blocks, jnp.arange(nblk)))
    out_x = ox.swapaxes(0, 1).reshape(B, S, B_WIDTH) * jax.nn.silu(gx)
    out_c = None
    if with_ctx_out:
        s = jnp.einsum('bqhgd,bjhd->bhgqj', qc, kc).astype(f32) * ATTN_SCALE
        p = sink_softmax(s).astype(vc.dtype)
        oc = jnp.einsum('bhgqj,bjhd->bqhgd', p, vc)
        out_c = oc.reshape(oc.shape[:2] + (B_WIDTH,)) * jax.nn.silu(gc)
    return out_x, out_c

def second_inputs(seed: int = 0) -> dict:
    key = jax.random.key(seed)
    ks = jax.random.split(key, 17)
    nrm = jax.random.normal
    f32 = jnp.float32
    return {
        'x': nrm(ks[0], (BATCH, SEQ, D_MODEL), f32),
        'c': nrm(ks[1], (BATCH, D_MODEL), f32),
        'ctx': nrm(ks[2], (BATCH, CTX_LEN, D_MODEL), f32),
        'c_ctx': nrm(ks[3], (D_MODEL,), f32),
        'w_mod': nrm(ks[4], (DEPTH_2, D_MODEL, 3 * D_MODEL), f32) * D_MODEL ** -0.5,
        'b_mod': 0.01 * nrm(ks[5], (DEPTH_2, 3 * D_MODEL), f32),
        'norm_g': 1.0 + 0.02 * nrm(ks[6], (DEPTH_2, D_MODEL), f32),
        'w_o': nrm(ks[7], (DEPTH_2, MIX_WIDTH, D_MODEL), f32) * MIX_WIDTH ** -0.5,
        'a_w_in': nrm(ks[8], (N_A_LAYERS, D_MODEL, A_IN_WIDTH), f32) * D_MODEL ** -0.5,
        'a_lambda_q1': 0.1 * nrm(ks[9], (N_A_LAYERS, HEAD_DIM), f32),
        'a_lambda_k1': 0.1 * nrm(ks[10], (N_A_LAYERS, HEAD_DIM), f32),
        'a_lambda_q2': 0.1 * nrm(ks[11], (N_A_LAYERS, HEAD_DIM), f32),
        'a_lambda_k2': 0.1 * nrm(ks[12], (N_A_LAYERS, HEAD_DIM), f32),
        'a_subln_g': 1.0 + 0.02 * nrm(ks[13], (N_A_LAYERS, 2 * HEAD_DIM), f32),
        'b_w_in': nrm(ks[14], (N_B_LAYERS, D_MODEL, B_IN_WIDTH), f32) * D_MODEL ** -0.5,
        'b_sink': 0.5 * nrm(ks[15], (N_B_LAYERS, B_HEADS), f32),
        'final_g': 1.0 + 0.02 * nrm(ks[16], (D_MODEL,), f32),
    }

def second_block(x, c, ctx, c_ctx, w_mod, b_mod, norm_g, w_o, a_w_in, a_lambda_q1, a_lambda_k1,
              a_lambda_q2, a_lambda_k2, a_subln_g, b_w_in, b_sink, final_g):
    n_tokens = x.shape[1]
    rows = n_tokens // GRID_W
    ang_r, ang_c = axial_angles(rows)
    sc = jax.nn.silu(c)
    sctx = jax.nn.silu(c_ctx)
    for i in range(DEPTH_2):
        last = i == DEPTH_2 - 1
        shift_x, scale_x, gate_x = jnp.split(sc @ w_mod[i] + b_mod[i], 3, axis=-1)
        shift_c, scale_c, gate_c = jnp.split(sctx @ w_mod[i] + b_mod[i], 3, axis=-1)
        hx = modulate(rms_norm_2(x, norm_g[i]), shift_x[:, None], scale_x[:, None])
        hc = modulate(rms_norm_2(ctx, norm_g[i]), shift_c, scale_c)
        j = i // 2
        if i % 2 == 0:
            ox, oc = diff_attention_mixer(hx, hc, a_w_in[j], a_lambda_q1[j], a_lambda_k1[j],
                                          a_lambda_q2[j], a_lambda_k2[j], a_subln_g[j], i,
                                          not last, ang_r, ang_c)
        else:
            ox, oc = window_gqa_mixer(hx, hc, b_w_in[j], b_sink[j], not last, ang_r, ang_c)
        x = x + gate_x[:, None] * (ox @ w_o[i])
        if not last:
            ctx = ctx + gate_c * (oc @ w_o[i])
    return rms_norm_2(x, final_g)


def setup_inputs(seed=0):
    out = dict(first_inputs(seed))
    for name, value in second_inputs(seed + 1).items():
        if name != "x":
            out[name + "_2"] = value
    return out


def reference(
    x, norm_mix_pre, norm_mix_post, norm_mlp_pre, norm_mlp_post, w_in, cmp_pos_k, cmp_w1_k,
    cmp_w2_k, cmp_pos_v, cmp_w1_v, cmp_w2_v, attn_sinks, rel_bias, w_up_nsa, w_up_swa, w_out,
    w_mlp_in, w_mlp_out, c_2, ctx_2, c_ctx_2, w_mod_2, b_mod_2, norm_g_2, w_o_2, a_w_in_2,
    a_lambda_q1_2, a_lambda_k1_2, a_lambda_q2_2, a_lambda_k2_2, a_subln_g_2, b_w_in_2, b_sink_2,
    final_g_2,
):
    x = first_block(
        x, norm_mix_pre, norm_mix_post, norm_mlp_pre, norm_mlp_post, w_in, cmp_pos_k, cmp_w1_k,
        cmp_w2_k, cmp_pos_v, cmp_w1_v, cmp_w2_v, attn_sinks, rel_bias, w_up_nsa, w_up_swa,
        w_out, w_mlp_in, w_mlp_out,
    )
    return second_block(
        x, c_2, ctx_2, c_ctx_2, w_mod_2, b_mod_2, norm_g_2, w_o_2, a_w_in_2, a_lambda_q1_2,
        a_lambda_k1_2, a_lambda_q2_2, a_lambda_k2_2, a_subln_g_2, b_w_in_2, b_sink_2, final_g_2,
    )


_drawn_inputs = setup_inputs


def setup_inputs(seed=0):
    import zlib

    import numpy as np

    out = dict(_drawn_inputs(seed))
    spreads = {}
    factors = {'attn_sinks': 8.0,
     'b_mod_2': 7.546,
     'norm_g_2': 7.92,
     'a_lambda_q1_2': 8.0,
     'a_lambda_k1_2': 200.0,
     'a_lambda_q2_2': 3.334,
     'a_lambda_k2_2': 2.982,
     'a_subln_g_2': 8.0,
     'b_sink_2': 8.0,
     'final_g_2': 20.784}
    for name, (base, spread) in spreads.items():
        noise = np.random.default_rng([zlib.crc32(name.encode()), seed]).standard_normal(out[name].shape)
        drawn = base * np.exp(spread * noise) if base else spread * noise
        out[name] = jnp.asarray(drawn.astype(out[name].dtype))
    for name, factor in factors.items():
        out[name] = (out[name] * factor).astype(out[name].dtype)
    return out
```

```python
from contextlib import ExitStack

import concourse.bass as bass
from concourse import mybir

F32 = mybir.dt.float32
F32R = mybir.dt.float32r
ALU = mybir.AluOpType
ACT = mybir.ActivationFunctionType
AX = mybir.AxisListType

P = 128
D = 1024
KT = D // P
S = 512
C = 256
SC = S + C
QT = S // P
HD = 64
REP = 4
NCMP = 31
HID = 256
EPS = 1e-6
SUB_EPS = 1e-5
LAM_INIT = 0.8 - 0.6
BIG = 1e30
GELU_C = 0.7978845608028654
RAW = 4
MRAW = 4
SPL = 2
BUCKETS = 32
TBL = 640

N_ATT = 25
N_UP = 24
N_OUT = 8
N_MLP = 64
N_MOD = 48
N_A = 32
N_B = 20
U_ATT = 0
U_UP = U_ATT + N_ATT
U_OUT = U_UP + N_UP
U_MLP = U_OUT + N_OUT
U_A = U_MLP + N_MLP
U_AO = U_A + N_A
U_B = U_AO + N_OUT
U_BO = U_B + N_B
U_END = U_BO + N_OUT

G_MIX_PRE, G_MIX_POST, G_MLP_PRE, G_MLP_POST, G_A, G_B, G_FINAL = range(7)
SHUFFLE = [(i + 16) % 32 for i in range(32)]


def build(nc, t, out):
    base = 16512
    KB = 1024
    with ExitStack() as ctx:
        def at(name, kb, shape, dt=F32):
            return nc.alloc_sbuf_tensor_at(name, shape, dt, offset=base + int(kb * KB))

        def sem(name):
            return ctx.enter_context(nc.semaphore(name))

        raw = at("raw", 0, [P, RAW, KT, P])
        w_h = at("w_h", 16, [P, SPL, KT, P], F32R)
        w_l = at("w_l", 24, [P, SPL, KT, P], F32R)
        x1h = at("x1h", 32, [P, KT, S], F32R)
        x1l = at("x1l", 48, [P, KT, S], F32R)
        x2h = at("x2h", 32, [P, KT, SC], F32R)
        x2l = at("x2l", 56, [P, KT, SC], F32R)
        hc = at("hc", 80, [P, KT, SC])
        c0 = 104
        ident = at("ident", c0, [P, P])
        ones = at("ones", c0 + 0.5, [P, P])
        small = at("small", c0 + 1, [P, 896])
        rstd = at("rstd", c0 + 4.5, [P, SC])
        sq = at("sq", c0 + 7.5, [P, 2, SC])
        sqsum = at("sqsum", c0 + 13.5, [P, SC])
        z = c0 + 16.5

        o_ = [0]

        def sm(n):
            a = small[:, o_[0]:o_[0] + n]
            o_[0] += n
            return a
        gains = sm(56).rearrange("p (g k) -> p g k", g=7)
        bmod = sm(48)
        cin = sm(16)
        ct = sm(16)
        cs = sm(16)
        mod = sm(96).rearrange("p (c v) -> p c v", v=2)
        sinks = sm(24)
        nsinks = sm(24)
        lamv = sm(4)
        lamp = sm(2)
        lame = sm(2)
        lam = sm(1)
        subg = sm(1)
        subs = sm(1)
        eps_t = sm(1)
        seps_t = sm(1)
        negm = sm(8)
        sums = sm(8)
        rs = sm(8)
        wgt = sm(8)
        esk = sm(8)
        spare = sm(1)
        mulx = sm(32).rearrange("p (l v k) -> p l v k", l=2, v=2)
        assert o_[0] <= 896

        q_n = at("q_n", 64, [P, REP, S])
        q_s = at("q_s", 72, [P, REP, S])
        k_all = at("k_all", 80, [P, 3, S])
        v_all = at("v_all", 86, [P, 3, QT, P])
        gate = at("gate", 92, [P, QT, P])
        strip_s = at("strip_s", 94, [P, 8, 256])
        kcmp = at("kcmp", 102, [P, 32])
        vcmp = at("vcmp", 102.25, [P, 2, HD])
        cmask = at("cmask", 102.75, [P, QT, NCMP])
        strip_n = at("strip_n", z, [P, 8, S])
        sb1 = [at("sb1_0", z + 16, [P, REP, S]), at("sb1_1", z + 24, [P, REP, S]), at("sb1_2", z + 72, [P, REP, S])]
        vT = at("vT", z + 32, [P, 4, S])
        pt1 = at("pt1", z + 32, [P, 4, S])
        o1h = at("o1h", z + 40, [P, 8, S], F32R)
        o1l = at("o1l", z + 56, [P, 8, S], F32R)
        xin = at("xin", z + 40, [P, KT, S])
        xn = at("xn", z + 56, [P, 2, SC])
        FW = 3 * 256 + 8
        fh = at("fh", z + 16, [P, 2, FW], F32R)
        fl = at("fl", z + 16 + 6.25, [P, 2, FW], F32R)
        g0 = z + 72
        hid = at("hid", g0, [P, 4, 2 * NCMP])
        gl1 = at("gl1", g0 + 1, [P, 4, 2 * NCMP])
        gl2 = at("gl2", g0 + 2, [P, 4, 2 * NCMP])
        gl3 = at("gl3", g0 + 3, [P, 4, 2 * NCMP])
        hbias = at("hbias", g0 + 4, [P, 4])
        w2 = at("w2", g0 + 4.25, [P, 2, 2, HD])
        pos = at("pos", g0 + 5.25, [P, 2, 16])
        brow = at("brow", g0 + 5.5, [16, TBL])
        onehot = at("onehot", g0 + 8, [34, TBL])
        blhs = at("blhs", g0 + 10.5, [34, 16])
        y1h = at("y1h", z, [P, 8, S], F32R)
        y1l = at("y1l", z + 16, [P, 8, S], F32R)
        tg = at("tg", z + 72, [P, 2, 2, S])
        ty = at("ty", z + 80, [P, 2, S])
        f_t = at("f_t", z + 32, [P, KT, S])
        m_h = at("m_h", z, [P, 8, S], F32R)
        m_l = at("m_l", z + 16, [P, 8, S], F32R)
        relu = at("relu", z + 48, [P, 2, S])
        msq = at("msq", z + 52, [P, 2, S])
        mraw = at("mraw", z + 70, [P, MRAW, KT, P])
        xn2 = at("xn2", z + 64, [P, 2, SC])
        o2h = at("o2h", z, [P, KT, SC], F32R)
        o2l = at("o2l", z + 24, [P, KT, SC], F32R)
        a_q = at("a_q", z + 48, [P, SC])
        a_k = at("a_k", z + 51, [P, SC])
        a_g = at("a_g", z + 54, [P, SC])
        cos_t = at("cos_t", z + 57, [P, S])
        sin_t = at("sin_t", z + 59, [P, S])
        a_p0 = at("a_p0", z + 61, [P, 2, SC])
        a_vT = at("a_vT", z + 61, [P, SC])
        a_p1 = at("a_p1", z + 67, [P, 2, SC])
        a_pt = at("a_pt", z + 73, [P, 6, S])
        ropea = at("ropea", z + 73, [P, 3, S])
        a_pt2 = at("a_pt2", c0 + 7.5, [P, 2, C])
        a_v = at("a_v", c0 + 13.5, [P, 6, P])
        a_p = [a_p0, a_p1]
        b_q = at("b_q", z, [P, 8, S])
        b_k = at("b_k", z + 16, [P, 2, SC])
        b_v = at("b_v", z + 22, [P, 6, 256])
        b_g = at("b_g", z + 28, [P, 8, S])
        bm0 = at("bm0", z + 44, [P, 512])
        bm1 = at("bm1", z + 46, [P, 640])
        b_pt = at("b_pt", z + 48.5, [P, 4, S])
        ropeb = at("ropeb", z + 48.5, [P, 3, S])
        b_sb = [at("b_sb0", z + 60.5, [P, REP, 640]), at("b_sb1", z + 70.5, [P, REP, 640]),
                at("b_sb2", 64, [P, REP, 640])]
        b_vT = at("b_vT", z + 64, [P, 2, SC])
        ot = at("ot", z + 80.5, [P, S])
        xo = at("xo", z, [P, KT, S])

        ps = ctx.enter_context(nc.psum_tensor("ps", [P, 8, 512], F32))

        def pair(n):
            return ps[:, 2 * n:2 * n + 2].rearrange("p b c -> p (b c)")

        dbias = nc.dram_tensor("dbias", [16, P, TBL], F32, kind="Internal").ap()

        raw_in = [sem(f"raw_in{i}") for i in range(RAW)]
        w_hi = sem("w_hi")
        w_lo = sem("w_lo")
        unit = sem("unit")
        const_in = sem("const_in")
        boot = sem("boot")
        brow_ok = sem("brow_ok")
        dbias_in = sem("dbias_in")
        strips_in = sem("strips_in")
        x_in = sem("x_in")
        tab_in = sem("tab_in")
        ctx_in = sem("ctx_in")
        out_done = sem("out_done")
        v_self = sem("v_self")

        block = ctx.enter_context(nc.Block())

        PHASES = ["prep", "nsa", "up", "wout", "norm2", "mlp", "norm3", "heads", "ao", "norm4", "bqkv", "battn"]
        phase_end = sem("phase_end")

        def end_phase(eng, name):
            eng.drain().then_inc(phase_end, 1)

        def begin_after(eng, name):
            eng.wait_ge(phase_end, 3 * (PHASES.index(name) + 1))

        class Own:
            n = 0

        def done(ins):
            Own.n += 1
            ins.then_inc(v_self, 1)

        def settle(v):
            v.wait_ge(v_self, Own.n)

        def split_high(act, u, i=None, step=0):
            if u >= U_END and i is None:
                return
            v = lambda c: c if i is None else i * step + c
            assert step % RAW == 0
            act.wait_ge(raw_in[u % RAW], 16 * (u // RAW + 1) if i is None else i * (16 * step // RAW) + 16 * (u // RAW + 1))
            if u >= SPL:
                act.wait_ge(unit, v(u - SPL + 1))
            nc.scalar.activation(w_h[:, u % SPL], raw[:, u % RAW], ACT.Copy).then_inc(w_hi, 1)

        def load_unit(sp, u, src, i=None, step=0):
            if u >= RAW:
                sp.wait_ge(w_lo, u - RAW + 1 if i is None else i * step + (u - RAW + 1))
            sp.dma_start(raw[:, u % RAW], src).then_inc(raw_in[u % RAW], 16)

        def products(u, parts, k0=0, k1=KT, first=True, last=True):
            for k in range(k0, k1):
                for wi, w in ((0, w_h), (1, w_l)):
                    for o, xh, xl in parts:
                        mm = nc.tensor.matmul(o, w[:, u % SPL, k], xh(k), start=(first and k == k0 and wi == 0),
                                              stop=(last and k == k1 - 1 and wi == 1))
                    if wi == 0:
                        for o, xh, xl in parts:
                            mm = nc.tensor.matmul(o, w[:, u % SPL, k], xl(k), start=False, stop=False)
            return mm

        def split_ready(pe, u, i=None, step=0):
            pe.wait_ge(w_lo, u + 1 if i is None else i * step + (u + 1))

        def unit_done(eng, u, i=None, step=0):
            eng.wait_ge(unit, u + 1 if i is None else i * step + (u + 1))

        NORM_SEMS = ["src", "sq", "add", "mm", "ln", "r", "t", "hi", "lo"]

        class Norm:
            sems = {n: sem("norm_" + n) for n in NORM_SEMS}
            ends = dict.fromkeys(NORM_SEMS, 0)

            def __init__(self, **counts):
                self.base = dict(Norm.ends)
                for n in NORM_SEMS:
                    Norm.ends[n] += counts.get(n, 1 if n in ("mm", "ln", "r") else 8)
                self.src, self.sq, self.add, self.mm, self.ln, self.r, self.t, self.hi, self.lo = \
                    [Norm.sems[n] for n in NORM_SEMS]

            def wait(self, eng, name, count):
                eng.wait_ge(Norm.sems[name], self.base[name] + count)

        def square_tile(act, nm, k, src, n):
            if k >= 2:
                nm.wait(act, "add", k - 1)
            nc.scalar.activation(sq[:, k % 2, 0:n], src, ACT.Square).then_inc(nm.sq, 1)

        def add_square(v, nm, k, n):
            nm.wait(v, "sq", k + 1)
            if k == 0:
                nc.vector.tensor_copy(sqsum[:, 0:n], sq[:, 0, 0:n]).then_inc(nm.add, 1)
            else:
                nm.wait(v, "add", k)
                nc.vector.tensor_tensor(sqsum[:, 0:n], sqsum[:, 0:n], sq[:, k % 2, 0:n], ALU.add).then_inc(nm.add, 1)

        def sum_features(pe, nm, n, bank, added=KT):
            nm.wait(pe, "add", added)
            mm = nc.tensor.matmul(ps[:, bank, 0:min(n, S)], ones[:], sqsum[:, 0:min(n, S)], start=True, stop=True)
            if n > S:
                mm = nc.tensor.matmul(ps[:, bank + 1, 0:n - S], ones[:], sqsum[:, S:n], start=True, stop=True)
            mm.then_inc(nm.mm, 1)

        def make_rstd(act, nm, n, bank):
            nm.wait(act, "mm", 1)
            src = ps[:, bank:bank + 2].rearrange("p b c -> p (b c)")[:, 0:n]
            nc.scalar.activation(rstd[:, 0:n], src, ACT.Ln, bias=eps_t[:], scale=1.0 / D).then_inc(nm.ln, 1)
            nm.wait(act, "ln", 1)
            nc.scalar.activation(rstd[:, 0:n], rstd[:, 0:n], ACT.Exp, scale=-0.5).then_inc(nm.r, 1)

        none = dict(src=0, t=0, hi=0, lo=0)
        nm1 = Norm(src=0)
        nm2a = Norm(**none, sq=0, add=10)
        nm2b = Norm()
        nm3a = Norm(**none)
        nm3b = Norm()
        nm4 = Norm(src=0)
        nm5 = Norm(src=0, hi=0, lo=0)
        cvec = sem("cvec")
        res_free = sem("res_free")
        f_hi = sem("f_hi")
        f_lo = sem("f_lo")
        th_a = sem("th_a")
        gel = sem("gel")
        gel_t = sem("gel_t")
        pr_mm = sem("pr_mm")
        pr_ev = sem("pr_ev")
        up_free = sem("up_free")
        up_v = sem("up_v")
        f_zero = sem("f_zero")
        up_t = sem("up_t")
        up_y = sem("up_y")
        up_hi = sem("up_hi")
        wo_free = [sem(f"wo_free{i}") for i in range(3)]
        wo_f = [sem(f"wo_f{i}") for i in range(3)]
        ml_relu = sem("ml_relu")
        ml_sq = sem("ml_sq")
        ml_hi = sem("ml_hi")
        ml_lo = sem("ml_lo")
        ml_f = sem("ml_f")
        mod_in = [sem(f"mod_in{i}") for i in range(MRAW)]
        mod_mm = sem("mod_mm")
        mod_ev = sem("mod_ev")
        ha = {n: sem("ha_" + n) for n in
              ["q", "k", "v", "g", "gt", "rope", "ro", "vt", "ve", "s", "m", "e", "a", "t", "te", "pv", "sq", "st",
               "ln", "r", "o", "hi", "lo", "w", "c", "on"]}
        hb = {n: sem("hb_" + n) for n in ["ev", "rope", "free", "gt", "vt", "ve"]}

        class Attn:
            def __init__(self, name, steps, slots, width, sbuf, ptbuf, sbn, finish):
                self.steps, self.slots, self.width, self.sb, self.pt, self.sbn, self.finish = \
                    steps, slots, width, sbuf, ptbuf, sbn, finish
                self.s, self.m, self.e, self.p, self.t, self.te, self.o, self.oh, self.ol, self.k = \
                    [sem(f"{name}_{n}") for n in ("s", "m", "e", "p", "t", "te", "o", "oh", "ol", "k")]
                self.blk = [sum(len(x["blocks"]) for x in steps[:n]) for n in range(len(steps) + 1)]
                self.grp = [sum(x["last"] for x in steps[:n]) for n in range(len(steps) + 1)]

            def sbank(self, m):
                if self.slots == 4:
                    return ps[:, m % 4]
                return pair(m % 2)

        def attn_scores(pe, A, n):
            st = A.steps[n]
            for r in range(REP):
                m = n * REP + r
                if m >= A.slots:
                    pe.wait_ge(A.m, m - A.slots + 1)
                for c, (o, rhs) in enumerate(st["k"]):
                    mm = nc.tensor.matmul(A.sbank(m)[:, o:o + rhs.shape[-1]], st["q"](r), rhs,
                                          start=st["kstart"][c], stop=True, skip_group_check=True)
                mm.then_inc(A.s, 1)

        def attn_out(pe, A, n):
            st = A.steps[n]
            pe.wait_ge(A.p, n + 1)
            nb = len(st["blocks"])
            g = A.grp[n]
            ob = ps[0:HD, 6 + g % 2]

            def turn(b):
                x = A.blk[n] + b
                if x >= 2:
                    pe.wait_ge(A.te, x - 1)
                o, w = st["blocks"][b]
                for r in range(REP):
                    mm = nc.tensor.transpose(ps[0:w, 4 + x % 2, r * P:(r + 1) * P],
                                             A.sb[n % A.sbn][:, r, o:o + w], ident[:])
                mm.then_inc(A.t, 1)

            def weigh(b):
                x = A.blk[n] + b
                pe.wait_ge(A.te, x + 1)
                o, w = st["blocks"][b]
                if b == 0 and st["first"] and g >= 2:
                    pe.wait_ge(A.ol, g - 1)
                mm = nc.tensor.matmul(ob, st["v"][b], A.pt[0:w, x % 4], start=(st["first"] and b == 0),
                                      stop=(st["last"] and b == nb - 1))
                if st["last"] and b == nb - 1:
                    mm.then_inc(A.o, 1)
                else:
                    mm.then_inc(A.k, 1)
            for b in range(nb):
                turn(b)
                if b:
                    weigh(b - 1)
            weigh(nb - 1)

        def attn_pe(pe, A):
            attn_scores(pe, A, 0)
            attn_scores(pe, A, 1)
            for n in range(len(A.steps)):
                if n + 2 < len(A.steps):
                    attn_scores(pe, A, n + 2)
                attn_out(pe, A, n)

        def attn_act(act, A):
            def turned(n):
                st = A.steps[n]
                for b, (o, w) in enumerate(st["blocks"]):
                    x = A.blk[n] + b
                    act.wait_ge(A.t, x + 1)
                    if x >= 4:
                        need = x - 3
                        gd = sum(1 for s in range(len(A.steps)) if A.steps[s]["last"] and A.blk[s + 1] <= need)
                        if gd:
                            act.wait_ge(A.o, gd)
                        if need - gd:
                            act.wait_ge(A.k, need - gd)
                    nc.scalar.activation(A.pt[0:w, x % 4], ps[0:w, 4 + x % 2], ACT.Copy).then_inc(A.te, 1)

            def finished(n):
                if A.steps[n]["last"]:
                    A.finish["act"](act, A, n, A.grp[n])

            for n, st in enumerate(A.steps):
                for r in range(REP):
                    m = n * REP + r
                    act.wait_ge(A.m, m + 1)
                    if st["sink"] is not None or st["clamp"]:
                        act.wait_ge(A.m, (n + 1) * REP)
                        act.wait_ge(mfix[A], fixn(A, n) + 1)
                    buf = A.sb[n % A.sbn][:, r, 0:st["keys"]]
                    c = (n % 2) * REP + r
                    nc.scalar.activation(buf, buf, ACT.Exp, bias=negm[:, c:c + 1], scale=-1.0,
                                         accum_out=sums[:, c:c + 1]).then_inc(A.e, 1)
                if st["sink"] is not None:
                    c = (n % 2) * REP
                    nc.scalar.activation(esk[:, c:c + REP], esk[:, c:c + REP], ACT.Exp).then_inc(A.e, 1)
                else:
                    act.wait_ge(A.e, 5 * n + 4)
                    nc.scalar.activation(spare, eps_t[:], ACT.Copy).then_inc(A.e, 1)
                if n:
                    turned(n - 1)
                if n >= 2:
                    finished(n - 2)
            turned(len(A.steps) - 1)
            finished(len(A.steps) - 2)
            finished(len(A.steps) - 1)

        mfix = {}

        def fixn(A, n):
            return sum(1 for s in A.steps[:n] if s["sink"] is not None or s["clamp"])

        def attn_dve(v, A):
            def finished(n):
                if A.steps[n]["last"]:
                    A.finish["dve"](v, A, n, A.grp[n])

            def minima(n):
                st = A.steps[n]
                c = (n % 2) * REP
                if n >= A.sbn:
                    v.wait_ge(A.t, A.blk[n - A.sbn + 1])
                for r in range(REP):
                    m = n * REP + r
                    v.wait_ge(A.s, m + 1)
                    nc.vector.tensor_tensor_reduce(
                        out=A.sb[n % A.sbn][:, r, 0:st["keys"]], in0=A.sbank(m)[:, st["off"]:st["off"] + st["keys"]],
                        in1=st["bias"](r), scale=1.0, scalar=3e38, op0=ALU.add, op1=ALU.min,
                        accum_out=negm[:, c + r:c + r + 1]).then_inc(A.m, 1)
                nm_ = negm[:, c:c + REP]
                if st["clamp"]:
                    v.wait_ge(A.m, (n + 1) * REP)
                    nc.vector.tensor_scalar(nm_, nm_, BIG / 10, None, ALU.min).then_inc(mfix[A], 1)
                if st["sink"] is not None:
                    v.wait_ge(A.m, (n + 1) * REP)
                    k = st["sink"]
                    done(nc.vector.tensor_tensor(nm_, nm_, nsinks[:, k:k + REP], ALU.min))
                    settle(v)
                    nc.vector.tensor_tensor(esk[:, c:c + REP], sinks[:, k:k + REP], nm_, ALU.add).then_inc(mfix[A], 1)

            minima(0)
            for n, st in enumerate(A.steps):
                c = (n % 2) * REP
                if n + 1 < len(A.steps):
                    minima(n + 1)
                if n >= 2:
                    finished(n - 2)
                v.wait_ge(A.e, 5 * (n + 1))
                su = sums[:, c:c + REP]
                if st["sink"] is not None:
                    done(nc.vector.tensor_tensor(rs[:, c:c + REP], su, esk[:, c:c + REP], ALU.add))
                else:
                    done(nc.vector.tensor_scalar(rs[:, c:c + REP], su, 1e-30, None, ALU.max))
                settle(v)
                done(nc.vector.reciprocal(wgt[:, c:c + REP], rs[:, c:c + REP]))
                if st["gate"] is not None:
                    settle(v)
                    done(nc.vector.tensor_tensor(wgt[:, c:c + REP], wgt[:, c:c + REP], st["gate"], ALU.mult))
                settle(v)
                for r in range(REP):
                    buf = A.sb[n % A.sbn][:, r, 0:st["keys"]]
                    ins = nc.vector.tensor_scalar(buf, buf, wgt[:, c + r:c + r + 1], None, ALU.mult)
                ins.then_inc(A.p, 1)
            finished(len(A.steps) - 2)
            finished(len(A.steps) - 1)

        def o_view(x):
            return x.rearrange("p (r q) -> p r q", r=REP)

        def fin1_act(act, A, n, g):
            act.wait_ge(A.o, g + 1)
            h, l = A.steps[n]["dst"]
            nc.scalar.activation(h, o_view(ps[0:HD, 6 + g % 2]), ACT.Copy).then_inc(A.oh, 1)

        def fin1_dve(v, A, n, g):
            h, l = A.steps[n]["dst"]
            v.wait_ge(A.oh, g + 1)
            nc.vector.tensor_tensor(l, o_view(ps[0:HD, 6 + g % 2]), h.bitcast(F32), ALU.subtract).then_inc(A.ol, 1)

        def fin2_act(act, A, n, g):
            act.wait_ge(A.oh, g + 1)
            h, l, gg, tmp = A.steps[n]["dst"]
            nc.scalar.activation(h, tmp, ACT.Copy).then_inc(A.k2, 1)

        def fin2_dve(v, A, n, g):
            h, l, gg, tmp = A.steps[n]["dst"]
            v.wait_ge(A.o, g + 1)
            if g:
                v.wait_ge(A.k2, g)
                v.wait_ge(A.ol, g)
            nc.vector.scalar_tensor_tensor(out=tmp, in0=o_view(ps[0:HD, 6 + g % 2]), scalar=0.5, in1=gg,
                                           op0=ALU.mult, op1=ALU.mult).then_inc(A.oh, 1)
            v.wait_ge(A.k2, g + 1)
            nc.vector.tensor_tensor(l, tmp, h.bitcast(F32), ALU.subtract).then_inc(A.ol, 1)

        def steps1():
            out = []
            for g in range(2):
                gs = slice(g * HD, (g + 1) * HD)
                for i in range(QT):
                    qs = slice(i * P, (i + 1) * P)
                    n = (i + 1) * P
                    dst = (o1h[gs, 0:REP, qs], o1l[gs, 0:REP, qs])
                    gcol = lambda b, g=g, i=i: gate[:, i, g * 12 + b:g * 12 + b + 12:3]
                    q = lambda r, gs=gs, qs=qs: q_n[gs, r, qs]
                    for kind in (0, 1):
                        out.append(dict(q=q, k=[(0, k_all[gs, kind, 0:n])], kstart=[True], off=0, keys=n,
                                        bias=lambda r, g=g, n=n: strip_n[:, g * REP + r, S - n:S],
                                        blocks=[(j * P, P) for j in range(i + 1)],
                                        v=[v_all[:, kind, j, gs] for j in range(i + 1)],
                                        first=(kind == 0), last=False, dst=dst, gate=gcol(1 + kind), sink=None,
                                        clamp=False))
                    out.append(dict(q=q, k=[(0, kcmp[gs, 0:NCMP + 1])], kstart=[True], off=0, keys=NCMP,
                                    bias=lambda r, i=i: cmask[:, i, :], blocks=[(0, NCMP)],
                                    v=[vcmp[0:NCMP, g, :]], first=False, last=True, dst=dst, gate=gcol(0), sink=None,
                                    clamp=True))
            for g in range(2):
                gs = slice(g * HD, (g + 1) * HD)
                for i in range(QT):
                    qs = slice(i * P, (i + 1) * P)
                    lo = max(i - 1, 0)
                    n = (i + 1 - lo) * P
                    out.append(dict(q=lambda r, gs=gs, qs=qs: q_s[gs, r, qs],
                                    k=[(0, k_all[gs, 2, lo * P:lo * P + n])], kstart=[True], off=0, keys=n,
                                    bias=lambda r, g=g, n=n: strip_s[:, g * REP + r, 256 - n:256],
                                    blocks=[(j * P, P) for j in range(n // P)],
                                    v=[v_all[:, 2, lo + j, gs] for j in range(n // P)],
                                    first=True, last=True, dst=(o1h[gs, REP:8, qs], o1l[gs, REP:8, qs]), gate=None,
                                    sink=g * REP, clamp=False))
            return out

        def steps2():
            out = []
            for kh in range(4):
                pb = (kh % 2) * HD
                gs = slice(pb, pb + HD)
                kt = kh // 2
                for i in range(QT):
                    qs = slice(i * P, (i + 1) * P)
                    lo, hi = max(i - 1, 0), min(i + 2, QT)
                    n = (hi - lo) * P
                    mask = bm0[:, 0:C + n] if i == 0 else bm1[:, 0:C + n]
                    ts = slice(kt * REP, (kt + 1) * REP)
                    out.append(dict(q=lambda r, gs=gs, qs=qs, kt=kt: b_q[gs, kt * REP + r, qs],
                                    k=[(C, b_k[gs, kt, S:SC]), (S, b_k[gs, kt, lo * P:hi * P])], kstart=[True, True],
                                    off=C, keys=C + n, bias=lambda r, mask=mask: mask,
                                    blocks=[(j * P, P) for j in range(2 + hi - lo)],
                                    v=[b_v[:, QT + j, kh * HD:(kh + 1) * HD] for j in range(2)]
                                    + [b_v[:, j, kh * HD:(kh + 1) * HD] for j in range(lo, hi)],
                                    first=True, last=True,
                                    dst=(x1h[gs, ts, qs], x1l[gs, ts, qs], b_g[gs, ts, qs], o_view(ot[gs, :])),
                                    gate=None, sink=8 + kh * REP, clamp=False))
            return out

        A1 = Attn("at1", steps1(), 4, 512, sb1, pt1, 3, dict(act=fin1_act, dve=fin1_dve))
        A2 = Attn("at2", steps2(), 2, 1024, b_sb, b_pt, 3, dict(act=fin2_act, dve=fin2_dve))
        A2.k2 = sem("at2_hi")
        mfix[A1] = sem("at1_fix")
        mfix[A2] = sem("at2_fix")

        @block.sync
        def _(sp):
            for dst, name in ((ident[:], "ident"), (gains, "gains"), (bmod, "bmod"), (cin, "cin"), (lamv[0:HD], "lamv"),
                              (subg, "subg"), (w2[:], "w2"), (pos[:], "pos"), (onehot[:], "onehot"),
                              (blhs[0:BUCKETS], "rel_bias"), (blhs[BUCKETS:34], "selrows"), (cmask[:], "cmask")):
                sp.dma_start(dst, t[name]).then_inc(const_in, 16)
            sp.dma_start(sinks, bass.AP(t["sinks"].tensor, 0, [[0, P], [1, 24]])).then_inc(const_in, 16)
            sp.dma_start(xin[:], t["xT"]).then_inc(x_in, 16)
            for u in range(RAW):
                load_unit(sp, u, t["w_att"][u])
            sp.wait_ge(brow_ok, 2)
            sp.dma_start(dbias, brow[:].unsqueeze(1).to_broadcast([16, P, TBL])).then_inc(dbias_in, 16)
            sp.wait_ge(dbias_in, 16)
            sp.dma_start(strip_n[:], bass.AP(dbias.tensor, 127, [[TBL - 1, P], [P * TBL, 8], [1, 512]])).then_inc(strips_in, 16)
            sp.dma_start(strip_s[:], bass.AP(dbias.tensor, 8 * P * TBL + 383, [[TBL - 1, P], [P * TBL, 8], [1, 256]])).then_inc(strips_in, 16)
            for u in range(RAW, N_ATT):
                load_unit(sp, u, t["w_att"][u])
            with sp.Fori(0, 2) as i:
                for j in range(12):
                    load_unit(sp, U_UP + j, t["w_up"][bass.ds(i * 12 + j, 1)].rearrange("o p k m -> p (o k) m"), i, 12)
            begin_after(sp, "nsa")
            sp.dma_start(hc[:, :, 0:S], t["xT"]).then_inc(x_in, 16)
            sp.dma_start(hc[:, :, S:SC], t["ctxT"]).then_inc(ctx_in, 16)
            with sp.Fori(0, 2) as i:
                for j in range(4):
                    load_unit(sp, U_OUT + j, t["w_out"][bass.ds(i * 4 + j, 1)].rearrange("o p k m -> p (o k) m"), i, 4)
            with sp.Fori(0, 4) as i:
                for j in range(16):
                    load_unit(sp, U_MLP + j, t["w_mlp"][bass.ds(i * 16 + j, 1)].rearrange("o p k m -> p (o k) m"), i, 16)
            with sp.Fori(0, 8) as i:
                for j in range(4):
                    load_unit(sp, U_A + j, t["w_a"][bass.ds(i * 4 + j, 1)].rearrange("o p k m -> p (o k) m"), i, 4)
            with sp.Fori(0, 2) as i:
                for j in range(4):
                    load_unit(sp, U_AO + j, t["w_ao"][bass.ds(i * 4 + j, 1)].rearrange("o p k m -> p (o k) m"), i, 4)
            with sp.Fori(0, 5) as i:
                for j in range(4):
                    load_unit(sp, U_B + j, t["w_b"][bass.ds(i * 4 + j, 1)].rearrange("o p k m -> p (o k) m"), i, 4)
            with sp.Fori(0, 2) as i:
                for j in range(4):
                    load_unit(sp, U_BO + j, t["w_bo"][bass.ds(i * 4 + j, 1)].rearrange("o p k m -> p (o k) m"), i, 4)
            for k in range(KT):
                nm5.wait(sp, "t", k + 1)
                sp.dma_start(out[:, k], xo[:, k]).then_inc(out_done, 16)
            sp.wait_ge(out_done, 16 * KT)

        @block.gpsimd
        def _(g):
            def low(u, i=None):
                g.wait_ge(w_hi, u + 1 if i is None else i * 4 + (u + 1))
                nc.gpsimd.tensor_tensor(w_l[:, u % SPL], raw[:, u % RAW], w_h[:, u % SPL].bitcast(F32),
                                        ALU.subtract).then_inc(w_lo, 1)
            head = U_END % 4
            for u in range(head):
                low(u)
            with g.Fori(0, (U_END - head) // 4) as i:
                for j in range(4):
                    low(head + j, i)

        CONSTS = 16 * 13

        @block.tensor
        def _(pe):
            pe.wait_ge(const_in, CONSTS)
            pe.wait_ge(boot, 1)
            nc.tensor.matmul(ps[0:16, 6, :], blhs[:], onehot[:, 0:512], start=True, stop=True)
            nc.tensor.matmul(ps[0:16, 7, 0:128], blhs[:], onehot[:, 512:640], start=True, stop=True)
            pe.wait_ge(boot, 3)
            nc.tensor.matmul(ps[:, 5, 0:2], ones[0:HD, :], lamp[0:HD, :], start=True, stop=True).then_inc(cvec, 1)
            sum_features(pe, nm1, S, 4)
            plain = [(lambda k: x1h[:, k, :], lambda k: x1l[:, k, :])]
            r = 0
            for u in range(N_ATT):
                cmp_u = 2 <= u < 10
                first = not (cmp_u and u % 2 == 1)
                if u == 0:
                    pass
                split_ready(pe, u)
                if first and r >= 2:
                    pe.wait_ge(res_free, r - 1)
                if not cmp_u:
                    if u == 0:
                        for k in range(KT):
                            nm1.wait(pe, "lo", k + 1)
                            mm = products(u, [(ps[:, 0], lambda k: x1h[:, k, :], lambda k: x1l[:, k, :])], k, k + 1,
                                          first=(k == 0), last=(k == KT - 1))
                    else:
                        mm = products(u, [(ps[:, r % 2], lambda k: x1h[:, k, :], lambda k: x1l[:, k, :])])
                    r += 1
                else:
                    kv = (u - 2) // 4
                    kk = u % 2
                    pe.wait_ge(f_lo, kv + 1)

                    def fr(f, kv=kv, kk=kk):
                        return lambda k: bass.AP(f, kv * FW + kk * 8 + k, [[2 * FW, P], [256, 3], [8, 32]])
                    mm = products(u, [(ps[:, r % 2, 0:96], fr(fh), fr(fl))], first=(kk == 0), last=(kk == 1))
                    if kk == 1:
                        r += 1
                mm.then_inc(unit, 1)
            pe.wait_ge(gel, 1)
            glv = gl3[:, :, :].rearrange("p c (g n) -> p c g n", g=2)
            for g in range(2):
                for mt in range(2):
                    nc.tensor.matmul(ps[g * HD:(g + 1) * HD, 2, 0:NCMP], w2[:, 0, mt, :], glv[:, mt, g, :],
                                     start=(mt == 0), stop=(mt == 1))
            for g in range(2):
                for mt in range(2):
                    mm = nc.tensor.matmul(ps[0:NCMP, 3, g * HD:(g + 1) * HD], glv[:, 2 + mt, g, :], w2[:, 1, mt, :],
                                          start=(mt == 0), stop=(mt == 1))
            mm.then_inc(pr_mm, 1)
            pe.wait_ge(res_free, 21)
            for n in range(4):
                for tt in range(QT):
                    mm = nc.tensor.transpose(ps[:, 4 + n, tt * P:(tt + 1) * P], vT[:, n, tt * P:(tt + 1) * P], ident[:])
                mm.then_inc(pr_mm, 1)
            end_phase(pe, "prep")
            begin_after(pe, "prep")
            attn_pe(pe, A1)
            end_phase(pe, "nsa")
            begin_after(pe, "nsa")
            with pe.Fori(0, 2) as i:
                for m in range(4):
                    b = m % 2
                    pe.wait_ge(up_free, i * 4 + (m + 1))
                    for j, bank in ((0, b), (1, 2 + b)):
                        u = U_UP + m * 3 + j
                        split_ready(pe, u, i, 12)
                        products(u, [(ps[:, bank], lambda k: x1h[:, k, :], lambda k: x1l[:, k, :])]).then_inc(unit, 1)
                    u = U_UP + m * 3 + 2
                    split_ready(pe, u, i, 12)
                    products(u, [(ps[:, 4 + b], lambda k: o1h[:, k, :], lambda k: o1l[:, k, :])], 0, 4)
                    products(u, [(ps[:, 6 + b], lambda k: o1h[:, k, :], lambda k: o1l[:, k, :])], 4, 8).then_inc(unit, 1)
            end_phase(pe, "up")
            begin_after(pe, "up")

            def out_products(n, u0, yh, yl, wide):
                with pe.Fori(0, 2) as i:
                    for j in range(4):
                        split_ready(pe, u0 + j, i, 4)
                        pe.wait_ge(wo_free[n], i * 4 + (j + 1))
                        if wide:
                            parts = [(ps[:, 2 * (j % 2)], lambda k: yh[:, k, 0:S], lambda k: yl[:, k, 0:S]),
                                     (ps[:, 2 * (j % 2) + 1, 0:C], lambda k: yh[:, k, S:SC], lambda k: yl[:, k, S:SC])]
                        else:
                            parts = [(ps[:, j % 2], lambda k: yh[:, k, :], lambda k: yl[:, k, :])]
                        products(u0 + j, parts).then_inc(unit, 1)
            out_products(0, U_OUT, y1h, y1l, False)
            sum_features(pe, nm2a, S, 4, KT + 2)
            end_phase(pe, "wout")
            begin_after(pe, "wout")
            sum_features(pe, nm2b, S, 6)
            end_phase(pe, "norm2")
            begin_after(pe, "norm2")
            with pe.Fori(0, 4) as i:
                pe.wait_ge(mod_ev, i + 1)
                for j in range(16):
                    u = U_MLP + j
                    split_ready(pe, u, i, 16)
                    pe.wait_ge(ml_f, i * 16 + (j + 1))
                    if j < 8:
                        mm = products(u, [(ps[:, j % 2], lambda k: x1h[:, k, :], lambda k: x1l[:, k, :])])
                    else:
                        if j == 8:
                            pe.wait_ge(ml_lo, i * 8 + 7)
                            products(u, [(ps[:, j % 2], lambda k: m_h[:, k, :], lambda k: m_l[:, k, :])], 0, 7, last=False)
                            pe.wait_ge(ml_lo, i * 8 + 8)
                            mm = products(u, [(ps[:, j % 2], lambda k: m_h[:, k, :], lambda k: m_l[:, k, :])], 7, 8, first=False)
                        else:
                            mm = products(u, [(ps[:, j % 2], lambda k: m_h[:, k, :], lambda k: m_l[:, k, :])])
                    mm.then_inc(unit, 1)
                    if j % 4 != 3:
                        c = j // 4 * 3 + j % 4
                        pe.wait_ge(mod_in[c % MRAW], i * (16 * 12 // MRAW) + 16 * (c // MRAW + 1))
                        for k in range(KT):
                            mm = nc.tensor.matmul(ps[:, 7, 2 * c:2 * c + 2], mraw[:, c % MRAW, k], cs[:, 2 * k:2 * k + 2],
                                                  start=(k == 0), stop=(k == KT - 1))
                        mm.then_inc(mod_mm, 1)
            sum_features(pe, nm3a, S, 4)
            end_phase(pe, "mlp")
            begin_after(pe, "mlp")
            sum_features(pe, nm3b, SC, 6)
            end_phase(pe, "norm3")
            begin_after(pe, "norm3")
            with pe.Fori(0, 8) as h:
                for j in range(4):
                    u = U_A + j
                    split_ready(pe, u, h, 4)
                    if j == 0:
                        pe.wait_ge(ha["e"], h * 12 + 1)
                    if j == 2:
                        pe.wait_ge(ha["q"], h + 1)
                    if j == 3:
                        pe.wait_ge(ha["k"], h + 1)
                    products(u, [(ps[:, 2 * (j % 2)], lambda k: x2h[:, k, 0:S], lambda k: x2l[:, k, 0:S]),
                                 (ps[:, 2 * (j % 2) + 1, 0:C], lambda k: x2h[:, k, S:SC], lambda k: x2l[:, k, S:SC])]
                             ).then_inc(unit, 1)
                pe.wait_ge(ha["v"], h + 1)
                pe.wait_ge(ha["r"], h + 1)
                for b in range(6):
                    mm = nc.tensor.transpose(ps[:, 4 + b // 4, (b % 4) * P:(b % 4 + 1) * P], a_vT[:, b * P:(b + 1) * P], ident[:])
                mm.then_inc(ha["vt"], 1)
                pe.wait_ge(ha["ro"], h * 2 + 3)
                pe.wait_ge(ha["g"], h + 1)

                def scores(qt):
                    for m in range(2):
                        s = 2 * qt + m
                        if s >= 2:
                            pe.wait_ge(ha["e"], h * 12 + s)
                        ms = slice(m * HD, (m + 1) * HD)
                        q = a_q[ms, qt * P:(qt + 1) * P]
                        if qt < QT:
                            nc.tensor.matmul(ps[:, 2 * m], q, a_k[ms, 0:S], start=True, stop=True)
                            mm = nc.tensor.matmul(ps[:, 2 * m + 1, 0:C], q, a_k[ms, S:SC], start=True, stop=True)
                        else:
                            mm = nc.tensor.matmul(ps[:, 2 * m, 0:C], q, a_k[ms, S:SC], start=True, stop=True)
                        mm.then_inc(ha["s"], 1)

                def turns(qt):
                    pe.wait_ge(ha["a"], h * 6 + (qt + 1))
                    if qt == 0:
                        pe.wait_ge(ha["ve"], h + 1)
                    else:
                        pe.wait_ge(ha["te"], h * 6 + qt)
                    nb = 6 if qt < QT else 2
                    for b in range(nb):
                        mm = nc.tensor.transpose(ps[:, 4 + b // 4, (b % 4) * P:(b % 4 + 1) * P],
                                                 a_p[qt % 2][:, 0, b * P:(b + 1) * P], ident[:])
                    mm.then_inc(ha["t"], 1)
                scores(0)
                for qt in range(6):
                    if qt < 5:
                        scores(qt + 1)
                    turns(qt)
                pe.wait_ge(ha["lo"], h + 1)
                pe.wait_ge(ha["te"], h * 6 + 4)
                for b in range(6):
                    mm = nc.tensor.matmul(ps[:, 6], a_v[:, b, :], a_pt[:, b, :], start=(b == 0), stop=(b == 5))
                pe.wait_ge(ha["te"], h * 6 + 6)
                for b in range(2):
                    mm = nc.tensor.matmul(ps[:, 7, 0:C], a_v[:, 4 + b, :], a_pt2[:, b, :], start=(b == 0), stop=(b == 1))
                mm.then_inc(ha["pv"], 1)
                pe.wait_ge(ha["sq"], h + 1)
                nc.tensor.matmul(ps[:, 4], ones[:], a_p0[:, 0, 0:S], start=True, stop=True)
                nc.tensor.matmul(ps[:, 5, 0:C], ones[:], a_p0[:, 0, S:SC], start=True, stop=True).then_inc(ha["st"], 1)
            end_phase(pe, "heads")
            begin_after(pe, "heads")
            out_products(1, U_AO, o2h, o2l, True)
            end_phase(pe, "ao")
            begin_after(pe, "ao")
            sum_features(pe, nm4, SC, 6)
            end_phase(pe, "norm4")
            begin_after(pe, "norm4")
            for u in range(N_B):
                split_ready(pe, U_B + u)
                if u >= 2:
                    pe.wait_ge(hb["free"], u - 1)
                parts = [(ps[:, 2 * (u % 2)], lambda k: x2h[:, k, 0:S], lambda k: x2l[:, k, 0:S])]
                if 8 <= u < 12:
                    parts.append((ps[:, 2 * (u % 2) + 1, 0:C], lambda k: x2h[:, k, S:SC], lambda k: x2l[:, k, S:SC]))
                products(U_B + u, parts).then_inc(unit, 1)
                if u == 13:
                    for n in range(2):
                        if n:
                            pe.wait_ge(hb["ve"], 1)
                        for b in range(6):
                            mm = nc.tensor.transpose(ps[:, 4 + b // 4, (b % 4) * P:(b % 4 + 1) * P],
                                                     b_vT[:, n, b * P:(b + 1) * P], ident[:])
                        mm.then_inc(hb["vt"], 1)
            end_phase(pe, "bqkv")
            begin_after(pe, "bqkv")
            attn_pe(pe, A2)
            end_phase(pe, "battn")
            begin_after(pe, "battn")
            out_products(2, U_BO, x1h, x1l, False)
            sum_features(pe, nm5, S, 4)

        @block.scalar
        def _(act):
            act.wait_ge(const_in, CONSTS)
            act.wait_ge(boot, 1)
            nc.scalar.activation(ct, cin, ACT.Tanh, scale=0.5).then_inc(cvec, 1)
            act.wait_ge(x_in, 16)
            for k in range(KT):
                square_tile(act, nm1, k, xin[:, k, :], S)
            act.wait_ge(boot, 4)
            nc.scalar.activation(lame, lame, ACT.Exp).then_inc(cvec, 1)
            split_high(act, 0)
            make_rstd(act, nm1, S, 4)
            for k in range(KT):
                nm1.wait(act, "t", k + 1)
                nc.scalar.activation(x1h[:, k, :], xn[:, k % 2, 0:S], ACT.Copy).then_inc(nm1.hi, 1)
            r = 0
            for u in range(N_ATT):
                split_high(act, u + 1)
                if u in (0, 1):
                    unit_done(act, u)
                    if u == 0:
                        nm1.wait(act, "lo", KT)
                    for g in range(2):
                        for op in range(2):
                            src = ps[g * HD:(g + 1) * HD, u % 2].rearrange("p (t o) -> p t o", o=2)[:, :, op]
                            ins = nc.scalar.activation(fh[op * HD:(op + 1) * HD, u, g * 256:(g + 1) * 256], src, ACT.Copy)
                            ins.then_inc(f_hi, 1)
                    nc.scalar.activation(fh[:, u, 512:520 + 0], pos[:, u, 0:8], ACT.Copy).then_inc(f_hi, 1)
                    nc.scalar.activation(fh[:, u, 520:528], pos[:, u, 8:16], ACT.Copy).then_inc(f_hi, 1)
                if u == 10:
                    act.wait_ge(gel_t, 1)
                    nc.scalar.activation(gl2[:], gl1[:], ACT.Tanh, scale=GELU_C).then_inc(th_a, 1)
                if u == 18:
                    unit_done(act, u)
                    nc.scalar.activation(vT[:, 3, :], ps[:, 0], ACT.Tanh, scale=0.5).then_inc(th_a, 1)
            end_phase(act, "prep")
            begin_after(act, "prep")
            act.wait_ge(strips_in, 32)
            attn_act(act, A1)
            end_phase(act, "nsa")
            begin_after(act, "nsa")
            with act.Fori(0, 2) as i:
                for m in range(4):
                    b = m % 2
                    for j in range(3):
                        split_high(act, U_UP + m * 3 + j + 1, i, 12)
                        if j < 2:
                            unit_done(act, U_UP + m * 3 + j, i, 12)
                            if j == 0:
                                act.wait_ge(up_free, i * 4 + (m + 1))
                            nc.scalar.activation(tg[:, b, j, :], ps[:, 2 * j + b], ACT.Tanh, scale=0.5).then_inc(up_t, 1)
                    act.wait_ge(up_y, i * 4 + (m + 1))
                    nc.scalar.activation(y1h[:, bass.ds(i * 4 + m, 1), :].rearrange("p a s -> p (a s)"), ty[:, b, :],
                                         ACT.Copy).then_inc(up_hi, 1)
            end_phase(act, "up")
            begin_after(act, "up")
            with act.Fori(0, 2) as i:
                for j in range(4):
                    split_high(act, U_OUT + j + 1, i, 4)
                    unit_done(act, U_OUT + j, i, 4)
                    nc.scalar.activation(f_t[:, bass.ds(i * 4 + j, 1), :].rearrange("p a s -> p (a s)"), ps[:, j % 2],
                                         ACT.Copy).then_inc(wo_f[0], 1)
                    nm2a.wait(act, "add", i * 4 + (j + 1))
                    nc.scalar.activation(sq[:, j % 2, 0:S], ps[:, j % 2], ACT.Square).then_inc(wo_free[0], 1)
            make_rstd(act, nm2a, S, 4)
            end_phase(act, "wout")
            begin_after(act, "wout")
            for c in range(MRAW - 1):
                act.dma_start(mraw[:, c], t["w_mod"][c]).then_inc(mod_in[c], 16)
            for k in range(KT):
                nm2b.wait(act, "src", k + 1)
                square_tile(act, nm2b, k, hc[:, k, 0:S], S)
            make_rstd(act, nm2b, S, 6)
            for k in range(KT):
                nm2b.wait(act, "t", k + 1)
                nc.scalar.activation(x1h[:, k, :], xn2[:, k % 2, 0:S], ACT.Copy).then_inc(nm2b.hi, 1)
            end_phase(act, "norm2")
            begin_after(act, "norm2")
            with act.Fori(0, 4) as i:
                for j in range(16):
                    split_high(act, U_MLP + j + 1, i, 16)
                    unit_done(act, U_MLP + j, i, 16)
                    if j < 8:
                        if j == 0:
                            pass
                        nc.scalar.activation(relu[:, j % 2, :], ps[:, j % 2], ACT.Relu).then_inc(ml_relu, 1)
                        act.wait_ge(ml_sq, i * 8 + (j + 1))
                        nc.scalar.activation(m_h[:, j, :], msq[:, j % 2, :], ACT.Copy).then_inc(ml_hi, 1)
                    if j % 4 != 3:
                        c = j // 4 * 3 + j % 4 + MRAW - 1
                        act.dma_start(mraw[:, c % MRAW], t["w_mod"][bass.ds(i * 12 + c, 1)].rearrange("o p k m -> p (o k) m")
                                      ).then_inc(mod_in[c % MRAW], 16)
            for c in range(MRAW - 1):
                act.wait_ge(mod_in[c], 16 * (N_MOD // MRAW + 1))
            for k in range(KT):
                square_tile(act, nm3a, k, f_t[:, k, :], S)
            make_rstd(act, nm3a, S, 4)
            end_phase(act, "mlp")
            begin_after(act, "mlp")
            for k in range(KT):
                nm3b.wait(act, "src", k + 1)
                square_tile(act, nm3b, k, hc[:, k, :], SC)
            make_rstd(act, nm3b, SC, 6)
            for k in range(KT):
                nm3b.wait(act, "t", k + 1)
                nc.scalar.activation(x2h[:, k, :], xn2[:, k % 2, :], ACT.Copy).then_inc(nm3b.hi, 1)
            end_phase(act, "norm3")
            begin_after(act, "norm3")
            act.dma_start(cos_t[:], t["cos"]).then_inc(tab_in, 16)
            act.dma_start(sin_t[:], t["sin"]).then_inc(tab_in, 16)
            with act.Fori(0, 8) as h:
                for j in range(4):
                    split_high(act, U_A + j + 1, h, 4)
                    unit_done(act, U_A + j, h, 4)
                    src = pair(j % 2)[:, 0:SC]
                    if j == 0:
                        act.wait_ge(ha["lo"], h + 1)
                        nc.scalar.activation(a_q[:], src, ACT.Copy, scale=-0.125).then_inc(ha["q"], 1)
                    elif j == 1:
                        nc.scalar.activation(a_k[:], src, ACT.Copy).then_inc(ha["k"], 1)
                    elif j == 2:
                        nc.scalar.activation(a_vT[:], src, ACT.Copy).then_inc(ha["v"], 1)
                    else:
                        nc.scalar.activation(a_g[:], src, ACT.Tanh, scale=0.5).then_inc(ha["gt"], 1)
                act.wait_ge(ha["vt"], h + 1)
                nc.scalar.activation(a_v[:].rearrange("p b e -> p (b e)"), pair(2)[:, 0:SC], ACT.Copy).then_inc(ha["ve"], 1)

                def exps(qt):
                    n = SC if qt < QT else C
                    for m in range(2):
                        act.wait_ge(ha["m"], h * 12 + (2 * qt + m + 1))
                        if qt >= 2:
                            act.wait_ge(ha["t"], h * 6 + (qt - 1))
                        nc.scalar.activation(a_p[qt % 2][:, m, 0:n], pair(m)[:, 0:n], ACT.Exp,
                                             bias=negm[:, 2 * (qt % 2) + m:2 * (qt % 2) + m + 1], scale=-1.0,
                                             accum_out=sums[:, 2 * (qt % 2) + m:2 * (qt % 2) + m + 1]).then_inc(ha["e"], 1)

                def turned(qt):
                    act.wait_ge(ha["t"], h * 6 + (qt + 1))
                    if qt < QT:
                        nc.scalar.activation(a_pt[:, :, qt * P:(qt + 1) * P],
                                             pair(2)[:, 0:SC].rearrange("p (b q) -> p b q", b=6), ACT.Copy).then_inc(ha["te"], 1)
                    else:
                        nc.scalar.activation(a_pt2[:, :, (qt - QT) * P:(qt - QT + 1) * P],
                                             pair(2)[:, 0:C].rearrange("p (b q) -> p b q", b=2), ACT.Copy).then_inc(ha["te"], 1)
                for qt in range(6):
                    exps(qt)
                    if qt:
                        turned(qt - 1)
                turned(5)
                act.wait_ge(ha["pv"], h + 1)
                act.wait_ge(ha["t"], h * 6 + 6)
                nc.scalar.activation(a_p0[:, 0, :], pair(3)[:, 0:SC], ACT.Square).then_inc(ha["sq"], 1)
                act.wait_ge(ha["st"], h + 1)
                nc.scalar.activation(rstd[:], pair(2)[:, 0:SC], ACT.Ln, bias=seps_t[:], scale=1.0 / P).then_inc(ha["ln"], 1)
                act.wait_ge(ha["ln"], h + 1)
                nc.scalar.activation(rstd[:], rstd[:], ACT.Exp, scale=-0.5).then_inc(ha["r"], 1)
                act.wait_ge(ha["o"], h + 1)
                nc.scalar.activation(o2h[:, bass.ds(h, 1), :].rearrange("p a s -> p (a s)"), a_p1[:, 0, :],
                                     ACT.Copy).then_inc(ha["hi"], 1)
            end_phase(act, "heads")
            begin_after(act, "heads")
            with act.Fori(0, 2) as i:
                for j in range(4):
                    split_high(act, U_AO + j + 1, i, 4)
            end_phase(act, "ao")
            begin_after(act, "ao")
            for k in range(KT):
                square_tile(act, nm4, k, hc[:, k, :], SC)
            make_rstd(act, nm4, SC, 6)
            for k in range(KT):
                nm4.wait(act, "t", k + 1)
                nc.scalar.activation(x2h[:, k, :], xn2[:, k % 2, :],
                                     ACT.Copy).then_inc(nm4.hi, 1)
            end_phase(act, "norm4")
            begin_after(act, "norm4")
            act.dma_start(bm0[:], t["bm0"]).then_inc(tab_in, 16)
            act.dma_start(bm1[:], t["bm1"]).then_inc(tab_in, 16)
            for u in range(N_B):
                split_high(act, U_B + u + 1)
                unit_done(act, U_B + u)
                b = u % 2
                if u < 8:
                    nc.scalar.activation(b_q[:, u, :], ps[:, 2 * b], ACT.Copy, scale=-0.125).then_inc(hb["free"], 1)
                elif u < 10:
                    nc.scalar.activation(b_k[:, u - 8, :], pair(b)[:, 0:SC], ACT.Copy).then_inc(hb["free"], 1)
                elif u < 12:
                    nc.scalar.activation(b_vT[:, u - 10, :], pair(b)[:, 0:SC], ACT.Copy).then_inc(hb["free"], 1)
                else:
                    nc.scalar.activation(b_g[:, u - 12, :], ps[:, 2 * b], ACT.Tanh, scale=0.5).then_inc(hb["gt"], 1)
                    if u == 14:
                        pass
            end_phase(act, "bqkv")
            begin_after(act, "bqkv")
            attn_act(act, A2)
            end_phase(act, "battn")
            begin_after(act, "battn")
            for j in range(N_OUT):
                split_high(act, U_BO + j + 1)
            for k in range(KT):
                act.wait_ge(wo_free[2], 2 + k + 1)
                square_tile(act, nm5, k, hc[:, k, 0:S], S)
            make_rstd(act, nm5, S, 4)

        @block.vector
        def _(v):
            nc.vector.memset(ones[:], 1.0)
            nc.vector.memset(eps_t, EPS)
            nc.vector.memset(seps_t, SUB_EPS)
            nc.vector.memset(fh[:].bitcast(F32), 0.0)
            nc.vector.memset(fl[:].bitcast(F32), 0.0)
            nc.vector.memset(kcmp[:], 0.0).then_inc(boot, 1)
            v.wait_ge(const_in, CONSTS)
            done(nc.vector.tensor_scalar(nsinks, sinks, -1.0, None, ALU.mult))
            done(nc.vector.tensor_scalar(subs, subg, 0.5 * (1.0 - LAM_INIT), None, ALU.mult))
            v.wait_ge(cvec, 1)
            lv = lamv[0:HD].rearrange("p (a b) -> p a b", b=2)
            nc.vector.tensor_tensor(lamp[0:HD], lv[:, :, 0], lv[:, :, 1], ALU.mult).then_inc(boot, 2)
            for k in range(KT):
                add_square(v, nm1, k, S)
            v.wait_ge(cvec, 2)
            done(nc.vector.scalar_tensor_tensor(out=cs, in0=ct, scalar=1.0, in1=cin, op0=ALU.add, op1=ALU.mult))
            settle(v)
            done(nc.vector.tensor_scalar(cs, cs, 0.5, None, ALU.mult))
            nc.vector.tensor_copy(brow[:, 0:512], ps[0:16, 6, :]).then_inc(brow_ok, 1)
            nc.vector.tensor_copy(brow[:, 512:640], ps[0:16, 7, 0:128]).then_inc(brow_ok, 1)
            nc.vector.tensor_copy(lame, ps[:, 5, 0:2]).then_inc(boot, 1)
            v.wait_ge(cvec, 3)
            done(nc.vector.tensor_scalar(lam, lame[:, 0:1], lame[:, 1:2], LAM_INIT, ALU.subtract, ALU.add))

            def normed(nm, k, src, gain, dst_t, lo_dst, hi_src, n, shift=None):
                if k >= 2:
                    nm.wait(v, "lo", k - 1)
                if shift is None:
                    nc.vector.scalar_tensor_tensor(out=dst_t(k), in0=src, scalar=gain, in1=rstd[:, 0:n],
                                                   op0=ALU.mult, op1=ALU.mult).then_inc(nm.t, 1)
                else:
                    for a, b, gn, sh in shift:
                        done(nc.vector.scalar_tensor_tensor(out=dst_t(k)[:, a:b], in0=src[:, a:b], scalar=gn,
                                                            in1=rstd[:, a:b], op0=ALU.mult, op1=ALU.mult))
                    settle(v)
                    for x, (a, b, gn, sh) in enumerate(shift):
                        ins = nc.vector.tensor_scalar(dst_t(k)[:, a:b], dst_t(k)[:, a:b], sh, None, ALU.add)
                    ins.then_inc(nm.t, 1)

            def lowed(nm, k, dst_t, lo_dst, hi_src):
                nm.wait(v, "hi", k + 1)
                nc.vector.tensor_tensor(lo_dst(k), dst_t(k), hi_src(k).bitcast(F32), ALU.subtract).then_inc(nm.lo, 1)

            def norm_tiles(nm, src, gain, dst_t, lo_dst, hi_src, n, shift=lambda k: None):
                nm.wait(v, "r", 1)
                for k in range(KT):
                    normed(nm, k, src(k), gain(k), dst_t, lo_dst, hi_src, n, shift(k))
                    if k:
                        lowed(nm, k - 1, dst_t, lo_dst, hi_src)
                lowed(nm, KT - 1, dst_t, lo_dst, hi_src)

            norm_tiles(nm1, lambda k: xin[:, k, :], lambda k: gains[:, G_MIX_PRE, k:k + 1], lambda k: xn[:, k % 2, 0:S],
                       lambda k: x1l[:, k, :], lambda k: x1h[:, k, :], S)
            r = 0
            for u in range(N_ATT):
                if 2 <= u < 10:
                    if u % 2 == 1:
                        unit_done(v, u)
                        c = (u - 2) // 2
                        done(nc.vector.tensor_copy(hbias[:, c:c + 1], ps[:, r % 2, 64:65]))
                        settle(v)
                        src = ps[:, r % 2, 0:64].rearrange("p (g n) -> p g n", g=2)[:, :, 0:NCMP]
                        nc.vector.tensor_scalar(hid[:, c, :].rearrange("p (g n) -> p g n", g=2), src, hbias[:, c:c + 1], None,
                                                ALU.add).then_inc(res_free, 1)
                        r += 1
                    if u == 9:
                        v.wait_ge(res_free, 6)
                        done(nc.vector.tensor_tensor(gl1[:], hid[:], hid[:], ALU.mult))
                        settle(v)
                        done(nc.vector.tensor_scalar(gl1[:], gl1[:], 0.044715, 1.0, ALU.mult, ALU.add))
                        settle(v)
                        nc.vector.tensor_tensor(gl1[:], gl1[:], hid[:], ALU.mult).then_inc(gel_t, 1)
                    continue
                if u in (0, 1):
                    for g in range(2):
                        for op in range(2):
                            v.wait_ge(f_hi, 6 * u + 4)
                            src = ps[g * HD:(g + 1) * HD, u % 2].rearrange("p (t o) -> p t o", o=2)[:, :, op]
                            dsl = (slice(op * HD, (op + 1) * HD), u, slice(g * 256, (g + 1) * 256))
                            ins = nc.vector.tensor_tensor(fl[dsl], src, fh[dsl].bitcast(F32), ALU.subtract)
                    ins.then_inc(res_free, 1)
                    v.wait_ge(f_hi, 6 * u + 6)
                    for a, b in ((0, 8), (8, 16)):
                        ins = nc.vector.tensor_tensor(fl[:, u, 512 + a:512 + b], pos[:, u, a:b],
                                                      fh[:, u, 512 + a:512 + b].bitcast(F32), ALU.subtract)
                    ins.then_inc(f_lo, 1)
                elif u < 14:
                    unit_done(v, u)
                    nc.vector.tensor_scalar(q_n[:, u - 10, :], ps[:, r % 2], -0.125, None, ALU.mult).then_inc(res_free, 1)
                elif u < 16:
                    unit_done(v, u)
                    nc.vector.tensor_copy(k_all[:, u - 14, :], ps[:, r % 2]).then_inc(res_free, 1)
                elif u < 18:
                    unit_done(v, u)
                    nc.vector.tensor_copy(vT[:, u - 16, :], ps[:, r % 2]).then_inc(res_free, 1)
                elif u == 18:
                    v.wait_ge(th_a, 2)
                    done(nc.vector.tensor_scalar(hbias[:, 0:1], lam, 1.0, None, ALU.mult))
                    settle(v)
                    nc.vector.tensor_copy(hbias[:, 1:2], hbias[:, 0:1]).then_inc(res_free, 1)
                elif u < 23:
                    unit_done(v, u)
                    nc.vector.tensor_scalar(q_s[:, u - 19, :], ps[:, r % 2], -0.125, None, ALU.mult).then_inc(res_free, 1)
                elif u == 23:
                    unit_done(v, u)
                    nc.vector.tensor_copy(k_all[:, 2, :], ps[:, r % 2]).then_inc(res_free, 1)
                else:
                    unit_done(v, u)
                    nc.vector.tensor_copy(vT[:, 2, :], ps[:, r % 2]).then_inc(res_free, 1)
                r += 1
                if u == 10:
                    v.wait_ge(th_a, 1)
                    done(nc.vector.scalar_tensor_tensor(out=gl3[:], in0=gl2[:], scalar=1.0, in1=hid[:], op0=ALU.add,
                                                        op1=ALU.mult))
                    settle(v)
                    nc.vector.tensor_scalar(gl3[:], gl3[:], 0.5, None, ALU.mult).then_inc(gel, 1)
            v.wait_ge(pr_mm, 1)
            nc.vector.tensor_copy(kcmp[:, 0:NCMP], ps[:, 2, 0:NCMP])
            nc.vector.tensor_copy(vcmp[0:NCMP].rearrange("p g d -> p (g d)"), ps[0:NCMP, 3, 0:P])
            for n in range(4):
                v.wait_ge(pr_mm, n + 2)
                if n < 3:
                    nc.vector.tensor_copy(v_all[:, n].rearrange("p t d -> p (t d)"), ps[:, 4 + n])
                else:
                    nc.vector.tensor_scalar(gate[:].rearrange("p t d -> p (t d)"), ps[:, 4 + n], 0.5, 0.5, ALU.mult, ALU.add)
            end_phase(v, "prep")
            begin_after(v, "prep")
            v.wait_ge(strips_in, 32)
            attn_dve(v, A1)
            end_phase(v, "nsa")
            begin_after(v, "nsa")
            v.drain().then_inc(up_free, 2)
            with v.Fori(0, 2) as i:
                for m in range(4):
                    b = m % 2
                    unit_done(v, U_UP + m * 3 + 2, i, 12)
                    v.wait_ge(up_t, i * 8 + (2 * m + 2))
                    for j in range(2):
                        ins = nc.vector.scalar_tensor_tensor(out=tg[:, b, j, :], in0=tg[:, b, j, :], scalar=1.0,
                                                             in1=ps[:, 4 + 2 * j + b], op0=ALU.add, op1=ALU.mult)
                        ins.then_inc(up_v, 1)
                    v.wait_ge(up_v, i * 12 + (3 * m + 2))
                    nc.vector.tensor_tensor(tg[:, b, 0, :], tg[:, b, 0, :], tg[:, b, 1, :], ALU.add).then_inc(up_v, 1)
                    v.wait_ge(up_v, i * 12 + (3 * m + 3))
                    nc.vector.tensor_scalar(ty[:, b, :], tg[:, b, 0, :], 0.5, None, ALU.mult).then_inc(up_y, 1)
                    v.wait_ge(up_hi, i * 4 + (m + 1))
                    yi = bass.ds(i * 4 + m, 1)
                    nc.vector.tensor_tensor(y1l[:, yi, :].rearrange("p a s -> p (a s)"), ty[:, b, :],
                                            y1h[:, yi, :].rearrange("p a s -> p (a s)").bitcast(F32),
                                            ALU.subtract).then_inc(up_free, 1)
            end_phase(v, "up")
            begin_after(v, "up")
            nc.vector.memset(sqsum[:, 0:S], 0.0).then_inc(nm2a.add, 2)
            nm2a.wait(v, "add", 2)
            v.drain().then_inc(wo_free[0], 2)
            with v.Fori(0, 2) as i:
                for j in range(4):
                    v.wait_ge(wo_free[0], i * 4 + (j + 3))
                    nm2a.wait(v, "add", i * 4 + (j + 2))
                    nc.vector.tensor_tensor(sqsum[:, 0:S], sqsum[:, 0:S], sq[:, j % 2, 0:S], ALU.add).then_inc(nm2a.add, 1)
            nm2a.wait(v, "r", 1)
            end_phase(v, "wout")
            begin_after(v, "wout")
            v.wait_ge(x_in, 32)

            def post_norm(nmb, gain_row, n2):
                for k in range(KT):
                    done(nc.vector.scalar_tensor_tensor(out=f_t[:, k, :], in0=f_t[:, k, :], scalar=gains[:, gain_row, k:k + 1],
                                                        in1=rstd[:, 0:S], op0=ALU.mult, op1=ALU.mult))
                for k in range(KT):
                    settle(v)
                    nc.vector.tensor_tensor(hc[:, k, 0:S], hc[:, k, 0:S], f_t[:, k, :], ALU.add).then_inc(nmb.src, 1)
                    if k:
                        add_square(v, nmb, k - 1, n2)
                add_square(v, nmb, KT - 1, n2)
            post_norm(nm2b, G_MIX_POST, S)
            norm_tiles(nm2b, lambda k: hc[:, k, 0:S], lambda k: gains[:, G_MLP_PRE, k:k + 1], lambda k: xn2[:, k % 2, 0:S],
                       lambda k: x1l[:, k, :], lambda k: x1h[:, k, :], S)
            nc.vector.memset(f_t[:], 0.0).then_inc(f_zero, 1)
            end_phase(v, "norm2")
            begin_after(v, "norm2")
            v.drain().then_inc(ml_f, 2)
            v.drain().then_inc(mod_ev, 1)
            v.wait_ge(f_zero, 1)
            with v.Fori(0, 4) as i:
                for j in range(16):
                    unit_done(v, U_MLP + j, i, 16)
                    if j < 8:
                        v.wait_ge(ml_relu, i * 8 + (j + 1))
                        nc.vector.scalar_tensor_tensor(out=msq[:, j % 2, :], in0=ps[:, j % 2], scalar=0.0, in1=relu[:, j % 2, :],
                                                       op0=ALU.max, op1=ALU.mult).then_inc(ml_sq, 1)
                        v.wait_ge(ml_hi, i * 8 + (j + 1))
                        nc.vector.tensor_tensor(m_l[:, j, :], msq[:, j % 2, :], m_h[:, j, :].bitcast(F32),
                                                ALU.subtract).then_inc(ml_lo, 1)
                        v.wait_ge(ml_lo, i * 8 + (j + 1))
                        nc.vector.memset(esk[:, 0:1], 0.0).then_inc(ml_f, 1)
                    else:
                        nc.vector.tensor_tensor(f_t[:, j - 8, :], ps[:, j % 2], f_t[:, j - 8, :], ALU.add).then_inc(ml_f, 1)
                v.wait_ge(mod_mm, i * 12 + 12)
                nc.vector.tensor_tensor(mod[:, bass.ds(i * 12, 12), :], ps[:, 7, 0:24].rearrange("p (c v) -> p c v", v=2),
                                        bmod[:, bass.ds(i * 12, 12)].unsqueeze(2).to_broadcast([P, 12, 2]),
                                        ALU.add).then_inc(mod_ev, 1)
            for k in range(KT):
                add_square(v, nm3a, k, S)
            v.wait_ge(mod_ev, 5)
            for l in range(2):
                for w in range(2):
                    done(nc.vector.scalar_tensor_tensor(out=mulx[:, l, w, :], in0=mod[:, l * 24 + 8:l * 24 + 16, w], scalar=1.0,
                                                        in1=gains[:, G_A + l, :], op0=ALU.add, op1=ALU.mult))
            settle(v)
            nm3a.wait(v, "r", 1)
            end_phase(v, "mlp")
            begin_after(v, "mlp")
            v.wait_ge(ctx_in, 16)
            post_norm(nm3b, G_MLP_POST, SC)

            def modulated(nm, l, dst):
                norm_tiles(nm, lambda k: hc[:, k, :], lambda k: None, dst, lambda k: x2l[:, k, :], lambda k: x2h[:, k, :], SC,
                           lambda k: [(0, S, mulx[:, l, 0, k:k + 1], mod[:, l * 24 + k, 0:1]),
                                      (S, SC, mulx[:, l, 1, k:k + 1], mod[:, l * 24 + k, 1:2])])
            modulated(nm3b, 0, lambda k: xn2[:, k % 2, :])
            end_phase(v, "norm3")
            begin_after(v, "norm3")
            v.wait_ge(tab_in, 32)
            for n in ("e", "r", "lo", "ro"):
                v.drain().then_inc(ha[n], 1)
            with v.Fori(0, 8) as h:
                for n, (x, ready) in enumerate(((a_q, "q"), (a_k, "k"))):
                    v.wait_ge(ha[ready], h + 1)
                    v.wait_ge(ha["ro"], h * 2 + (n + 1))
                    nc.vector.tensor_tensor(ropea[:, 2, :], x[:, 0:S], cos_t[:], ALU.mult).then_inc(ha["c"], 1)
                    nc.vector.stream_shuffle(ropea[:, 0, :], x[:, 0:S], SHUFFLE).then_inc(ha["c"], 1)
                    v.wait_ge(ha["c"], h * 6 + (3 * n + 2))
                    nc.vector.tensor_tensor(ropea[:, 1, :], ropea[:, 0, :], sin_t[:], ALU.mult).then_inc(ha["c"], 1)
                    v.wait_ge(ha["c"], h * 6 + (3 * n + 3))
                    nc.vector.tensor_tensor(x[:, 0:S], ropea[:, 1, :], ropea[:, 2, :], ALU.add).then_inc(ha["ro"], 1)
                v.wait_ge(ha["gt"], h + 1)
                nc.vector.scalar_tensor_tensor(out=a_g[:], in0=a_g[:], scalar=1.0, in1=pair(1)[:, 0:SC], op0=ALU.add,
                                               op1=ALU.mult).then_inc(ha["g"], 1)

                def mins(qt):
                    n = SC if qt < QT else C
                    for m in range(2):
                        v.wait_ge(ha["s"], h * 12 + (2 * qt + m + 1))
                        c = 2 * (qt % 2) + m
                        nc.vector.tensor_reduce(negm[:, c:c + 1], pair(m)[:, 0:n], AX.X, ALU.min).then_inc(ha["m"], 1)

                def combine(qt):
                    n = SC if qt < QT else C
                    c = 2 * (qt % 2)
                    v.wait_ge(ha["e"], h * 12 + (2 * qt + 3))
                    nc.vector.reciprocal(rs[:, c:c + 2], sums[:, c:c + 2]).then_inc(ha["w"], 1)
                    v.wait_ge(ha["w"], h * 18 + (3 * qt + 1))
                    nc.vector.tensor_tensor(wgt[:, c:c + 1], rs[:, c + 1:c + 2], lam, ALU.mult).then_inc(ha["w"], 1)
                    v.wait_ge(ha["w"], h * 18 + (3 * qt + 2))
                    pp = a_p[qt % 2]
                    nc.vector.tensor_scalar(pp[:, 1, 0:n], pp[:, 1, 0:n], wgt[:, c:c + 1], None, ALU.mult).then_inc(ha["w"], 1)
                    v.wait_ge(ha["w"], h * 18 + (3 * qt + 3))
                    nc.vector.scalar_tensor_tensor(out=pp[:, 0, 0:n], in0=pp[:, 0, 0:n], scalar=rs[:, c:c + 1],
                                                   in1=pp[:, 1, 0:n], op0=ALU.mult, op1=ALU.subtract).then_inc(ha["a"], 1)
                mins(0)
                for qt in range(6):
                    combine(qt)
                    if qt < 5:
                        mins(qt + 1)
                v.wait_ge(ha["r"], h + 2)
                nc.vector.scalar_tensor_tensor(out=a_p1[:, 1, :], in0=pair(3)[:, 0:SC], scalar=subs, in1=rstd[:], op0=ALU.mult,
                                               op1=ALU.mult).then_inc(ha["on"], 1)
                v.wait_ge(ha["on"], h + 1)
                nc.vector.tensor_tensor(a_p1[:, 0, :], a_p1[:, 1, :], a_g[:], ALU.mult).then_inc(ha["o"], 1)
                v.wait_ge(ha["hi"], h + 1)
                nc.vector.tensor_tensor(o2l[:, bass.ds(h, 1), :].rearrange("p a s -> p (a s)"), a_p1[:, 0, :],
                                        o2h[:, bass.ds(h, 1), :].rearrange("p a s -> p (a s)").bitcast(F32),
                                        ALU.subtract).then_inc(ha["lo"], 1)
            end_phase(v, "heads")
            begin_after(v, "heads")

            def residual(n, l, u0, wide):
                v.drain().then_inc(wo_free[n], 2)
                with v.Fori(0, 2) as i:
                    for j in range(4):
                        unit_done(v, u0 + j, i, 4)
                        k = bass.ds(i * 4 + j, 1)
                        gcol = mod[:, bass.ds(l * 24 + 16 + i * 4 + j, 1), :].rearrange("p a v -> p (a v)")
                        for w, a, b in ((0, 0, S), (1, S, SC))[0:1 + wide]:
                            src = (pair(j % 2) if wide else ps[:, j % 2])[:, a:b]
                            hk = hc[:, k, a:b].rearrange("p a s -> p (a s)")
                            ins = nc.vector.scalar_tensor_tensor(out=hk, in0=src, scalar=gcol[:, w:w + 1], in1=hk,
                                                                 op0=ALU.mult, op1=ALU.add)
                        ins.then_inc(wo_free[n], 1)
            residual(1, 0, U_AO, 1)
            end_phase(v, "ao")
            begin_after(v, "ao")
            for k in range(KT):
                add_square(v, nm4, k, SC)
            modulated(nm4, 1, lambda k: xn2[:, k % 2, :])
            end_phase(v, "norm4")
            begin_after(v, "norm4")
            for u in range(N_B):
                if u < 10:
                    x = b_q[:, u, :] if u < 8 else b_k[:, u - 8, 0:S]
                    v.wait_ge(hb["free"], u + 1)
                    nc.vector.stream_shuffle(ropeb[:, 0, :], x, SHUFFLE)
                    done(nc.vector.tensor_tensor(ropeb[:, 2, :], x, cos_t[:], ALU.mult))
                    settle(v)
                    done(nc.vector.tensor_tensor(ropeb[:, 1, :], ropeb[:, 0, :], sin_t[:], ALU.mult))
                    settle(v)
                    done(nc.vector.tensor_tensor(x, ropeb[:, 1, :], ropeb[:, 2, :], ALU.add))
                    settle(v)
                elif u >= 12:
                    v.wait_ge(hb["gt"], u - 11)
                    nc.vector.scalar_tensor_tensor(out=b_g[:, u - 12, :], in0=b_g[:, u - 12, :], scalar=1.0, in1=ps[:, 2 * (u % 2)],
                                                   op0=ALU.add, op1=ALU.mult).then_inc(hb["free"], 1)
                if u == 13:
                    for n in range(2):
                        v.wait_ge(hb["vt"], n + 1)
                        nc.vector.tensor_copy(b_v[:, :, n * P:(n + 1) * P],
                                              pair(2)[:, 0:SC].rearrange("p (b d) -> p b d", b=6)).then_inc(hb["ve"], 1)
            v.wait_ge(tab_in, 64)
            end_phase(v, "bqkv")
            begin_after(v, "bqkv")
            attn_dve(v, A2)
            end_phase(v, "battn")
            begin_after(v, "battn")
            residual(2, 1, U_BO, 0)
            for k in range(KT):
                add_square(v, nm5, k, S)
            nm5.wait(v, "r", 1)
            for k in range(KT):
                nc.vector.scalar_tensor_tensor(out=xo[:, k, :], in0=hc[:, k, 0:S], scalar=gains[:, G_FINAL, k:k + 1],
                                               in1=rstd[:, 0:S], op0=ALU.mult, op1=ALU.mult).then_inc(nm5.t, 1)


def _units(w):
    import numpy as np
    k, m = w.shape
    return np.ascontiguousarray(w.reshape(k // 1024, 8, 128, m // 128, 128).transpose(3, 0, 2, 1, 4))


def _tables():
    import math
    import numpy as np
    f = np.float32
    dist = 511 - np.arange(TBL)
    d = np.maximum(dist, 0)
    df = np.maximum(d, 1).astype(f)
    large = 16 + (np.log(df / f(16)) / f(math.log(1024 / 16)) * f(16)).astype(np.int32)
    bucket = np.where(d < 16, d, np.minimum(large, BUCKETS - 1))
    onehot = np.zeros((34, TBL), f)
    onehot[bucket, np.arange(TBL)] = -1.0
    onehot[32] = np.where(dist >= 0, 0.0, BIG)
    onehot[33] = np.where((dist >= 0) & (dist < 128), 0.0, BIG)
    selrows = np.zeros((2, 16), f)
    selrows[0, 0:8] = 1.0
    selrows[1, 8:16] = 1.0
    p = np.arange(P)
    tq = np.arange(QT)[None, :] * P + p[:, None]
    cmask = np.where(np.arange(NCMP)[None, None, :] * 16 + 31 <= tq[:, :, None], 0.0, BIG).astype(f)
    band = np.where(np.abs(p[:, None] - np.arange(384)[None, :] + 128) <= 128, 0.0, BIG).astype(f)
    bm1 = np.concatenate([np.zeros((P, C), f), band], 1)
    bm0 = np.concatenate([np.zeros((P, C), f), band[:, 128:384]], 1)
    tok = np.arange(S)
    inv = f(10000.0) ** (-np.arange(0, 32, 2, dtype=f) / f(32))
    row, col = (tok // 64).astype(f), (tok % 64).astype(f)
    feat = np.arange(64)
    ang = np.where((feat < 32)[:, None], row[None, :], col[None, :]).astype(f) * inv[feat % 16][:, None]
    cos, sin = np.cos(ang).astype(f), np.sin(ang).astype(f)
    sin = np.where((feat % 32 < 16)[:, None], -sin, sin)
    return dict(ident=np.eye(P, dtype=f), onehot=onehot, selrows=selrows, cmask=cmask, bm0=bm0, bm1=bm1,
                cos=np.concatenate([cos, cos], 0), sin=np.concatenate([sin, sin], 0))


def kernel(x, norm_mix_pre, norm_mix_post, norm_mlp_pre, norm_mlp_post, w_in, cmp_pos_k, cmp_w1_k, cmp_w2_k, cmp_pos_v,
           cmp_w1_v, cmp_w2_v, attn_sinks, rel_bias, w_up_nsa, w_up_swa, w_out, w_mlp_in, w_mlp_out, c_2, ctx_2, c_ctx_2,
           w_mod_2, b_mod_2, norm_g_2, w_o_2, a_w_in_2, a_lambda_q1_2, a_lambda_k1_2, a_lambda_q2_2, a_lambda_k2_2,
           a_subln_g_2, b_w_in_2, b_sink_2, final_g_2):
    import numpy as np
    import concourse.bacc as bacc
    from concourse import mybir as mb
    from concourse.bass_utils import run_bass_kernel_spmd

    def cols(a):
        a = np.asarray(a)
        return np.moveaxis(a.reshape(a.shape[:-1] + (-1, P)), -1, 0)

    def tmajor(a):
        a = np.asarray(a)
        return a.reshape(a.shape[0], KT, P).transpose(2, 1, 0)

    def pair_heads(n_kv, rep, w):
        i = np.arange(n_kv * rep * HD).reshape(n_kv // 2, 2, rep, HD)
        return w + i.transpose(0, 2, 1, 3).reshape(-1)

    w_in = np.asarray(w_in)[0]
    qn = pair_heads(2, 4, 0)
    w_att = [_units(w_in[:, 512:768])[:, 0]]
    for w in (cmp_w1_k, cmp_w1_v):
        w_att.append(_units(np.asarray(w)[0]).reshape(4, P, KT, P))
    gcols = np.zeros((D, P), np.float32)
    gcols[:, 0:24] = w_in[:, 1280:1304]
    att_cols = np.concatenate([w_in[:, qn], w_in[:, 768:896], w_in[:, 1024:1152], w_in[:, 896:1024], w_in[:, 1152:1280],
                               gcols, w_in[:, 1304 + qn], w_in[:, 1816:1944], w_in[:, 1944:2072]], 1)
    w_att.append(_units(att_cols)[:, 0])
    ga, gb = _units(w_in[:, 2072:3096])[:, 0], _units(w_in[:, 3096:4120])[:, 0]
    up = np.concatenate([np.asarray(w_up_nsa)[0][qn], np.asarray(w_up_swa)[0][qn]], 0)
    w_up = np.stack([ga, gb, _units(up)[:, 0]], 1).reshape(24, P, KT, P)
    m_in = _units(np.asarray(w_mlp_in)[0])[:, 0].reshape(4, 8, P, KT, P)
    m_out = _units(np.asarray(w_mlp_out)[0]).transpose(1, 0, 2, 3, 4)
    w_mlp = np.concatenate([m_in, m_out], 1).reshape(64, P, KT, P)
    w_mod = np.concatenate([_units(np.asarray(w_mod_2)[l])[:, 0] for l in range(2)], 0)
    w_mod = np.concatenate([w_mod, w_mod[0:3]], 0)
    w_a = _units(np.asarray(a_w_in_2)[0])[:, 0].reshape(4, 8, P, KT, P).transpose(1, 0, 2, 3, 4).reshape(32, P, KT, P)
    wo = np.asarray(w_o_2)
    bw = np.asarray(b_w_in_2)[0]
    bq = pair_heads(4, 4, 0)
    w_b = _units(np.concatenate([bw[:, bq], bw[:, 1024:1536], bw[:, 1536 + bq]], 1))[:, 0]
    w2 = np.stack([np.asarray(w)[0].reshape(2, P, HD) for w in (cmp_w2_k, cmp_w2_v)], 0).transpose(2, 0, 1, 3)
    pos = np.stack([np.asarray(w)[0].reshape(16, P).T for w in (cmp_pos_k, cmp_pos_v)], 1)
    gains = np.stack([np.asarray(norm_mix_pre)[0], np.asarray(norm_mix_post)[0], np.asarray(norm_mlp_pre)[0],
                      np.asarray(norm_mlp_post)[0], np.asarray(norm_g_2)[0], np.asarray(norm_g_2)[1],
                      np.asarray(final_g_2)], 0)
    ins = dict(_tables())
    ins.update(
        xT=tmajor(np.asarray(x)[0]), ctxT=tmajor(np.asarray(ctx_2)[0]), gains=cols(gains),
        bmod=cols(np.asarray(b_mod_2)).reshape(P, 48),
        cin=cols(np.stack([np.asarray(c_2)[0], np.asarray(c_ctx_2)], 0)).transpose(0, 2, 1).reshape(P, 16),
        lamv=np.stack([np.asarray(a)[0] for a in (a_lambda_q1_2, a_lambda_k1_2, a_lambda_q2_2, a_lambda_k2_2)], 1),
        subg=np.asarray(a_subln_g_2)[0].reshape(P, 1), w2=w2, pos=pos, rel_bias=np.asarray(rel_bias),
        sinks=np.concatenate([np.asarray(attn_sinks)[0], np.asarray(b_sink_2)[0]]).reshape(1, 24),
        w_att=np.concatenate(w_att, 0), w_up=w_up, w_out=_units(np.asarray(w_out)[0])[:, 0], w_mlp=w_mlp, w_mod=w_mod,
        w_a=w_a, w_ao=_units(wo[0])[:, 0], w_b=w_b, w_bo=_units(wo[1][bq])[:, 0])
    nc = bacc.Bacc("TRN2", target_bir_lowering=False, num_devices=1)
    arrays, t = {}, {}
    for name, a in ins.items():
        a = np.ascontiguousarray(a)
        arrays["in_" + name] = a
        t[name] = nc.dram_tensor("in_" + name, a.shape, mb.dt.from_np(a.dtype), kind="ExternalInput").ap()
    out = nc.dram_tensor("out", (P, KT, S), mb.dt.float32, kind="ExternalOutput").ap()
    build(nc, t, out)
    r = run_bass_kernel_spmd(nc, [arrays], core_ids=[0])
    y = r.results[0]["out"]
    return np.ascontiguousarray(y.transpose(2, 1, 0).reshape(1, S, D))
```

```python
from contextlib import ExitStack

import concourse.bass as bass
from concourse import mybir

F32 = mybir.dt.float32
F32R = mybir.dt.float32r
ALU = mybir.AluOpType
ACT = mybir.ActivationFunctionType
AX = mybir.AxisListType

P = 128
D = 1024
KT = D // P
S = 512
C = 256
SC = S + C
QT = S // P
HD = 64
REP = 4
NCMP = 31
HID = 256
EPS = 1e-6
SUB_EPS = 1e-5
LAM_INIT = 0.8 - 0.6
BIG = 1e30
GELU_C = 0.7978845608028654
RAW = 4
MRAW = 4
SPL = 2
BUCKETS = 32
TBL = 640

N_ATT = 25
N_UP = 24
N_OUT = 8
N_MLP = 64
N_MOD = 48
N_A = 32
N_B = 20
U_ATT = 0
U_UP = U_ATT + N_ATT
U_OUT = U_UP + N_UP
U_MLP = U_OUT + N_OUT
U_A = U_MLP + N_MLP
U_AO = U_A + N_A
U_B = U_AO + N_OUT
U_BO = U_B + N_B
U_END = U_BO + N_OUT

G_MIX_PRE, G_MIX_POST, G_MLP_PRE, G_MLP_POST, G_A, G_B, G_FINAL = range(7)
SHUFFLE = [(i + 16) % 32 for i in range(32)]


def build(nc, t, out):
    base = 16512
    KB = 1024
    with ExitStack() as ctx:
        def at(name, kb, shape, dt=F32):
            return nc.alloc_sbuf_tensor_at(name, shape, dt, offset=base + int(kb * KB))

        def sem(name):
            return ctx.enter_context(nc.semaphore(name))

        raw = at("raw", 0, [P, RAW, KT, P])
        w_h = at("w_h", 16, [P, SPL, KT, P], F32R)
        w_l = at("w_l", 24, [P, SPL, KT, P], F32R)
        x1h = at("x1h", 32, [P, KT, S], F32R)
        x1l = at("x1l", 48, [P, KT, S], F32R)
        x2h = at("x2h", 32, [P, KT, SC], F32R)
        x2l = at("x2l", 56, [P, KT, SC], F32R)
        hc = at("hc", 80, [P, KT, SC])
        c0 = 104
        ident = at("ident", c0, [P, P])
        ones = at("ones", c0 + 0.5, [P, P])
        small = at("small", c0 + 1, [P, 896])
        rstd = at("rstd", c0 + 4.5, [P, SC])
        sq = at("sq", c0 + 7.5, [P, 2, SC])
        sqsum = at("sqsum", c0 + 13.5, [P, SC])
        z = c0 + 16.5

        o_ = [0]

        def sm(n):
            a = small[:, o_[0]:o_[0] + n]
            o_[0] += n
            return a
        gains = sm(56).rearrange("p (g k) -> p g k", g=7)
        bmod = sm(48)
        cin = sm(16)
        ct = sm(16)
        cs = sm(16)
        mod = sm(96).rearrange("p (c v) -> p c v", v=2)
        sinks = sm(24)
        nsinks = sm(24)
        lamv = sm(4)
        lamp = sm(2)
        lame = sm(2)
        lam = sm(1)
        subg = sm(1)
        subs = sm(1)
        eps_t = sm(1)
        seps_t = sm(1)
        negm = sm(8)
        sums = sm(8)
        rs = sm(8)
        wgt = sm(8)
        esk = sm(8)
        spare = sm(1)
        zero = sm(1)
        tick = sm(1)
        mulx = sm(32).rearrange("p (l v k) -> p l v k", l=2, v=2)
        assert o_[0] <= 896

        q_n = at("q_n", 64, [P, REP, S])
        q_s = at("q_s", 72, [P, REP, S])
        k_all = at("k_all", 80, [P, 3, S])
        v_all = at("v_all", 86, [P, 3, QT, P])
        gate = at("gate", 92, [P, QT, P])
        strip_s = at("strip_s", 94, [P, 8, 256])
        kcmp = at("kcmp", 102, [P, 32])
        vcmp = at("vcmp", 102.25, [P, 2, HD])
        cmask = at("cmask", 102.75, [P, QT, NCMP])
        strip_n = at("strip_n", z, [P, 8, S])
        sb1 = [at("sb1_0", z + 16, [P, REP, S]), at("sb1_1", z + 24, [P, REP, S]), at("sb1_2", z + 72, [P, REP, S])]
        vT = at("vT", z + 32, [P, 4, S])
        pt1 = at("pt1", z + 32, [P, 4, S])
        o1h = at("o1h", z + 40, [P, 8, S], F32R)
        o1l = at("o1l", z + 56, [P, 8, S], F32R)
        xin = at("xin", z + 40, [P, KT, S])
        xn = at("xn", z + 56, [P, 2, SC])
        FW = 3 * 256 + 8
        fh = at("fh", z + 16, [P, 2, FW], F32R)
        fl = at("fl", z + 16 + 6.25, [P, 2, FW], F32R)
        g0 = z + 72
        hid = at("hid", g0, [P, 4, 2 * NCMP])
        gl1 = at("gl1", g0 + 1, [P, 4, 2 * NCMP])
        gl2 = at("gl2", g0 + 2, [P, 4, 2 * NCMP])
        gl3 = at("gl3", g0 + 3, [P, 4, 2 * NCMP])
        hbias = at("hbias", g0 + 4, [P, 4])
        w2 = at("w2", g0 + 4.25, [P, 2, 2, HD])
        pos = at("pos", g0 + 5.25, [P, 2, 16])
        brow = at("brow", g0 + 5.5, [16, TBL])
        onehot = at("onehot", g0 + 8, [34, TBL])
        blhs = at("blhs", g0 + 10.5, [34, 16])
        y1h = at("y1h", z, [P, 8, S], F32R)
        y1l = at("y1l", z + 16, [P, 8, S], F32R)
        tg = at("tg", z + 72, [P, 2, 2, S])
        ty = at("ty", z + 80, [P, 2, S])
        f_t = at("f_t", z + 32, [P, KT, S])
        m_h = at("m_h", z, [P, 8, S], F32R)
        m_l = at("m_l", z + 16, [P, 8, S], F32R)
        relu = at("relu", z + 48, [P, 2, S])
        msq = at("msq", z + 52, [P, 2, S])
        mraw = at("mraw", z + 70, [P, MRAW, KT, P])
        xn2 = at("xn2", z + 64, [P, 2, SC])
        o2 = at("o2", z, [P, KT, SC])
        a_q = [at("a_q0", z + 48, [P, SC]), at("a_q1", z + 24, [P, SC])]
        a_k = [at("a_k0", z + 51, [P, SC]), at("a_k1", z + 27, [P, SC])]
        a_g = [at("a_g0", z + 54, [P, SC]), at("a_g1", z + 30, [P, SC])]
        a_vT = at("a_vT", z + 33, [P, SC])
        ropea = at("ropea", z + 36, [P, 3, S])
        a_sq = at("a_sq", z + 42, [P, SC])
        cos_t = at("cos_t", z + 57, [P, S])
        sin_t = at("sin_t", z + 59, [P, S])
        a_p = [[at(f"a_p{n}{m}", o, [P, SC]) for m, o in enumerate(os)]
               for n, os in enumerate(((z + 61, z + 64), (z + 67, z + 70), (z + 45, c0 + 9.5)))]
        a_pt = at("a_pt", z + 73, [P, 6, S])
        a_pt2 = at("a_pt2", c0 + 7.5, [P, 2, C])
        a_v = at("a_v", c0 + 13.5, [P, 6, P])
        b_q = at("b_q", z, [P, 8, S])
        b_k = at("b_k", z + 16, [P, 2, SC])
        b_v = at("b_v", z + 22, [P, 6, 256])
        b_g = at("b_g", z + 28, [P, 8, S])
        bm0 = at("bm0", z + 44, [P, 512])
        bm1 = at("bm1", z + 46, [P, 640])
        b_pt = at("b_pt", z + 48.5, [P, 4, S])
        ropeb = at("ropeb", z + 48.5, [P, 3, S])
        b_sb = [at("b_sb0", z + 60.5, [P, REP, 640]), at("b_sb1", z + 70.5, [P, REP, 640]),
                at("b_sb2", 64, [P, REP, 640])]
        b_vT = at("b_vT", z + 64, [P, 2, SC])
        ot = at("ot", z + 80.5, [P, S])
        xo = at("xo", z, [P, KT, S])

        ps = ctx.enter_context(nc.psum_tensor("ps", [P, 8, 512], F32))

        def pair(n):
            return ps[:, 2 * n:2 * n + 2].rearrange("p b c -> p (b c)")

        dbias = nc.dram_tensor("dbias", [16, P, TBL], F32, kind="Internal").ap()

        raw_in = [sem(f"raw_in{i}") for i in range(RAW)]
        w_hi = sem("w_hi")
        w_lo = sem("w_lo")
        unit = sem("unit")
        const_in = sem("const_in")
        boot = sem("boot")
        brow_ok = sem("brow_ok")
        dbias_in = sem("dbias_in")
        strips_in = sem("strips_in")
        x_in = sem("x_in")
        tab_in = sem("tab_in")
        ctx_in = sem("ctx_in")
        out_done = sem("out_done")
        v_self = sem("v_self")

        block = ctx.enter_context(nc.Block())

        PHASES = ["prep", "nsa", "up", "wout", "norm2", "mlp", "norm3", "heads", "ao", "norm4", "bqkv", "battn"]
        phase_end = sem("phase_end")

        def end_phase(eng, name):
            eng.drain().then_inc(phase_end, 1)

        def begin_after(eng, name):
            eng.wait_ge(phase_end, 3 * (PHASES.index(name) + 1))

        class Own:
            n = 0

        def done(ins):
            Own.n += 1
            ins.then_inc(v_self, 1)

        def settle(v):
            v.wait_ge(v_self, Own.n)

        def split_high(act, u, i=None, step=0):
            if u >= U_END and i is None:
                return
            v = lambda c: c if i is None else i * step + c
            assert step % RAW == 0
            act.wait_ge(raw_in[u % RAW], 16 * (u // RAW + 1) if i is None else i * (16 * step // RAW) + 16 * (u // RAW + 1))
            if u >= SPL:
                act.wait_ge(unit, v(u - SPL + 1))
            nc.scalar.activation(w_h[:, u % SPL], raw[:, u % RAW], ACT.Copy).then_inc(w_hi, 1)

        def load_unit(sp, u, src, i=None, step=0):
            if u >= RAW:
                sp.wait_ge(w_lo, u - RAW + 1 if i is None else i * step + (u - RAW + 1))
            sp.dma_start(raw[:, u % RAW], src).then_inc(raw_in[u % RAW], 16)

        def products(u, parts, k0=0, k1=KT, first=True, last=True):
            for k in range(k0, k1):
                for wi, w in ((0, w_h), (1, w_l)):
                    for o, xh, xl in parts:
                        mm = nc.tensor.matmul(o, w[:, u % SPL, k], xh(k), start=(first and k == k0 and wi == 0),
                                              stop=(last and k == k1 - 1 and wi == 1))
                    if wi == 0:
                        for o, xh, xl in parts:
                            mm = nc.tensor.matmul(o, w[:, u % SPL, k], xl(k), start=False, stop=False)
            return mm

        def split_ready(pe, u, i=None, step=0):
            pe.wait_ge(w_lo, u + 1 if i is None else i * step + (u + 1))

        def unit_done(eng, u, i=None, step=0):
            eng.wait_ge(unit, u + 1 if i is None else i * step + (u + 1))

        NORM_SEMS = ["src", "sq", "add", "mm", "ln", "r", "t", "hi", "lo"]

        class Norm:
            sems = {n: sem("norm_" + n) for n in NORM_SEMS}
            ends = dict.fromkeys(NORM_SEMS, 0)

            def __init__(self, **counts):
                self.base = dict(Norm.ends)
                for n in NORM_SEMS:
                    Norm.ends[n] += counts.get(n, 1 if n in ("mm", "ln", "r") else 8)
                self.src, self.sq, self.add, self.mm, self.ln, self.r, self.t, self.hi, self.lo = \
                    [Norm.sems[n] for n in NORM_SEMS]

            def wait(self, eng, name, count):
                eng.wait_ge(Norm.sems[name], self.base[name] + count)

        def square_tile(act, nm, k, src, n):
            if k >= 2:
                nm.wait(act, "add", k - 1)
            nc.scalar.activation(sq[:, k % 2, 0:n], src, ACT.Square).then_inc(nm.sq, 1)

        def add_square(v, nm, k, n):
            nm.wait(v, "sq", k + 1)
            if k == 0:
                nc.vector.tensor_copy(sqsum[:, 0:n], sq[:, 0, 0:n]).then_inc(nm.add, 1)
            else:
                nm.wait(v, "add", k)
                nc.vector.tensor_tensor(sqsum[:, 0:n], sqsum[:, 0:n], sq[:, k % 2, 0:n], ALU.add).then_inc(nm.add, 1)

        def sum_features(pe, nm, n, bank, added=KT):
            nm.wait(pe, "add", added)
            mm = nc.tensor.matmul(ps[:, bank, 0:min(n, S)], ones[:], sqsum[:, 0:min(n, S)], start=True, stop=True)
            if n > S:
                mm = nc.tensor.matmul(ps[:, bank + 1, 0:n - S], ones[:], sqsum[:, S:n], start=True, stop=True)
            mm.then_inc(nm.mm, 1)

        def make_rstd(act, nm, n, bank):
            nm.wait(act, "mm", 1)
            src = ps[:, bank:bank + 2].rearrange("p b c -> p (b c)")[:, 0:n]
            nc.scalar.activation(rstd[:, 0:n], src, ACT.Ln, bias=eps_t[:], scale=1.0 / D).then_inc(nm.ln, 1)
            nm.wait(act, "ln", 1)
            nc.scalar.activation(rstd[:, 0:n], rstd[:, 0:n], ACT.Exp, scale=-0.5).then_inc(nm.r, 1)

        none = dict(src=0, t=0, hi=0, lo=0)
        nm1 = Norm(src=0)
        nm2a = Norm(**none, sq=0, add=10)
        nm2b = Norm()
        nm3a = Norm(**none)
        nm3b = Norm()
        nm4 = Norm(src=0)
        nm5 = Norm(src=0, hi=0, lo=0)
        cvec = sem("cvec")
        res_free = sem("res_free")
        f_hi = sem("f_hi")
        f_lo = sem("f_lo")
        th_a = sem("th_a")
        gel = sem("gel")
        gel_t = sem("gel_t")
        pr_mm = sem("pr_mm")
        pr_ev = sem("pr_ev")
        up_free = sem("up_free")
        up_v = sem("up_v")
        f_zero = sem("f_zero")
        up_t = sem("up_t")
        up_y = sem("up_y")
        up_hi = sem("up_hi")
        wo_free = [sem(f"wo_free{i}") for i in range(3)]
        wo_f = [sem(f"wo_f{i}") for i in range(3)]
        ml_relu = sem("ml_relu")
        ml_sq = sem("ml_sq")
        ml_hi = sem("ml_hi")
        ml_lo = sem("ml_lo")
        ml_f = sem("ml_f")
        mod_in = [sem(f"mod_in{i}") for i in range(MRAW)]
        mod_mm = sem("mod_mm")
        mod_ev = sem("mod_ev")
        ha = {n: sem("ha_" + n) for n in
              ["q", "k", "v", "g", "gt", "rope", "ro", "vt", "ve", "s", "m", "e", "a", "t", "te", "pv", "sq", "st",
               "ln", "r", "o", "hi", "lo", "w", "c", "on"]}


        def wait_head(eng, name, head, per, k):
            i, c = head
            if i is not None:
                eng.wait_ge(ha[name], i * (2 * per) + (c * per + k))
            elif c * per + k > 0:
                eng.wait_ge(ha[name], c * per + k)

        def all_heads(eng, turn):
            turn((None, 0), True)
            with eng.Fori(0, 3) as i:
                turn((i, 1), True)
                turn((i, 2), True)
            turn((None, 7), False)

        hb = {n: sem("hb_" + n) for n in ["ev", "rope", "free", "gt", "vt", "ve"]}

        class Attn:
            def __init__(self, name, steps, slots, width, sbuf, ptbuf, sbn, finish):
                self.steps, self.slots, self.width, self.sb, self.pt, self.sbn, self.finish = \
                    steps, slots, width, sbuf, ptbuf, sbn, finish
                self.s, self.m, self.e, self.p, self.t, self.te, self.o, self.oh, self.ol, self.k = \
                    [sem(f"{name}_{n}") for n in ("s", "m", "e", "p", "t", "te", "o", "oh", "ol", "k")]
                self.blk = [sum(len(x["blocks"]) for x in steps[:n]) for n in range(len(steps) + 1)]
                self.grp = [sum(x["last"] for x in steps[:n]) for n in range(len(steps) + 1)]

            def sbank(self, m):
                if self.slots == 4:
                    return ps[:, m % 4]
                return pair(m % 2)

        def attn_scores(pe, A, n):
            st = A.steps[n]
            for r in range(REP):
                m = n * REP + r
                if m >= A.slots:
                    pe.wait_ge(A.m, m - A.slots + 1)
                for c, (o, rhs) in enumerate(st["k"]):
                    mm = nc.tensor.matmul(A.sbank(m)[:, o:o + rhs.shape[-1]], st["q"](r), rhs,
                                          start=st["kstart"][c], stop=True, skip_group_check=True)
                mm.then_inc(A.s, 1)

        def attn_out(pe, A, n):
            st = A.steps[n]
            pe.wait_ge(A.p, n + 1)
            nb = len(st["blocks"])
            g = A.grp[n]
            ob = ps[0:HD, 6 + g % 2]

            def turn(b):
                x = A.blk[n] + b
                if x >= 2:
                    pe.wait_ge(A.te, x - 1)
                o, w = st["blocks"][b]
                for r in range(REP):
                    mm = nc.tensor.transpose(ps[0:w, 4 + x % 2, r * P:(r + 1) * P],
                                             A.sb[n % A.sbn][:, r, o:o + w], ident[:])
                mm.then_inc(A.t, 1)

            def weigh(b):
                x = A.blk[n] + b
                pe.wait_ge(A.te, x + 1)
                o, w = st["blocks"][b]
                if b == 0 and st["first"] and g >= 2:
                    pe.wait_ge(A.ol, g - 1)
                mm = nc.tensor.matmul(ob, st["v"][b], A.pt[0:w, x % 4], start=(st["first"] and b == 0),
                                      stop=(st["last"] and b == nb - 1))
                if st["last"] and b == nb - 1:
                    mm.then_inc(A.o, 1)
                else:
                    mm.then_inc(A.k, 1)
            for b in range(nb):
                turn(b)
                if b:
                    weigh(b - 1)
            weigh(nb - 1)

        def attn_pe(pe, A):
            attn_scores(pe, A, 0)
            attn_scores(pe, A, 1)
            for n in range(len(A.steps)):
                if n + 2 < len(A.steps):
                    attn_scores(pe, A, n + 2)
                attn_out(pe, A, n)

        def attn_act(act, A):
            def turned(n):
                st = A.steps[n]
                for b, (o, w) in enumerate(st["blocks"]):
                    x = A.blk[n] + b
                    act.wait_ge(A.t, x + 1)
                    if x >= 4:
                        need = x - 3
                        gd = sum(1 for s in range(len(A.steps)) if A.steps[s]["last"] and A.blk[s + 1] <= need)
                        if gd:
                            act.wait_ge(A.o, gd)
                        if need - gd:
                            act.wait_ge(A.k, need - gd)
                    nc.scalar.activation(A.pt[0:w, x % 4], ps[0:w, 4 + x % 2], ACT.Copy).then_inc(A.te, 1)

            def finished(n):
                if A.steps[n]["last"]:
                    A.finish["act"](act, A, n, A.grp[n])

            for n, st in enumerate(A.steps):
                for r in range(REP):
                    m = n * REP + r
                    act.wait_ge(A.m, m + 1)
                    if st["sink"] is not None or st["clamp"]:
                        act.wait_ge(A.m, (n + 1) * REP)
                        act.wait_ge(mfix[A], fixn(A, n) + 1)
                    buf = A.sb[n % A.sbn][:, r, 0:st["keys"]]
                    c = (n % 2) * REP + r
                    nc.scalar.activation(buf, buf, ACT.Exp, bias=negm[:, c:c + 1], scale=-1.0,
                                         accum_out=sums[:, c:c + 1]).then_inc(A.e, 1)
                if st["sink"] is not None:
                    c = (n % 2) * REP
                    nc.scalar.activation(esk[:, c:c + REP], esk[:, c:c + REP], ACT.Exp).then_inc(A.e, 1)
                else:
                    act.wait_ge(A.e, 5 * n + 4)
                    nc.scalar.activation(spare, eps_t[:], ACT.Copy).then_inc(A.e, 1)
                if n:
                    turned(n - 1)
                if n >= 2:
                    finished(n - 2)
            turned(len(A.steps) - 1)
            finished(len(A.steps) - 2)
            finished(len(A.steps) - 1)

        mfix = {}

        def fixn(A, n):
            return sum(1 for s in A.steps[:n] if s["sink"] is not None or s["clamp"])

        def attn_dve(v, A):
            def finished(n):
                if A.steps[n]["last"]:
                    A.finish["dve"](v, A, n, A.grp[n])

            def minima(n):
                st = A.steps[n]
                c = (n % 2) * REP
                if n >= A.sbn:
                    v.wait_ge(A.t, A.blk[n - A.sbn + 1])
                for r in range(REP):
                    m = n * REP + r
                    v.wait_ge(A.s, m + 1)
                    nc.vector.tensor_tensor_reduce(
                        out=A.sb[n % A.sbn][:, r, 0:st["keys"]], in0=A.sbank(m)[:, st["off"]:st["off"] + st["keys"]],
                        in1=st["bias"](r), scale=1.0, scalar=3e38, op0=ALU.add, op1=ALU.min,
                        accum_out=negm[:, c + r:c + r + 1]).then_inc(A.m, 1)
                nm_ = negm[:, c:c + REP]
                if st["clamp"]:
                    v.wait_ge(A.m, (n + 1) * REP)
                    nc.vector.tensor_scalar(nm_, nm_, BIG / 10, None, ALU.min).then_inc(mfix[A], 1)
                if st["sink"] is not None:
                    v.wait_ge(A.m, (n + 1) * REP)
                    k = st["sink"]
                    done(nc.vector.tensor_tensor(nm_, nm_, nsinks[:, k:k + REP], ALU.min))
                    settle(v)
                    nc.vector.tensor_tensor(esk[:, c:c + REP], sinks[:, k:k + REP], nm_, ALU.add).then_inc(mfix[A], 1)

            minima(0)
            for n, st in enumerate(A.steps):
                c = (n % 2) * REP
                if n + 1 < len(A.steps):
                    minima(n + 1)
                if n >= 2:
                    finished(n - 2)
                v.wait_ge(A.e, 5 * (n + 1))
                su = sums[:, c:c + REP]
                if st["sink"] is not None:
                    done(nc.vector.tensor_tensor(rs[:, c:c + REP], su, esk[:, c:c + REP], ALU.add))
                else:
                    done(nc.vector.tensor_scalar(rs[:, c:c + REP], su, 1e-30, None, ALU.max))
                settle(v)
                done(nc.vector.reciprocal(wgt[:, c:c + REP], rs[:, c:c + REP]))
                if st["gate"] is not None:
                    settle(v)
                    done(nc.vector.tensor_tensor(wgt[:, c:c + REP], wgt[:, c:c + REP], st["gate"], ALU.mult))
                settle(v)
                for r in range(REP):
                    buf = A.sb[n % A.sbn][:, r, 0:st["keys"]]
                    ins = nc.vector.tensor_scalar(buf, buf, wgt[:, c + r:c + r + 1], None, ALU.mult)
                ins.then_inc(A.p, 1)
            finished(len(A.steps) - 2)
            finished(len(A.steps) - 1)

        def o_view(x):
            return x.rearrange("p (r q) -> p r q", r=REP)

        def fin1_act(act, A, n, g):
            act.wait_ge(A.o, g + 1)
            h, l = A.steps[n]["dst"]
            nc.scalar.activation(h, o_view(ps[0:HD, 6 + g % 2]), ACT.Copy).then_inc(A.oh, 1)

        def fin1_dve(v, A, n, g):
            h, l = A.steps[n]["dst"]
            v.wait_ge(A.oh, g + 1)
            nc.vector.tensor_tensor(l, o_view(ps[0:HD, 6 + g % 2]), h.bitcast(F32), ALU.subtract).then_inc(A.ol, 1)

        def fin2_act(act, A, n, g):
            act.wait_ge(A.oh, g + 1)
            h, l, gg, tmp = A.steps[n]["dst"]
            nc.scalar.activation(h, tmp, ACT.Copy).then_inc(A.k2, 1)

        def fin2_dve(v, A, n, g):
            h, l, gg, tmp = A.steps[n]["dst"]
            v.wait_ge(A.o, g + 1)
            if g:
                v.wait_ge(A.k2, g)
                v.wait_ge(A.ol, g)
            nc.vector.scalar_tensor_tensor(out=tmp, in0=o_view(ps[0:HD, 6 + g % 2]), scalar=0.5, in1=gg,
                                           op0=ALU.mult, op1=ALU.mult).then_inc(A.oh, 1)
            v.wait_ge(A.k2, g + 1)
            nc.vector.tensor_tensor(l, tmp, h.bitcast(F32), ALU.subtract).then_inc(A.ol, 1)

        def steps1():
            out = []
            for g in range(2):
                gs = slice(g * HD, (g + 1) * HD)
                for i in range(QT):
                    qs = slice(i * P, (i + 1) * P)
                    n = (i + 1) * P
                    dst = (o1h[gs, 0:REP, qs], o1l[gs, 0:REP, qs])
                    gcol = lambda b, g=g, i=i: gate[:, i, g * 12 + b:g * 12 + b + 12:3]
                    q = lambda r, gs=gs, qs=qs: q_n[gs, r, qs]
                    for kind in (0, 1):
                        out.append(dict(q=q, k=[(0, k_all[gs, kind, 0:n])], kstart=[True], off=0, keys=n,
                                        bias=lambda r, g=g, n=n: strip_n[:, g * REP + r, S - n:S],
                                        blocks=[(j * P, P) for j in range(i + 1)],
                                        v=[v_all[:, kind, j, gs] for j in range(i + 1)],
                                        first=(kind == 0), last=False, dst=dst, gate=gcol(1 + kind), sink=None,
                                        clamp=False))
                    out.append(dict(q=q, k=[(0, kcmp[gs, 0:NCMP + 1])], kstart=[True], off=0, keys=NCMP,
                                    bias=lambda r, i=i: cmask[:, i, :], blocks=[(0, NCMP)],
                                    v=[vcmp[0:NCMP, g, :]], first=False, last=True, dst=dst, gate=gcol(0), sink=None,
                                    clamp=True))
            for g in range(2):
                gs = slice(g * HD, (g + 1) * HD)
                for i in range(QT):
                    qs = slice(i * P, (i + 1) * P)
                    lo = max(i - 1, 0)
                    n = (i + 1 - lo) * P
                    out.append(dict(q=lambda r, gs=gs, qs=qs: q_s[gs, r, qs],
                                    k=[(0, k_all[gs, 2, lo * P:lo * P + n])], kstart=[True], off=0, keys=n,
                                    bias=lambda r, g=g, n=n: strip_s[:, g * REP + r, 256 - n:256],
                                    blocks=[(j * P, P) for j in range(n // P)],
                                    v=[v_all[:, 2, lo + j, gs] for j in range(n // P)],
                                    first=True, last=True, dst=(o1h[gs, REP:8, qs], o1l[gs, REP:8, qs]), gate=None,
                                    sink=g * REP, clamp=False))
            return out

        def steps2():
            out = []
            for kh in range(4):
                pb = (kh % 2) * HD
                gs = slice(pb, pb + HD)
                kt = kh // 2
                for i in range(QT):
                    qs = slice(i * P, (i + 1) * P)
                    lo, hi = max(i - 1, 0), min(i + 2, QT)
                    n = (hi - lo) * P
                    mask = bm0[:, 0:C + n] if i == 0 else bm1[:, 0:C + n]
                    ts = slice(kt * REP, (kt + 1) * REP)
                    out.append(dict(q=lambda r, gs=gs, qs=qs, kt=kt: b_q[gs, kt * REP + r, qs],
                                    k=[(C, b_k[gs, kt, S:SC]), (S, b_k[gs, kt, lo * P:hi * P])], kstart=[True, True],
                                    off=C, keys=C + n, bias=lambda r, mask=mask: mask,
                                    blocks=[(j * P, P) for j in range(2 + hi - lo)],
                                    v=[b_v[:, QT + j, kh * HD:(kh + 1) * HD] for j in range(2)]
                                    + [b_v[:, j, kh * HD:(kh + 1) * HD] for j in range(lo, hi)],
                                    first=True, last=True,
                                    dst=(x1h[gs, ts, qs], x1l[gs, ts, qs], b_g[gs, ts, qs], o_view(ot[gs, :])),
                                    gate=None, sink=8 + kh * REP, clamp=False))
            return out

        A1 = Attn("at1", steps1(), 4, 512, sb1, pt1, 3, dict(act=fin1_act, dve=fin1_dve))
        A2 = Attn("at2", steps2(), 2, 1024, b_sb, b_pt, 3, dict(act=fin2_act, dve=fin2_dve))
        A2.k2 = sem("at2_hi")
        mfix[A1] = sem("at1_fix")
        mfix[A2] = sem("at2_fix")

        @block.sync
        def _(sp):
            for dst, name in ((ident[:], "ident"), (gains, "gains"), (bmod, "bmod"), (cin, "cin"), (lamv[0:HD], "lamv"),
                              (subg, "subg"), (w2[:], "w2"), (pos[:], "pos"), (onehot[:], "onehot"),
                              (blhs[0:BUCKETS], "rel_bias"), (blhs[BUCKETS:34], "selrows"), (cmask[:], "cmask")):
                sp.dma_start(dst, t[name]).then_inc(const_in, 16)
            sp.dma_start(sinks, bass.AP(t["sinks"].tensor, 0, [[0, P], [1, 24]])).then_inc(const_in, 16)
            sp.dma_start(xin[:], t["xT"]).then_inc(x_in, 16)
            for u in range(RAW):
                load_unit(sp, u, t["w_att"][u])
            sp.wait_ge(brow_ok, 2)
            sp.dma_start(dbias, brow[:].unsqueeze(1).to_broadcast([16, P, TBL])).then_inc(dbias_in, 16)
            sp.wait_ge(dbias_in, 16)
            sp.dma_start(strip_n[:], bass.AP(dbias.tensor, 127, [[TBL - 1, P], [P * TBL, 8], [1, 512]])).then_inc(strips_in, 16)
            sp.dma_start(strip_s[:], bass.AP(dbias.tensor, 8 * P * TBL + 383, [[TBL - 1, P], [P * TBL, 8], [1, 256]])).then_inc(strips_in, 16)
            for u in range(RAW, N_ATT):
                load_unit(sp, u, t["w_att"][u])
            with sp.Fori(0, 2) as i:
                for j in range(12):
                    load_unit(sp, U_UP + j, t["w_up"][bass.ds(i * 12 + j, 1)].rearrange("o p k m -> p (o k) m"), i, 12)
            begin_after(sp, "nsa")
            sp.dma_start(hc[:, :, 0:S], t["xT"]).then_inc(x_in, 16)
            sp.dma_start(hc[:, :, S:SC], t["ctxT"]).then_inc(ctx_in, 16)
            with sp.Fori(0, 2) as i:
                for j in range(4):
                    load_unit(sp, U_OUT + j, t["w_out"][bass.ds(i * 4 + j, 1)].rearrange("o p k m -> p (o k) m"), i, 4)
            with sp.Fori(0, 4) as i:
                for j in range(16):
                    load_unit(sp, U_MLP + j, t["w_mlp"][bass.ds(i * 16 + j, 1)].rearrange("o p k m -> p (o k) m"), i, 16)
            with sp.Fori(0, 8) as i:
                for j in range(4):
                    load_unit(sp, U_A + j, t["w_a"][bass.ds(i * 4 + j, 1)].rearrange("o p k m -> p (o k) m"), i, 4)
            with sp.Fori(0, 2) as i:
                for j in range(4):
                    load_unit(sp, U_AO + j, t["w_ao"][bass.ds(i * 4 + j, 1)].rearrange("o p k m -> p (o k) m"), i, 4)
            with sp.Fori(0, 5) as i:
                for j in range(4):
                    load_unit(sp, U_B + j, t["w_b"][bass.ds(i * 4 + j, 1)].rearrange("o p k m -> p (o k) m"), i, 4)
            with sp.Fori(0, 2) as i:
                for j in range(4):
                    load_unit(sp, U_BO + j, t["w_bo"][bass.ds(i * 4 + j, 1)].rearrange("o p k m -> p (o k) m"), i, 4)
            for k in range(KT):
                nm5.wait(sp, "t", k + 1)
                sp.dma_start(out[:, k], xo[:, k]).then_inc(out_done, 16)
            sp.wait_ge(out_done, 16 * KT)

        @block.gpsimd
        def _(g):
            def low(u, i=None):
                g.wait_ge(w_hi, u + 1 if i is None else i * 4 + (u + 1))
                nc.gpsimd.tensor_tensor(w_l[:, u % SPL], raw[:, u % RAW], w_h[:, u % SPL].bitcast(F32),
                                        ALU.subtract).then_inc(w_lo, 1)
            head = U_END % 4
            for u in range(head):
                low(u)
            with g.Fori(0, (U_END - head) // 4) as i:
                for j in range(4):
                    low(head + j, i)

        CONSTS = 16 * 13

        @block.tensor
        def _(pe):
            pe.wait_ge(const_in, CONSTS)
            pe.wait_ge(boot, 1)
            nc.tensor.matmul(ps[0:16, 6, :], blhs[:], onehot[:, 0:512], start=True, stop=True)
            nc.tensor.matmul(ps[0:16, 7, 0:128], blhs[:], onehot[:, 512:640], start=True, stop=True)
            pe.wait_ge(boot, 3)
            nc.tensor.matmul(ps[:, 5, 0:2], ones[0:HD, :], lamp[0:HD, :], start=True, stop=True).then_inc(cvec, 1)
            sum_features(pe, nm1, S, 4)
            plain = [(lambda k: x1h[:, k, :], lambda k: x1l[:, k, :])]
            r = 0
            for u in range(N_ATT):
                cmp_u = 2 <= u < 10
                first = not (cmp_u and u % 2 == 1)
                if u == 0:
                    pass
                split_ready(pe, u)
                if first and r >= 2:
                    pe.wait_ge(res_free, r - 1)
                if not cmp_u:
                    if u == 0:
                        for k in range(KT):
                            nm1.wait(pe, "lo", k + 1)
                            mm = products(u, [(ps[:, 0], lambda k: x1h[:, k, :], lambda k: x1l[:, k, :])], k, k + 1,
                                          first=(k == 0), last=(k == KT - 1))
                    else:
                        mm = products(u, [(ps[:, r % 2], lambda k: x1h[:, k, :], lambda k: x1l[:, k, :])])
                    r += 1
                else:
                    kv = (u - 2) // 4
                    kk = u % 2
                    pe.wait_ge(f_lo, kv + 1)

                    def fr(f, kv=kv, kk=kk):
                        return lambda k: bass.AP(f, kv * FW + kk * 8 + k, [[2 * FW, P], [256, 3], [8, 32]])
                    mm = products(u, [(ps[:, r % 2, 0:96], fr(fh), fr(fl))], first=(kk == 0), last=(kk == 1))
                    if kk == 1:
                        r += 1
                mm.then_inc(unit, 1)
            pe.wait_ge(gel, 1)
            glv = gl3[:, :, :].rearrange("p c (g n) -> p c g n", g=2)
            for g in range(2):
                for mt in range(2):
                    nc.tensor.matmul(ps[g * HD:(g + 1) * HD, 2, 0:NCMP], w2[:, 0, mt, :], glv[:, mt, g, :],
                                     start=(mt == 0), stop=(mt == 1))
            for g in range(2):
                for mt in range(2):
                    mm = nc.tensor.matmul(ps[0:NCMP, 3, g * HD:(g + 1) * HD], glv[:, 2 + mt, g, :], w2[:, 1, mt, :],
                                          start=(mt == 0), stop=(mt == 1))
            mm.then_inc(pr_mm, 1)
            pe.wait_ge(res_free, 21)
            for n in range(4):
                for tt in range(QT):
                    mm = nc.tensor.transpose(ps[:, 4 + n, tt * P:(tt + 1) * P], vT[:, n, tt * P:(tt + 1) * P], ident[:])
                mm.then_inc(pr_mm, 1)
            end_phase(pe, "prep")
            begin_after(pe, "prep")
            attn_pe(pe, A1)
            end_phase(pe, "nsa")
            begin_after(pe, "nsa")
            with pe.Fori(0, 2) as i:
                for m in range(4):
                    b = m % 2
                    pe.wait_ge(up_free, i * 4 + (m + 1))
                    for j, bank in ((0, b), (1, 2 + b)):
                        u = U_UP + m * 3 + j
                        split_ready(pe, u, i, 12)
                        products(u, [(ps[:, bank], lambda k: x1h[:, k, :], lambda k: x1l[:, k, :])]).then_inc(unit, 1)
                    u = U_UP + m * 3 + 2
                    split_ready(pe, u, i, 12)
                    products(u, [(ps[:, 4 + b], lambda k: o1h[:, k, :], lambda k: o1l[:, k, :])], 0, 4)
                    products(u, [(ps[:, 6 + b], lambda k: o1h[:, k, :], lambda k: o1l[:, k, :])], 4, 8).then_inc(unit, 1)
            end_phase(pe, "up")
            begin_after(pe, "up")

            def out_products(n, u0, yh, yl, wide):
                with pe.Fori(0, 2) as i:
                    for j in range(4):
                        split_ready(pe, u0 + j, i, 4)
                        pe.wait_ge(wo_free[n], i * 4 + (j + 1))
                        if wide:
                            parts = [(ps[:, 2 * (j % 2)], lambda k: yh[:, k, 0:S], lambda k: yl[:, k, 0:S]),
                                     (ps[:, 2 * (j % 2) + 1, 0:C], lambda k: yh[:, k, S:SC], lambda k: yl[:, k, S:SC])]
                        else:
                            parts = [(ps[:, j % 2], lambda k: yh[:, k, :], lambda k: yl[:, k, :])]
                        if n == 1 and j == 0:
                            for k in range(KT):
                                pe.wait_ge(ha["lo"], k + 1)
                                mm = products(u0, parts, k, k + 1, first=(k == 0), last=(k == KT - 1))
                            mm.then_inc(unit, 1)
                        else:
                            products(u0 + j, parts).then_inc(unit, 1)
            out_products(0, U_OUT, y1h, y1l, False)
            sum_features(pe, nm2a, S, 4, KT + 2)
            end_phase(pe, "wout")
            begin_after(pe, "wout")
            sum_features(pe, nm2b, S, 6)
            end_phase(pe, "norm2")
            begin_after(pe, "norm2")
            with pe.Fori(0, 4) as i:
                pe.wait_ge(mod_ev, i + 1)
                for j in range(16):
                    u = U_MLP + j
                    split_ready(pe, u, i, 16)
                    pe.wait_ge(ml_f, i * 16 + (j + 1))
                    if j < 8:
                        mm = products(u, [(ps[:, j % 2], lambda k: x1h[:, k, :], lambda k: x1l[:, k, :])])
                    else:
                        if j == 8:
                            pe.wait_ge(ml_lo, i * 8 + 7)
                            products(u, [(ps[:, j % 2], lambda k: m_h[:, k, :], lambda k: m_l[:, k, :])], 0, 7, last=False)
                            pe.wait_ge(ml_lo, i * 8 + 8)
                            mm = products(u, [(ps[:, j % 2], lambda k: m_h[:, k, :], lambda k: m_l[:, k, :])], 7, 8, first=False)
                        else:
                            mm = products(u, [(ps[:, j % 2], lambda k: m_h[:, k, :], lambda k: m_l[:, k, :])])
                    mm.then_inc(unit, 1)
                    if j % 4 != 3:
                        c = j // 4 * 3 + j % 4
                        pe.wait_ge(mod_in[c % MRAW], i * (16 * 12 // MRAW) + 16 * (c // MRAW + 1))
                        for k in range(KT):
                            mm = nc.tensor.matmul(ps[:, 7, 2 * c:2 * c + 2], mraw[:, c % MRAW, k], cs[:, 2 * k:2 * k + 2],
                                                  start=(k == 0), stop=(k == KT - 1))
                        mm.then_inc(mod_mm, 1)
            sum_features(pe, nm3a, S, 4)
            end_phase(pe, "mlp")
            begin_after(pe, "mlp")
            sum_features(pe, nm3b, SC, 6)
            end_phase(pe, "norm3")
            begin_after(pe, "norm3")
            def project(head, pos, n):
                i, c = head
                for x in range(pos, pos + n):
                    j, k = divmod(x, KT)
                    u = U_A + 4 * c + j
                    if k == 0:
                        split_ready(pe, u, i, 8)
                        wait_head(pe, "gqkv"[j], head, 1, 1 if j else 0)
                    mm = products(u, [(ps[:, 0], lambda k: x2h[:, k, 0:S], lambda k: x2l[:, k, 0:S]),
                                      (ps[:, 1, 0:C], lambda k: x2h[:, k, S:SC], lambda k: x2l[:, k, S:SC])],
                                  k, k + 1, first=(k == 0), last=(k == KT - 1))
                    if k == KT - 1:
                        mm.then_inc(unit, 1)

            def attend(head, more):
                i, c = head
                pos = [0]
                aq, ak = a_q[c % 2], a_k[c % 2]

                def dense(n):
                    if more:
                        project((i, c + 1), pos[0], n)
                        pos[0] += n

                def score(qt, m):
                    wait_head(pe, "m", head, 12, 2 * qt + m)
                    ms = slice(m * HD, (m + 1) * HD)
                    q = aq[ms, qt * P:(qt + 1) * P]
                    if qt < QT:
                        nc.tensor.matmul(ps[:, 2], q, ak[ms, 0:S], start=True, stop=True)
                        mm = nc.tensor.matmul(ps[:, 3, 0:C], q, ak[ms, S:SC], start=True, stop=True)
                    else:
                        mm = nc.tensor.matmul(ps[:, 2, 0:C], q, ak[ms, S:SC], start=True, stop=True)
                    mm.then_inc(ha["s"], 1)

                def turns(qt):
                    wait_head(pe, "a", head, 6, qt + 1)
                    if qt == 0:
                        wait_head(pe, "ve", head, 1, 1)
                    else:
                        wait_head(pe, "te", head, 6, qt)
                    for b in range(6 if qt < QT else 2):
                        mm = nc.tensor.transpose(ps[:, 4 + b // 4, (b % 4) * P:(b % 4 + 1) * P],
                                                 a_p[qt % 3][0][:, b * P:(b + 1) * P], ident[:])
                    mm.then_inc(ha["t"], 1)

                wait_head(pe, "ro", head, 2, 2)
                score(0, 0)
                dense(2)
                score(0, 1)
                dense(2)
                wait_head(pe, "v", head, 1, 1)
                wait_head(pe, "ln", head, 1, 0)
                for b in range(6):
                    mm = nc.tensor.transpose(ps[:, 4 + b // 4, (b % 4) * P:(b % 4 + 1) * P], a_vT[:, b * P:(b + 1) * P], ident[:])
                mm.then_inc(ha["vt"], 1)
                score(1, 0)
                dense(2)
                score(1, 1)
                dense(2)
                for qt, (n0, n1, n2) in enumerate(((1, 1, 1), (1, 1, 2), (1, 0, 2), (1, 1, 1))):
                    score(qt + 2, 0)
                    dense(n0)
                    score(qt + 2, 1)
                    dense(n1)
                    turns(qt)
                    dense(n2)
                turns(4)
                dense(1)
                wait_head(pe, "on", head, 1, 0)
                wait_head(pe, "te", head, 6, 4)
                for b in range(6):
                    mm = nc.tensor.matmul(ps[:, 6], a_v[:, b, :], a_pt[:, b, :], start=(b == 0), stop=(b == 5))
                dense(2)
                turns(5)
                dense(2)
                wait_head(pe, "te", head, 6, 6)
                for b in range(2):
                    mm = nc.tensor.matmul(ps[:, 7, 0:C], a_v[:, 4 + b, :], a_pt2[:, b, :], start=(b == 0), stop=(b == 1))
                mm.then_inc(ha["pv"], 1)
                dense(6)
                wait_head(pe, "sq", head, 1, 1)
                nc.tensor.matmul(ps[:, 4], ones[:], a_sq[:, 0:S], start=True, stop=True)
                nc.tensor.matmul(ps[:, 5, 0:C], ones[:], a_sq[:, S:SC], start=True, stop=True).then_inc(ha["st"], 1)

            project((None, 0), 0, 4 * KT)
            all_heads(pe, attend)
            end_phase(pe, "heads")
            begin_after(pe, "heads")
            out_products(1, U_AO, x2h, x2l, True)
            end_phase(pe, "ao")
            begin_after(pe, "ao")
            sum_features(pe, nm4, SC, 6)
            end_phase(pe, "norm4")
            begin_after(pe, "norm4")
            for u in range(N_B):
                split_ready(pe, U_B + u)
                if u >= 2:
                    pe.wait_ge(hb["free"], u - 1)
                parts = [(ps[:, 2 * (u % 2)], lambda k: x2h[:, k, 0:S], lambda k: x2l[:, k, 0:S])]
                if 8 <= u < 12:
                    parts.append((ps[:, 2 * (u % 2) + 1, 0:C], lambda k: x2h[:, k, S:SC], lambda k: x2l[:, k, S:SC]))
                products(U_B + u, parts).then_inc(unit, 1)
                if u == 13:
                    for n in range(2):
                        if n:
                            pe.wait_ge(hb["ve"], 1)
                        for b in range(6):
                            mm = nc.tensor.transpose(ps[:, 4 + b // 4, (b % 4) * P:(b % 4 + 1) * P],
                                                     b_vT[:, n, b * P:(b + 1) * P], ident[:])
                        mm.then_inc(hb["vt"], 1)
            end_phase(pe, "bqkv")
            begin_after(pe, "bqkv")
            attn_pe(pe, A2)
            end_phase(pe, "battn")
            begin_after(pe, "battn")
            out_products(2, U_BO, x1h, x1l, False)
            sum_features(pe, nm5, S, 4)

        @block.scalar
        def _(act):
            act.wait_ge(const_in, CONSTS)
            act.wait_ge(boot, 1)
            nc.scalar.activation(ct, cin, ACT.Tanh, scale=0.5).then_inc(cvec, 1)
            act.wait_ge(x_in, 16)
            for k in range(KT):
                square_tile(act, nm1, k, xin[:, k, :], S)
            act.wait_ge(boot, 4)
            nc.scalar.activation(lame, lame, ACT.Exp).then_inc(cvec, 1)
            split_high(act, 0)
            make_rstd(act, nm1, S, 4)
            for k in range(KT):
                nm1.wait(act, "t", k + 1)
                nc.scalar.activation(x1h[:, k, :], xn[:, k % 2, 0:S], ACT.Copy).then_inc(nm1.hi, 1)
            r = 0
            for u in range(N_ATT):
                split_high(act, u + 1)
                if u in (0, 1):
                    unit_done(act, u)
                    if u == 0:
                        nm1.wait(act, "lo", KT)
                    for g in range(2):
                        for op in range(2):
                            src = ps[g * HD:(g + 1) * HD, u % 2].rearrange("p (t o) -> p t o", o=2)[:, :, op]
                            ins = nc.scalar.activation(fh[op * HD:(op + 1) * HD, u, g * 256:(g + 1) * 256], src, ACT.Copy)
                            ins.then_inc(f_hi, 1)
                    nc.scalar.activation(fh[:, u, 512:520 + 0], pos[:, u, 0:8], ACT.Copy).then_inc(f_hi, 1)
                    nc.scalar.activation(fh[:, u, 520:528], pos[:, u, 8:16], ACT.Copy).then_inc(f_hi, 1)
                if u == 10:
                    act.wait_ge(gel_t, 1)
                    nc.scalar.activation(gl2[:], gl1[:], ACT.Tanh, scale=GELU_C).then_inc(th_a, 1)
                if u == 18:
                    unit_done(act, u)
                    nc.scalar.activation(vT[:, 3, :], ps[:, 0], ACT.Tanh, scale=0.5).then_inc(th_a, 1)
            end_phase(act, "prep")
            begin_after(act, "prep")
            act.wait_ge(strips_in, 32)
            attn_act(act, A1)
            end_phase(act, "nsa")
            begin_after(act, "nsa")
            with act.Fori(0, 2) as i:
                for m in range(4):
                    b = m % 2
                    for j in range(3):
                        split_high(act, U_UP + m * 3 + j + 1, i, 12)
                        if j < 2:
                            unit_done(act, U_UP + m * 3 + j, i, 12)
                            if j == 0:
                                act.wait_ge(up_free, i * 4 + (m + 1))
                            nc.scalar.activation(tg[:, b, j, :], ps[:, 2 * j + b], ACT.Tanh, scale=0.5).then_inc(up_t, 1)
                    act.wait_ge(up_y, i * 4 + (m + 1))
                    nc.scalar.activation(y1h[:, bass.ds(i * 4 + m, 1), :].rearrange("p a s -> p (a s)"), ty[:, b, :],
                                         ACT.Copy).then_inc(up_hi, 1)
            end_phase(act, "up")
            begin_after(act, "up")
            with act.Fori(0, 2) as i:
                for j in range(4):
                    split_high(act, U_OUT + j + 1, i, 4)
                    unit_done(act, U_OUT + j, i, 4)
                    nc.scalar.activation(f_t[:, bass.ds(i * 4 + j, 1), :].rearrange("p a s -> p (a s)"), ps[:, j % 2],
                                         ACT.Copy).then_inc(wo_f[0], 1)
                    nm2a.wait(act, "add", i * 4 + (j + 1))
                    nc.scalar.activation(sq[:, j % 2, 0:S], ps[:, j % 2], ACT.Square).then_inc(wo_free[0], 1)
            make_rstd(act, nm2a, S, 4)
            end_phase(act, "wout")
            begin_after(act, "wout")
            for c in range(MRAW - 1):
                act.dma_start(mraw[:, c], t["w_mod"][c]).then_inc(mod_in[c], 16)
            for k in range(KT):
                nm2b.wait(act, "src", k + 1)
                square_tile(act, nm2b, k, hc[:, k, 0:S], S)
            make_rstd(act, nm2b, S, 6)
            for k in range(KT):
                nm2b.wait(act, "t", k + 1)
                nc.scalar.activation(x1h[:, k, :], xn2[:, k % 2, 0:S], ACT.Copy).then_inc(nm2b.hi, 1)
            end_phase(act, "norm2")
            begin_after(act, "norm2")
            with act.Fori(0, 4) as i:
                for j in range(16):
                    split_high(act, U_MLP + j + 1, i, 16)
                    unit_done(act, U_MLP + j, i, 16)
                    if j < 8:
                        if j == 0:
                            pass
                        nc.scalar.activation(relu[:, j % 2, :], ps[:, j % 2], ACT.Relu).then_inc(ml_relu, 1)
                        act.wait_ge(ml_sq, i * 8 + (j + 1))
                        nc.scalar.activation(m_h[:, j, :], msq[:, j % 2, :], ACT.Copy).then_inc(ml_hi, 1)
                    if j % 4 != 3:
                        c = j // 4 * 3 + j % 4 + MRAW - 1
                        act.dma_start(mraw[:, c % MRAW], t["w_mod"][bass.ds(i * 12 + c, 1)].rearrange("o p k m -> p (o k) m")
                                      ).then_inc(mod_in[c % MRAW], 16)
            for c in range(MRAW - 1):
                act.wait_ge(mod_in[c], 16 * (N_MOD // MRAW + 1))
            for k in range(KT):
                square_tile(act, nm3a, k, f_t[:, k, :], S)
            make_rstd(act, nm3a, S, 4)
            end_phase(act, "mlp")
            begin_after(act, "mlp")
            for k in range(KT):
                nm3b.wait(act, "src", k + 1)
                square_tile(act, nm3b, k, hc[:, k, :], SC)
            make_rstd(act, nm3b, SC, 6)
            for k in range(KT):
                nm3b.wait(act, "t", k + 1)
                nc.scalar.activation(x2h[:, k, :], xn2[:, k % 2, :], ACT.Copy).then_inc(nm3b.hi, 1)
            end_phase(act, "norm3")
            begin_after(act, "norm3")
            act.dma_start(cos_t[:], t["cos"]).then_inc(tab_in, 16)
            act.dma_start(sin_t[:], t["sin"]).then_inc(tab_in, 16)
            def take(head, j, ahead):
                i, c = head
                unit_done(act, U_A + 4 * c + j, i, 8)
                src = pair(0)[:, 0:SC]
                if j == 0:
                    nc.scalar.activation(a_q[c % 2][:], src, ACT.Copy, scale=-0.125).then_inc(ha["q"], 1)
                elif j == 1:
                    nc.scalar.activation(a_k[c % 2][:], src, ACT.Copy).then_inc(ha["k"], 1)
                elif j == 2:
                    nc.scalar.activation(a_vT[:], src, ACT.Copy).then_inc(ha["v"], 1)
                else:
                    nc.scalar.activation(a_g[c % 2][:], src, ACT.Tanh, scale=0.5).then_inc(ha["gt"], 1)
                if ahead:
                    split_high(act, U_A + 4 * c + j + 2, i, 8)

            def attend(head, more):
                i, c = head

                def exps(qt, m):
                    n = SC if qt < QT else C
                    cc = 2 * (qt % 3) + m
                    wait_head(act, "m", head, 12, 2 * qt + m + 1)
                    buf = a_p[qt % 3][m][:, 0:n]
                    nc.scalar.activation(buf, buf, ACT.Exp, bias=negm[:, cc:cc + 1], scale=-1.0,
                                         accum_out=sums[:, cc:cc + 1]).then_inc(ha["e"], 1)

                def turned(qt):
                    wait_head(act, "t", head, 6, qt + 1)
                    if qt < QT:
                        nc.scalar.activation(a_pt[:, :, qt * P:(qt + 1) * P],
                                             pair(2)[:, 0:SC].rearrange("p (b q) -> p b q", b=6), ACT.Copy).then_inc(ha["te"], 1)
                    else:
                        nc.scalar.activation(a_pt2[:, :, (qt - QT) * P:(qt - QT + 1) * P],
                                             pair(2)[:, 0:C].rearrange("p (b q) -> p b q", b=2), ACT.Copy).then_inc(ha["te"], 1)
                exps(0, 0)
                exps(0, 1)
                wait_head(act, "vt", head, 1, 1)
                nc.scalar.activation(a_v[:].rearrange("p b e -> p (b e)"), pair(2)[:, 0:SC], ACT.Copy).then_inc(ha["ve"], 1)
                exps(1, 0)
                exps(1, 1)
                if more:
                    take((i, c + 1), 0, True)
                for qt in range(6):
                    if qt < 4:
                        exps(qt + 2, 0)
                        if qt == 2 and more:
                            take((i, c + 1), 1, True)
                        exps(qt + 2, 1)
                    if qt == 5 and more:
                        take((i, c + 1), 2, True)
                    turned(qt)
                wait_head(act, "pv", head, 1, 1)
                wait_head(act, "on", head, 1, 0)
                nc.scalar.activation(a_sq[:], pair(3)[:, 0:SC], ACT.Square).then_inc(ha["sq"], 1)
                if more:
                    take((i, c + 1), 3, True)
                wait_head(act, "st", head, 1, 1)
                nc.scalar.activation(rstd[:], pair(2)[:, 0:SC], ACT.Ln, bias=seps_t[:], scale=1.0 / P).then_inc(ha["ln"], 1)
                wait_head(act, "ln", head, 1, 1)
                nc.scalar.activation(rstd[:], rstd[:], ACT.Exp, scale=-0.5).then_inc(ha["r"], 1)

            split_high(act, U_A + 1)
            for j in range(4):
                take((None, 0), j, True)
            all_heads(act, attend)
            end_phase(act, "heads")
            begin_after(act, "heads")
            for k in range(KT):
                nc.scalar.activation(x2h[:, k, :], o2[:, k, :], ACT.Copy).then_inc(ha["hi"], 1)
            for j in range(1, N_OUT):
                split_high(act, U_AO + j + 1)
            end_phase(act, "ao")
            begin_after(act, "ao")
            for k in range(KT):
                square_tile(act, nm4, k, hc[:, k, :], SC)
            make_rstd(act, nm4, SC, 6)
            for k in range(KT):
                nm4.wait(act, "t", k + 1)
                nc.scalar.activation(x2h[:, k, :], xn2[:, k % 2, :],
                                     ACT.Copy).then_inc(nm4.hi, 1)
            end_phase(act, "norm4")
            begin_after(act, "norm4")
            act.dma_start(bm0[:], t["bm0"]).then_inc(tab_in, 16)
            act.dma_start(bm1[:], t["bm1"]).then_inc(tab_in, 16)
            for u in range(N_B):
                split_high(act, U_B + u + 1)
                unit_done(act, U_B + u)
                b = u % 2
                if u < 8:
                    nc.scalar.activation(b_q[:, u, :], ps[:, 2 * b], ACT.Copy, scale=-0.125).then_inc(hb["free"], 1)
                elif u < 10:
                    nc.scalar.activation(b_k[:, u - 8, :], pair(b)[:, 0:SC], ACT.Copy).then_inc(hb["free"], 1)
                elif u < 12:
                    nc.scalar.activation(b_vT[:, u - 10, :], pair(b)[:, 0:SC], ACT.Copy).then_inc(hb["free"], 1)
                else:
                    nc.scalar.activation(b_g[:, u - 12, :], ps[:, 2 * b], ACT.Tanh, scale=0.5).then_inc(hb["gt"], 1)
                    if u == 14:
                        pass
            end_phase(act, "bqkv")
            begin_after(act, "bqkv")
            attn_act(act, A2)
            end_phase(act, "battn")
            begin_after(act, "battn")
            for j in range(N_OUT):
                split_high(act, U_BO + j + 1)
            for k in range(KT):
                act.wait_ge(wo_free[2], 2 + k + 1)
                square_tile(act, nm5, k, hc[:, k, 0:S], S)
            make_rstd(act, nm5, S, 4)

        @block.vector
        def _(v):
            nc.vector.memset(ones[:], 1.0)
            nc.vector.memset(eps_t, EPS)
            nc.vector.memset(seps_t, SUB_EPS)
            nc.vector.memset(zero, 0.0)
            nc.vector.memset(fh[:].bitcast(F32), 0.0)
            nc.vector.memset(fl[:].bitcast(F32), 0.0)
            nc.vector.memset(kcmp[:], 0.0).then_inc(boot, 1)
            v.wait_ge(const_in, CONSTS)
            done(nc.vector.tensor_scalar(nsinks, sinks, -1.0, None, ALU.mult))
            done(nc.vector.tensor_scalar(subs, subg, 0.5 * (1.0 - LAM_INIT), None, ALU.mult))
            v.wait_ge(cvec, 1)
            lv = lamv[0:HD].rearrange("p (a b) -> p a b", b=2)
            nc.vector.tensor_tensor(lamp[0:HD], lv[:, :, 0], lv[:, :, 1], ALU.mult).then_inc(boot, 2)
            for k in range(KT):
                add_square(v, nm1, k, S)
            v.wait_ge(cvec, 2)
            done(nc.vector.scalar_tensor_tensor(out=cs, in0=ct, scalar=1.0, in1=cin, op0=ALU.add, op1=ALU.mult))
            settle(v)
            done(nc.vector.tensor_scalar(cs, cs, 0.5, None, ALU.mult))
            nc.vector.tensor_copy(brow[:, 0:512], ps[0:16, 6, :]).then_inc(brow_ok, 1)
            nc.vector.tensor_copy(brow[:, 512:640], ps[0:16, 7, 0:128]).then_inc(brow_ok, 1)
            nc.vector.tensor_copy(lame, ps[:, 5, 0:2]).then_inc(boot, 1)
            v.wait_ge(cvec, 3)
            done(nc.vector.tensor_scalar(lam, lame[:, 0:1], lame[:, 1:2], LAM_INIT, ALU.subtract, ALU.add))

            def normed(nm, k, src, gain, dst_t, lo_dst, hi_src, n, shift=None):
                if k >= 2:
                    nm.wait(v, "lo", k - 1)
                if shift is None:
                    nc.vector.scalar_tensor_tensor(out=dst_t(k), in0=src, scalar=gain, in1=rstd[:, 0:n],
                                                   op0=ALU.mult, op1=ALU.mult).then_inc(nm.t, 1)
                else:
                    for a, b, gn, sh in shift:
                        done(nc.vector.scalar_tensor_tensor(out=dst_t(k)[:, a:b], in0=src[:, a:b], scalar=gn,
                                                            in1=rstd[:, a:b], op0=ALU.mult, op1=ALU.mult))
                    settle(v)
                    for x, (a, b, gn, sh) in enumerate(shift):
                        ins = nc.vector.tensor_scalar(dst_t(k)[:, a:b], dst_t(k)[:, a:b], sh, None, ALU.add)
                    ins.then_inc(nm.t, 1)

            def lowed(nm, k, dst_t, lo_dst, hi_src):
                nm.wait(v, "hi", k + 1)
                nc.vector.tensor_tensor(lo_dst(k), dst_t(k), hi_src(k).bitcast(F32), ALU.subtract).then_inc(nm.lo, 1)

            def norm_tiles(nm, src, gain, dst_t, lo_dst, hi_src, n, shift=lambda k: None):
                nm.wait(v, "r", 1)
                for k in range(KT):
                    normed(nm, k, src(k), gain(k), dst_t, lo_dst, hi_src, n, shift(k))
                    if k:
                        lowed(nm, k - 1, dst_t, lo_dst, hi_src)
                lowed(nm, KT - 1, dst_t, lo_dst, hi_src)

            norm_tiles(nm1, lambda k: xin[:, k, :], lambda k: gains[:, G_MIX_PRE, k:k + 1], lambda k: xn[:, k % 2, 0:S],
                       lambda k: x1l[:, k, :], lambda k: x1h[:, k, :], S)
            r = 0
            for u in range(N_ATT):
                if 2 <= u < 10:
                    if u % 2 == 1:
                        unit_done(v, u)
                        c = (u - 2) // 2
                        done(nc.vector.tensor_copy(hbias[:, c:c + 1], ps[:, r % 2, 64:65]))
                        settle(v)
                        src = ps[:, r % 2, 0:64].rearrange("p (g n) -> p g n", g=2)[:, :, 0:NCMP]
                        nc.vector.tensor_scalar(hid[:, c, :].rearrange("p (g n) -> p g n", g=2), src, hbias[:, c:c + 1], None,
                                                ALU.add).then_inc(res_free, 1)
                        r += 1
                    if u == 9:
                        v.wait_ge(res_free, 6)
                        done(nc.vector.tensor_tensor(gl1[:], hid[:], hid[:], ALU.mult))
                        settle(v)
                        done(nc.vector.tensor_scalar(gl1[:], gl1[:], 0.044715, 1.0, ALU.mult, ALU.add))
                        settle(v)
                        nc.vector.tensor_tensor(gl1[:], gl1[:], hid[:], ALU.mult).then_inc(gel_t, 1)
                    continue
                if u in (0, 1):
                    for g in range(2):
                        for op in range(2):
                            v.wait_ge(f_hi, 6 * u + 4)
                            src = ps[g * HD:(g + 1) * HD, u % 2].rearrange("p (t o) -> p t o", o=2)[:, :, op]
                            dsl = (slice(op * HD, (op + 1) * HD), u, slice(g * 256, (g + 1) * 256))
                            ins = nc.vector.tensor_tensor(fl[dsl], src, fh[dsl].bitcast(F32), ALU.subtract)
                    ins.then_inc(res_free, 1)
                    v.wait_ge(f_hi, 6 * u + 6)
                    for a, b in ((0, 8), (8, 16)):
                        ins = nc.vector.tensor_tensor(fl[:, u, 512 + a:512 + b], pos[:, u, a:b],
                                                      fh[:, u, 512 + a:512 + b].bitcast(F32), ALU.subtract)
                    ins.then_inc(f_lo, 1)
                elif u < 14:
                    unit_done(v, u)
                    nc.vector.tensor_scalar(q_n[:, u - 10, :], ps[:, r % 2], -0.125, None, ALU.mult).then_inc(res_free, 1)
                elif u < 16:
                    unit_done(v, u)
                    nc.vector.tensor_copy(k_all[:, u - 14, :], ps[:, r % 2]).then_inc(res_free, 1)
                elif u < 18:
                    unit_done(v, u)
                    nc.vector.tensor_copy(vT[:, u - 16, :], ps[:, r % 2]).then_inc(res_free, 1)
                elif u == 18:
                    v.wait_ge(th_a, 2)
                    done(nc.vector.tensor_scalar(hbias[:, 0:1], lam, 1.0, None, ALU.mult))
                    settle(v)
                    nc.vector.tensor_copy(hbias[:, 1:2], hbias[:, 0:1]).then_inc(res_free, 1)
                elif u < 23:
                    unit_done(v, u)
                    nc.vector.tensor_scalar(q_s[:, u - 19, :], ps[:, r % 2], -0.125, None, ALU.mult).then_inc(res_free, 1)
                elif u == 23:
                    unit_done(v, u)
                    nc.vector.tensor_copy(k_all[:, 2, :], ps[:, r % 2]).then_inc(res_free, 1)
                else:
                    unit_done(v, u)
                    nc.vector.tensor_copy(vT[:, 2, :], ps[:, r % 2]).then_inc(res_free, 1)
                r += 1
                if u == 10:
                    v.wait_ge(th_a, 1)
                    done(nc.vector.scalar_tensor_tensor(out=gl3[:], in0=gl2[:], scalar=1.0, in1=hid[:], op0=ALU.add,
                                                        op1=ALU.mult))
                    settle(v)
                    nc.vector.tensor_scalar(gl3[:], gl3[:], 0.5, None, ALU.mult).then_inc(gel, 1)
            v.wait_ge(pr_mm, 1)
            nc.vector.tensor_copy(kcmp[:, 0:NCMP], ps[:, 2, 0:NCMP])
            nc.vector.tensor_copy(vcmp[0:NCMP].rearrange("p g d -> p (g d)"), ps[0:NCMP, 3, 0:P])
            for n in range(4):
                v.wait_ge(pr_mm, n + 2)
                if n < 3:
                    nc.vector.tensor_copy(v_all[:, n].rearrange("p t d -> p (t d)"), ps[:, 4 + n])
                else:
                    nc.vector.tensor_scalar(gate[:].rearrange("p t d -> p (t d)"), ps[:, 4 + n], 0.5, 0.5, ALU.mult, ALU.add)
            end_phase(v, "prep")
            begin_after(v, "prep")
            v.wait_ge(strips_in, 32)
            attn_dve(v, A1)
            end_phase(v, "nsa")
            begin_after(v, "nsa")
            v.drain().then_inc(up_free, 2)
            with v.Fori(0, 2) as i:
                for m in range(4):
                    b = m % 2
                    unit_done(v, U_UP + m * 3 + 2, i, 12)
                    v.wait_ge(up_t, i * 8 + (2 * m + 2))
                    for j in range(2):
                        ins = nc.vector.scalar_tensor_tensor(out=tg[:, b, j, :], in0=tg[:, b, j, :], scalar=1.0,
                                                             in1=ps[:, 4 + 2 * j + b], op0=ALU.add, op1=ALU.mult)
                        ins.then_inc(up_v, 1)
                    v.wait_ge(up_v, i * 12 + (3 * m + 2))
                    nc.vector.tensor_tensor(tg[:, b, 0, :], tg[:, b, 0, :], tg[:, b, 1, :], ALU.add).then_inc(up_v, 1)
                    v.wait_ge(up_v, i * 12 + (3 * m + 3))
                    nc.vector.tensor_scalar(ty[:, b, :], tg[:, b, 0, :], 0.5, None, ALU.mult).then_inc(up_y, 1)
                    v.wait_ge(up_hi, i * 4 + (m + 1))
                    yi = bass.ds(i * 4 + m, 1)
                    nc.vector.tensor_tensor(y1l[:, yi, :].rearrange("p a s -> p (a s)"), ty[:, b, :],
                                            y1h[:, yi, :].rearrange("p a s -> p (a s)").bitcast(F32),
                                            ALU.subtract).then_inc(up_free, 1)
            end_phase(v, "up")
            begin_after(v, "up")
            nc.vector.memset(sqsum[:, 0:S], 0.0).then_inc(nm2a.add, 2)
            nm2a.wait(v, "add", 2)
            v.drain().then_inc(wo_free[0], 2)
            with v.Fori(0, 2) as i:
                for j in range(4):
                    v.wait_ge(wo_free[0], i * 4 + (j + 3))
                    nm2a.wait(v, "add", i * 4 + (j + 2))
                    nc.vector.tensor_tensor(sqsum[:, 0:S], sqsum[:, 0:S], sq[:, j % 2, 0:S], ALU.add).then_inc(nm2a.add, 1)
            nm2a.wait(v, "r", 1)
            end_phase(v, "wout")
            begin_after(v, "wout")
            v.wait_ge(x_in, 32)

            def post_norm(nmb, gain_row, n2):
                for k in range(KT):
                    done(nc.vector.scalar_tensor_tensor(out=f_t[:, k, :], in0=f_t[:, k, :], scalar=gains[:, gain_row, k:k + 1],
                                                        in1=rstd[:, 0:S], op0=ALU.mult, op1=ALU.mult))
                for k in range(KT):
                    settle(v)
                    nc.vector.tensor_tensor(hc[:, k, 0:S], hc[:, k, 0:S], f_t[:, k, :], ALU.add).then_inc(nmb.src, 1)
                    if k:
                        add_square(v, nmb, k - 1, n2)
                add_square(v, nmb, KT - 1, n2)
            post_norm(nm2b, G_MIX_POST, S)
            norm_tiles(nm2b, lambda k: hc[:, k, 0:S], lambda k: gains[:, G_MLP_PRE, k:k + 1], lambda k: xn2[:, k % 2, 0:S],
                       lambda k: x1l[:, k, :], lambda k: x1h[:, k, :], S)
            nc.vector.memset(f_t[:], 0.0).then_inc(f_zero, 1)
            end_phase(v, "norm2")
            begin_after(v, "norm2")
            v.drain().then_inc(ml_f, 2)
            v.drain().then_inc(mod_ev, 1)
            v.wait_ge(f_zero, 1)
            with v.Fori(0, 4) as i:
                for j in range(16):
                    unit_done(v, U_MLP + j, i, 16)
                    if j < 8:
                        v.wait_ge(ml_relu, i * 8 + (j + 1))
                        nc.vector.scalar_tensor_tensor(out=msq[:, j % 2, :], in0=ps[:, j % 2], scalar=0.0, in1=relu[:, j % 2, :],
                                                       op0=ALU.max, op1=ALU.mult).then_inc(ml_sq, 1)
                        v.wait_ge(ml_hi, i * 8 + (j + 1))
                        nc.vector.tensor_tensor(m_l[:, j, :], msq[:, j % 2, :], m_h[:, j, :].bitcast(F32),
                                                ALU.subtract).then_inc(ml_lo, 1)
                        v.wait_ge(ml_lo, i * 8 + (j + 1))
                        nc.vector.memset(esk[:, 0:1], 0.0).then_inc(ml_f, 1)
                    else:
                        nc.vector.tensor_tensor(f_t[:, j - 8, :], ps[:, j % 2], f_t[:, j - 8, :], ALU.add).then_inc(ml_f, 1)
                v.wait_ge(mod_mm, i * 12 + 12)
                nc.vector.tensor_tensor(mod[:, bass.ds(i * 12, 12), :], ps[:, 7, 0:24].rearrange("p (c v) -> p c v", v=2),
                                        bmod[:, bass.ds(i * 12, 12)].unsqueeze(2).to_broadcast([P, 12, 2]),
                                        ALU.add).then_inc(mod_ev, 1)
            for k in range(KT):
                add_square(v, nm3a, k, S)
            v.wait_ge(mod_ev, 5)
            for l in range(2):
                for w in range(2):
                    done(nc.vector.scalar_tensor_tensor(out=mulx[:, l, w, :], in0=mod[:, l * 24 + 8:l * 24 + 16, w], scalar=1.0,
                                                        in1=gains[:, G_A + l, :], op0=ALU.add, op1=ALU.mult))
            settle(v)
            nm3a.wait(v, "r", 1)
            end_phase(v, "mlp")
            begin_after(v, "mlp")
            v.wait_ge(ctx_in, 16)
            post_norm(nm3b, G_MLP_POST, SC)

            def modulated(nm, l, dst):
                norm_tiles(nm, lambda k: hc[:, k, :], lambda k: None, dst, lambda k: x2l[:, k, :], lambda k: x2h[:, k, :], SC,
                           lambda k: [(0, S, mulx[:, l, 0, k:k + 1], mod[:, l * 24 + k, 0:1]),
                                      (S, SC, mulx[:, l, 1, k:k + 1], mod[:, l * 24 + k, 1:2])])
            modulated(nm3b, 0, lambda k: xn2[:, k % 2, :])
            end_phase(v, "norm3")
            begin_after(v, "norm3")
            v.wait_ge(tab_in, 32)
            def rotate(head, n, ready):
                x = (a_q, a_k)[n][head[1] % 2]
                wait_head(v, ready, head, 1, 1)
                wait_head(v, "ro", head, 2, n)
                nc.vector.tensor_tensor(ropea[:, 2, :], x[:, 0:S], cos_t[:], ALU.mult).then_inc(ha["c"], 1)
                nc.vector.stream_shuffle(ropea[:, 0, :], x[:, 0:S], SHUFFLE).then_inc(ha["c"], 1)
                wait_head(v, "c", head, 6, 3 * n + 2)
                nc.vector.tensor_tensor(ropea[:, 1, :], ropea[:, 0, :], sin_t[:], ALU.mult).then_inc(ha["c"], 1)
                wait_head(v, "c", head, 6, 3 * n + 3)
                nc.vector.tensor_tensor(x[:, 0:S], ropea[:, 1, :], ropea[:, 2, :], ALU.add).then_inc(ha["ro"], 1)

            def gate_up(head):
                g = a_g[head[1] % 2]
                wait_head(v, "gt", head, 1, 1)
                nc.vector.scalar_tensor_tensor(out=g[:], in0=g[:], scalar=1.0, in1=pair(0)[:, 0:SC], op0=ALU.add,
                                               op1=ALU.mult).then_inc(ha["g"], 1)

            def output(head):
                i, c = head
                wait_head(v, "r", head, 1, 1)
                nc.vector.scalar_tensor_tensor(out=a_sq[:], in0=pair(3)[:, 0:SC], scalar=subs, in1=rstd[:], op0=ALU.mult,
                                               op1=ALU.mult).then_inc(ha["on"], 1)
                wait_head(v, "on", head, 1, 1)
                dst = o2[:, c, :] if i is None else o2[:, bass.ds(i * 2 + c, 1), :].rearrange("p a s -> p (a s)")
                nc.vector.tensor_tensor(dst, a_sq[:], a_g[c % 2][:], ALU.mult).then_inc(ha["o"], 1)

            def attend(head, more):
                i, c = head

                def mins(qt):
                    n = SC if qt < QT else C
                    wait_head(v, "t", head, 6, qt - 2)
                    for m in range(2):
                        wait_head(v, "s", head, 12, 2 * qt + m + 1)
                        cc = 2 * (qt % 3) + m
                        nc.vector.memset(tick, 0.0)
                        nc.vector.tensor_tensor_reduce(
                            out=a_p[qt % 3][m][:, 0:n], in0=pair(1)[:, 0:n], in1=zero.to_broadcast([P, n]), scale=1.0,
                            scalar=3e38, op0=ALU.add, op1=ALU.min, accum_out=negm[:, cc:cc + 1]).then_inc(ha["m"], 1)

                def combine(qt):
                    n = SC if qt < QT else C
                    cc = 2 * (qt % 3)
                    wait_head(v, "e", head, 12, 2 * qt + 2)
                    nc.vector.reciprocal(rs[:, cc:cc + 2], sums[:, cc:cc + 2]).then_inc(ha["w"], 1)
                    wait_head(v, "w", head, 18, 3 * qt + 1)
                    nc.vector.tensor_tensor(wgt[:, cc:cc + 1], rs[:, cc + 1:cc + 2], lam, ALU.mult).then_inc(ha["w"], 1)
                    wait_head(v, "w", head, 18, 3 * qt + 2)
                    p0, p1 = [x[:, 0:n] for x in a_p[qt % 3]]
                    nc.vector.tensor_scalar(p1, p1, wgt[:, cc:cc + 1], None, ALU.mult).then_inc(ha["w"], 1)
                    wait_head(v, "w", head, 18, 3 * qt + 3)
                    nc.vector.scalar_tensor_tensor(out=p0, in0=p0, scalar=rs[:, cc:cc + 1],
                                                   in1=p1, op0=ALU.mult, op1=ALU.subtract).then_inc(ha["a"], 1)
                mins(0)
                mins(1)
                if c > 0:
                    output((i, c - 1))
                for qt in range(6):
                    combine(qt)
                    if qt < 4:
                        mins(qt + 2)
                    if qt == 1 and more:
                        rotate((i, c + 1), 0, "q")
                    if qt == 3 and more:
                        rotate((i, c + 1), 1, "k")
                if more:
                    gate_up((i, c + 1))

            rotate((None, 0), 0, "q")
            rotate((None, 0), 1, "k")
            gate_up((None, 0))
            all_heads(v, attend)
            output((None, 7))
            end_phase(v, "heads")
            begin_after(v, "heads")

            def residual(n, l, u0, wide):
                v.drain().then_inc(wo_free[n], 2)
                with v.Fori(0, 2) as i:
                    for j in range(4):
                        unit_done(v, u0 + j, i, 4)
                        k = bass.ds(i * 4 + j, 1)
                        gcol = mod[:, bass.ds(l * 24 + 16 + i * 4 + j, 1), :].rearrange("p a v -> p (a v)")
                        for w, a, b in ((0, 0, S), (1, S, SC))[0:1 + wide]:
                            src = (pair(j % 2) if wide else ps[:, j % 2])[:, a:b]
                            hk = hc[:, k, a:b].rearrange("p a s -> p (a s)")
                            ins = nc.vector.scalar_tensor_tensor(out=hk, in0=src, scalar=gcol[:, w:w + 1], in1=hk,
                                                                 op0=ALU.mult, op1=ALU.add)
                        ins.then_inc(wo_free[n], 1)
            for k in range(KT):
                v.wait_ge(ha["hi"], k + 1)
                nc.vector.tensor_tensor(x2l[:, k, :], o2[:, k, :], x2h[:, k, :].bitcast(F32), ALU.subtract).then_inc(ha["lo"], 1)
            residual(1, 0, U_AO, 1)
            end_phase(v, "ao")
            begin_after(v, "ao")
            for k in range(KT):
                add_square(v, nm4, k, SC)
            modulated(nm4, 1, lambda k: xn2[:, k % 2, :])
            end_phase(v, "norm4")
            begin_after(v, "norm4")
            for u in range(N_B):
                if u < 10:
                    x = b_q[:, u, :] if u < 8 else b_k[:, u - 8, 0:S]
                    v.wait_ge(hb["free"], u + 1)
                    nc.vector.stream_shuffle(ropeb[:, 0, :], x, SHUFFLE)
                    done(nc.vector.tensor_tensor(ropeb[:, 2, :], x, cos_t[:], ALU.mult))
                    settle(v)
                    done(nc.vector.tensor_tensor(ropeb[:, 1, :], ropeb[:, 0, :], sin_t[:], ALU.mult))
                    settle(v)
                    done(nc.vector.tensor_tensor(x, ropeb[:, 1, :], ropeb[:, 2, :], ALU.add))
                    settle(v)
                elif u >= 12:
                    v.wait_ge(hb["gt"], u - 11)
                    nc.vector.scalar_tensor_tensor(out=b_g[:, u - 12, :], in0=b_g[:, u - 12, :], scalar=1.0, in1=ps[:, 2 * (u % 2)],
                                                   op0=ALU.add, op1=ALU.mult).then_inc(hb["free"], 1)
                if u == 13:
                    for n in range(2):
                        v.wait_ge(hb["vt"], n + 1)
                        nc.vector.tensor_copy(b_v[:, :, n * P:(n + 1) * P],
                                              pair(2)[:, 0:SC].rearrange("p (b d) -> p b d", b=6)).then_inc(hb["ve"], 1)
            v.wait_ge(tab_in, 64)
            end_phase(v, "bqkv")
            begin_after(v, "bqkv")
            attn_dve(v, A2)
            end_phase(v, "battn")
            begin_after(v, "battn")
            residual(2, 1, U_BO, 0)
            for k in range(KT):
                add_square(v, nm5, k, S)
            nm5.wait(v, "r", 1)
            for k in range(KT):
                nc.vector.scalar_tensor_tensor(out=xo[:, k, :], in0=hc[:, k, 0:S], scalar=gains[:, G_FINAL, k:k + 1],
                                               in1=rstd[:, 0:S], op0=ALU.mult, op1=ALU.mult).then_inc(nm5.t, 1)


def _units(w):
    import numpy as np
    k, m = w.shape
    return np.ascontiguousarray(w.reshape(k // 1024, 8, 128, m // 128, 128).transpose(3, 0, 2, 1, 4))


def _tables():
    import math
    import numpy as np
    f = np.float32
    dist = 511 - np.arange(TBL)
    d = np.maximum(dist, 0)
    df = np.maximum(d, 1).astype(f)
    large = 16 + (np.log(df / f(16)) / f(math.log(1024 / 16)) * f(16)).astype(np.int32)
    bucket = np.where(d < 16, d, np.minimum(large, BUCKETS - 1))
    onehot = np.zeros((34, TBL), f)
    onehot[bucket, np.arange(TBL)] = -1.0
    onehot[32] = np.where(dist >= 0, 0.0, BIG)
    onehot[33] = np.where((dist >= 0) & (dist < 128), 0.0, BIG)
    selrows = np.zeros((2, 16), f)
    selrows[0, 0:8] = 1.0
    selrows[1, 8:16] = 1.0
    p = np.arange(P)
    tq = np.arange(QT)[None, :] * P + p[:, None]
    cmask = np.where(np.arange(NCMP)[None, None, :] * 16 + 31 <= tq[:, :, None], 0.0, BIG).astype(f)
    band = np.where(np.abs(p[:, None] - np.arange(384)[None, :] + 128) <= 128, 0.0, BIG).astype(f)
    bm1 = np.concatenate([np.zeros((P, C), f), band], 1)
    bm0 = np.concatenate([np.zeros((P, C), f), band[:, 128:384]], 1)
    tok = np.arange(S)
    inv = f(10000.0) ** (-np.arange(0, 32, 2, dtype=f) / f(32))
    row, col = (tok // 64).astype(f), (tok % 64).astype(f)
    feat = np.arange(64)
    ang = np.where((feat < 32)[:, None], row[None, :], col[None, :]).astype(f) * inv[feat % 16][:, None]
    cos, sin = np.cos(ang).astype(f), np.sin(ang).astype(f)
    sin = np.where((feat % 32 < 16)[:, None], -sin, sin)
    return dict(ident=np.eye(P, dtype=f), onehot=onehot, selrows=selrows, cmask=cmask, bm0=bm0, bm1=bm1,
                cos=np.concatenate([cos, cos], 0), sin=np.concatenate([sin, sin], 0))


def kernel(x, norm_mix_pre, norm_mix_post, norm_mlp_pre, norm_mlp_post, w_in, cmp_pos_k, cmp_w1_k, cmp_w2_k, cmp_pos_v,
           cmp_w1_v, cmp_w2_v, attn_sinks, rel_bias, w_up_nsa, w_up_swa, w_out, w_mlp_in, w_mlp_out, c_2, ctx_2, c_ctx_2,
           w_mod_2, b_mod_2, norm_g_2, w_o_2, a_w_in_2, a_lambda_q1_2, a_lambda_k1_2, a_lambda_q2_2, a_lambda_k2_2,
           a_subln_g_2, b_w_in_2, b_sink_2, final_g_2):
    import numpy as np
    import concourse.bacc as bacc
    from concourse import mybir as mb
    from concourse.bass_utils import run_bass_kernel_spmd

    def cols(a):
        a = np.asarray(a)
        return np.moveaxis(a.reshape(a.shape[:-1] + (-1, P)), -1, 0)

    def tmajor(a):
        a = np.asarray(a)
        return a.reshape(a.shape[0], KT, P).transpose(2, 1, 0)

    def pair_heads(n_kv, rep, w):
        i = np.arange(n_kv * rep * HD).reshape(n_kv // 2, 2, rep, HD)
        return w + i.transpose(0, 2, 1, 3).reshape(-1)

    w_in = np.asarray(w_in)[0]
    qn = pair_heads(2, 4, 0)
    w_att = [_units(w_in[:, 512:768])[:, 0]]
    for w in (cmp_w1_k, cmp_w1_v):
        w_att.append(_units(np.asarray(w)[0]).reshape(4, P, KT, P))
    gcols = np.zeros((D, P), np.float32)
    gcols[:, 0:24] = w_in[:, 1280:1304]
    att_cols = np.concatenate([w_in[:, qn], w_in[:, 768:896], w_in[:, 1024:1152], w_in[:, 896:1024], w_in[:, 1152:1280],
                               gcols, w_in[:, 1304 + qn], w_in[:, 1816:1944], w_in[:, 1944:2072]], 1)
    w_att.append(_units(att_cols)[:, 0])
    ga, gb = _units(w_in[:, 2072:3096])[:, 0], _units(w_in[:, 3096:4120])[:, 0]
    up = np.concatenate([np.asarray(w_up_nsa)[0][qn], np.asarray(w_up_swa)[0][qn]], 0)
    w_up = np.stack([ga, gb, _units(up)[:, 0]], 1).reshape(24, P, KT, P)
    m_in = _units(np.asarray(w_mlp_in)[0])[:, 0].reshape(4, 8, P, KT, P)
    m_out = _units(np.asarray(w_mlp_out)[0]).transpose(1, 0, 2, 3, 4)
    w_mlp = np.concatenate([m_in, m_out], 1).reshape(64, P, KT, P)
    w_mod = np.concatenate([_units(np.asarray(w_mod_2)[l])[:, 0] for l in range(2)], 0)
    w_mod = np.concatenate([w_mod, w_mod[0:3]], 0)
    w_a = _units(np.asarray(a_w_in_2)[0])[:, 0].reshape(4, 8, P, KT, P).transpose(1, 0, 2, 3, 4).reshape(32, P, KT, P)
    wo = np.asarray(w_o_2)
    bw = np.asarray(b_w_in_2)[0]
    bq = pair_heads(4, 4, 0)
    w_b = _units(np.concatenate([bw[:, bq], bw[:, 1024:1536], bw[:, 1536 + bq]], 1))[:, 0]
    w2 = np.stack([np.asarray(w)[0].reshape(2, P, HD) for w in (cmp_w2_k, cmp_w2_v)], 0).transpose(2, 0, 1, 3)
    pos = np.stack([np.asarray(w)[0].reshape(16, P).T for w in (cmp_pos_k, cmp_pos_v)], 1)
    gains = np.stack([np.asarray(norm_mix_pre)[0], np.asarray(norm_mix_post)[0], np.asarray(norm_mlp_pre)[0],
                      np.asarray(norm_mlp_post)[0], np.asarray(norm_g_2)[0], np.asarray(norm_g_2)[1],
                      np.asarray(final_g_2)], 0)
    ins = dict(_tables())
    ins.update(
        xT=tmajor(np.asarray(x)[0]), ctxT=tmajor(np.asarray(ctx_2)[0]), gains=cols(gains),
        bmod=cols(np.asarray(b_mod_2)).reshape(P, 48),
        cin=cols(np.stack([np.asarray(c_2)[0], np.asarray(c_ctx_2)], 0)).transpose(0, 2, 1).reshape(P, 16),
        lamv=np.stack([np.asarray(a)[0] for a in (a_lambda_q1_2, a_lambda_k1_2, a_lambda_q2_2, a_lambda_k2_2)], 1),
        subg=np.asarray(a_subln_g_2)[0].reshape(P, 1), w2=w2, pos=pos, rel_bias=np.asarray(rel_bias),
        sinks=np.concatenate([np.asarray(attn_sinks)[0], np.asarray(b_sink_2)[0]]).reshape(1, 24),
        w_att=np.concatenate(w_att, 0), w_up=w_up, w_out=_units(np.asarray(w_out)[0])[:, 0], w_mlp=w_mlp, w_mod=w_mod,
        w_a=w_a, w_ao=_units(wo[0])[:, 0], w_b=w_b, w_bo=_units(wo[1][bq])[:, 0])
    nc = bacc.Bacc("TRN2", target_bir_lowering=False, num_devices=1)
    arrays, t = {}, {}
    for name, a in ins.items():
        a = np.ascontiguousarray(a)
        arrays["in_" + name] = a
        t[name] = nc.dram_tensor("in_" + name, a.shape, mb.dt.from_np(a.dtype), kind="ExternalInput").ap()
    out = nc.dram_tensor("out", (P, KT, S), mb.dt.float32, kind="ExternalOutput").ap()
    build(nc, t, out)
    r = run_bass_kernel_spmd(nc, [arrays], core_ids=[0])
    y = r.results[0]["out"]
    return np.ascontiguousarray(y.transpose(2, 1, 0).reshape(1, S, D))
```

```python
from contextlib import ExitStack

import concourse.bass as bass
from concourse import mybir

F32 = mybir.dt.float32
F32R = mybir.dt.float32r
ALU = mybir.AluOpType
ACT = mybir.ActivationFunctionType
AX = mybir.AxisListType

P = 128
D = 1024
KT = D // P
S = 512
C = 256
SC = S + C
QT = S // P
HD = 64
REP = 4
NCMP = 31
HID = 256
EPS = 1e-6
SUB_EPS = 1e-5
LAM_INIT = 0.8 - 0.6
BIG = 1e30
GELU_C = 0.7978845608028654
RAW = 4
MRAW = 4
SPL = 2
BUCKETS = 32
TBL = 640

N_ATT = 25
N_G = 16
N_UP = 8
N_OUT = 8
N_MLP = 64
N_MOD = 48
N_A = 32
N_B = 20
U_ATT = 0
U_G = U_ATT + N_ATT
U_UP = U_G + N_G
U_OUT = U_UP + N_UP
U_MLP = U_OUT + N_OUT
U_A = U_MLP + N_MLP
U_AO = U_A + N_A
U_B = U_AO + N_OUT
U_BO = U_B + N_B
U_END = U_BO + N_OUT

G_MIX_PRE, G_MIX_POST, G_MLP_PRE, G_MLP_POST, G_A, G_B, G_FINAL = range(7)
SHUFFLE = [(i + 16) % 32 for i in range(32)]


def build(nc, t, out):
    base = 16512
    KB = 1024
    with ExitStack() as ctx:
        def at(name, kb, shape, dt=F32):
            return nc.alloc_sbuf_tensor_at(name, shape, dt, offset=base + int(kb * KB))

        def sem(name):
            return ctx.enter_context(nc.semaphore(name))

        raw = at("raw", 0, [P, RAW, KT, P])
        w_h = at("w_h", 16, [P, SPL, KT, P], F32R)
        w_l = at("w_l", 24, [P, SPL, KT, P], F32R)
        x1h = at("x1h", 32, [P, KT, S], F32R)
        x1l = at("x1l", 48, [P, KT, S], F32R)
        x2h = at("x2h", 32, [P, KT, SC], F32R)
        x2l = at("x2l", 56, [P, KT, SC], F32R)
        hc = at("hc", 80, [P, KT, SC])
        c0 = 104
        ident = at("ident", c0, [P, P])
        ones = at("ones", c0 + 0.5, [P, P])
        small = at("small", c0 + 1, [P, 896])
        rstd = at("rstd", c0 + 4.5, [P, SC])
        sq = at("sq", c0 + 7.5, [P, 2, SC])
        sqsum = at("sqsum", c0 + 13.5, [P, SC])
        z = c0 + 16.5

        o_ = [0]

        def sm(n):
            a = small[:, o_[0]:o_[0] + n]
            o_[0] += n
            return a
        gains = sm(56).rearrange("p (g k) -> p g k", g=7)
        bmod = sm(48)
        mod = sm(96).rearrange("p (c v) -> p c v", v=2)
        sinks = sm(24)
        nsinks = sm(24)
        lamv = sm(4)
        lamp = sm(2)
        lame = sm(2)
        lam = sm(1)
        subg = sm(1)
        subs = sm(1)
        eps_t = sm(1)
        seps_t = sm(1)
        negm = sm(8)
        sums = sm(8)
        rs = sm(8)
        wgt = sm(8)
        esk = sm(8)
        spare = sm(1)
        mcol = sm(24).rearrange("p (c v) -> p c v", v=2)
        zero = sm(1)
        tick = sm(3)
        mulx = sm(32).rearrange("p (l v k) -> p l v k", l=2, v=2)
        assert o_[0] <= 896

        q_n = at("q_n", 64, [P, REP, S])
        q_s = at("q_s", 72, [P, REP, S])
        k_all = at("k_all", 80, [P, 3, S])
        v_all = at("v_all", 86, [P, 3, QT, P])
        gate = at("gate", 92, [P, QT, P])
        strip_s = at("strip_s", 94, [P, 8, 256])
        kcmp = at("kcmp", 102, [P, 32])
        vcmp = at("vcmp", 102.25, [P, 2, HD])
        cmask = at("cmask", 102.75, [P, QT, NCMP])
        strip_n = at("strip_n", z, [P, 8, S])
        sb1 = [at("sb1_0", z + 16, [P, REP, S]), at("sb1_1", z + 24, [P, REP, S]), at("sb1_2", z + 72, [P, REP, S])]
        vT = at("vT", z + 32, [P, 4, S])
        pt1 = at("pt1", z + 32, [P, 4, S])
        o1h = at("o1h", z + 40, [P, 8, S], F32R)
        o1l = at("o1l", z + 56, [P, 8, S], F32R)
        xin = at("xin", z + 40, [P, KT, S])
        xn = at("xn", z + 56, [P, 2, SC])
        FW = 3 * 256 + 8
        fh = at("fh", z + 16, [P, 2, FW], F32R)
        fl = at("fl", z + 16 + 6.25, [P, 2, FW], F32R)
        g0 = z + 72
        hid = at("hid", g0, [P, 4, 2 * NCMP])
        gl1 = at("gl1", g0 + 1, [P, 4, 2 * NCMP])
        gl2 = at("gl2", g0 + 2, [P, 4, 2 * NCMP])
        gl3 = at("gl3", g0 + 3, [P, 4, 2 * NCMP])
        hbias = at("hbias", g0 + 4, [P, 4])
        w2 = at("w2", g0 + 4.25, [P, 2, 2, HD])
        pos = at("pos", g0 + 5.25, [P, 2, 16])
        brow = at("brow", g0 + 5.5, [16, TBL])
        onehot = at("onehot", g0 + 8, [34, TBL])
        blhs = at("blhs", g0 + 10.5, [34, 16])
        y1h = at("y1h", z, [P, 8, S], F32R)
        y1l = at("y1l", z + 16, [P, 8, S], F32R)
        tg_parts = [at("tg0", 64, [P, 4, 2, S]), at("tg1", z + 32, [P, 2, 2, S]), at("tg2", z + 72, [P, 2, 2, S])]
        tg = [tg_parts[0][:, m] if m < 4 else tg_parts[m // 2 - 1][:, m % 2] for m in range(8)]
        g_stage = at("g_stage", z + 80, [P, 3, S])
        ty = at("ty", z + 80, [P, 2, S])
        f_t = at("f_t", z + 32, [P, KT, S])
        m_h = at("m_h", z, [P, 8, S], F32R)
        m_l = at("m_l", z + 16, [P, 8, S], F32R)
        relu = at("relu", z + 48, [P, 2, S])
        msq = at("msq", z + 52, [P, 2, S])
        mraw = at("mraw", z + 70, [P, MRAW, KT, P])
        crow = at("crow", z + 56, [P, 2, D])
        ctanh = at("ctanh", z + 48, [P, 2, D])
        terms = at("terms", z + 64, [P, D])
        xn2 = at("xn2", z + 64, [P, 2, SC])
        o2 = at("o2", z, [P, KT, SC])
        a_q = [at("a_q0", z + 48, [P, SC]), at("a_q1", z + 24, [P, SC])]
        a_k = [at("a_k0", z + 51, [P, SC]), at("a_k1", z + 27, [P, SC])]
        a_g = [at("a_g0", z + 54, [P, SC]), at("a_g1", z + 30, [P, SC])]
        a_vT = at("a_vT", z + 33, [P, SC])
        ropea = at("ropea", z + 36, [P, 3, S])
        a_sq = at("a_sq", z + 42, [P, SC])
        cos_t = at("cos_t", z + 57, [P, S])
        sin_t = at("sin_t", z + 59, [P, S])
        a_p = [[at(f"a_p{n}{m}", o, [P, SC]) for m, o in enumerate(os)]
               for n, os in enumerate(((z + 61, z + 64), (z + 67, z + 70), (z + 45, c0 + 9.5)))]
        a_pt = at("a_pt", z + 73, [P, 6, S])
        a_pt2 = at("a_pt2", c0 + 7.5, [P, 2, C])
        a_v = at("a_v", c0 + 13.5, [P, 6, P])
        b_q = at("b_q", z, [P, 8, S])
        b_k = at("b_k", z + 16, [P, 2, SC])
        b_v = at("b_v", z + 22, [P, 6, 256])
        b_g = at("b_g", z + 28, [P, 8, S])
        bm0 = at("bm0", z + 44, [P, 512])
        bm1 = at("bm1", z + 46, [P, 640])
        b_pt = at("b_pt", z + 48.5, [P, 4, S])
        ropeb = at("ropeb", z + 48.5, [P, 3, S])
        b_sb = [at("b_sb0", z + 60.5, [P, REP, 640]), at("b_sb1", z + 70.5, [P, REP, 640]),
                at("b_sb2", 64, [P, REP, 640])]
        b_vT = at("b_vT", z + 64, [P, 2, SC])
        ot = at("ot", z + 80.5, [P, S])
        xo = at("xo", z, [P, KT, S])

        ps = ctx.enter_context(nc.psum_tensor("ps", [P, 8, 512], F32))

        def pair(n):
            return ps[:, 2 * n:2 * n + 2].rearrange("p b c -> p (b c)")

        dbias = nc.dram_tensor("dbias", [16, P, TBL], F32, kind="Internal").ap()

        gates = nc.dram_tensor("gates", [8, P, 2, S], F32, kind="Internal").ap()

        raw_in = [sem(f"raw_in{i}") for i in range(RAW)]
        w_hi = sem("w_hi")
        w_lo = sem("w_lo")
        unit = sem("unit")
        const_in = sem("const_in")
        boot = sem("boot")
        brow_ok = sem("brow_ok")
        dbias_in = sem("dbias_in")
        strips_in = sem("strips_in")
        x_in = [sem("x_in0"), sem("x_in1")]
        tab_in = sem("tab_in")
        ctx_in = sem("ctx_in")
        out_done = sem("out_done")
        v_self = sem("v_self")

        block = ctx.enter_context(nc.Block())

        PHASES = ["prep", "nsa", "up", "wout", "norm2", "mlp", "norm3", "heads", "ao", "norm4", "bqkv", "battn"]
        phase_end = sem("phase_end")

        def end_phase(eng, name):
            eng.drain().then_inc(phase_end, 1)

        def begin_after(eng, name):
            eng.wait_ge(phase_end, 3 * (PHASES.index(name) + 1))

        class Own:
            n = 0

        def done(ins):
            Own.n += 1
            ins.then_inc(v_self, 1)

        def settle(v):
            v.wait_ge(v_self, Own.n)

        def split_high(act, u, i=None, step=0):
            if u >= U_END and i is None:
                return
            v = lambda c: c if i is None else i * step + c
            assert step % RAW == 0
            act.wait_ge(raw_in[u % RAW], 16 * (u // RAW + 1) if i is None else i * (16 * step // RAW) + 16 * (u // RAW + 1))
            if u >= SPL:
                act.wait_ge(unit, v(u - SPL + 1))
            nc.scalar.activation(w_h[:, u % SPL], raw[:, u % RAW], ACT.Copy).then_inc(w_hi, 1)

        def load_unit(sp, u, src, i=None, step=0):
            if u >= RAW:
                sp.wait_ge(w_lo, u - RAW + 1 if i is None else i * step + (u - RAW + 1))
            sp.dma_start(raw[:, u % RAW], src).then_inc(raw_in[u % RAW], 16)

        def products(u, parts, k0=0, k1=KT, first=True, last=True):
            for k in range(k0, k1):
                for wi, w in ((0, w_h), (1, w_l)):
                    for o, xh, xl in parts:
                        mm = nc.tensor.matmul(o, w[:, u % SPL, k], xh(k), start=(first and k == k0 and wi == 0),
                                              stop=(last and k == k1 - 1 and wi == 1))
                    if wi == 0:
                        for o, xh, xl in parts:
                            mm = nc.tensor.matmul(o, w[:, u % SPL, k], xl(k), start=False, stop=False)
            return mm

        def split_ready(pe, u, i=None, step=0):
            pe.wait_ge(w_lo, u + 1 if i is None else i * step + (u + 1))

        def unit_done(eng, u, i=None, step=0):
            eng.wait_ge(unit, u + 1 if i is None else i * step + (u + 1))

        NORM_SEMS = ["src", "sq", "add", "mm", "ln", "r", "t", "hi", "lo"]

        class Norm:
            sems = {n: sem("norm_" + n) for n in NORM_SEMS}
            ends = dict.fromkeys(NORM_SEMS, 0)

            def __init__(self, **counts):
                self.base = dict(Norm.ends)
                for n in NORM_SEMS:
                    Norm.ends[n] += counts.get(n, 1 if n in ("mm", "ln", "r") else 8)
                self.src, self.sq, self.add, self.mm, self.ln, self.r, self.t, self.hi, self.lo = \
                    [Norm.sems[n] for n in NORM_SEMS]

            def wait(self, eng, name, count):
                eng.wait_ge(Norm.sems[name], self.base[name] + count)

        def square_tile(act, nm, k, src, n):
            if k >= 2:
                nm.wait(act, "add", k - 1)
            nc.scalar.activation(sq[:, k % 2, 0:n], src, ACT.Square).then_inc(nm.sq, 1)

        def add_square(v, nm, k, n):
            nm.wait(v, "sq", k + 1)
            if k == 0:
                nc.vector.tensor_copy(sqsum[:, 0:n], sq[:, 0, 0:n]).then_inc(nm.add, 1)
            else:
                nm.wait(v, "add", k)
                nc.vector.tensor_tensor(sqsum[:, 0:n], sqsum[:, 0:n], sq[:, k % 2, 0:n], ALU.add).then_inc(nm.add, 1)

        def sum_features(pe, nm, n, bank, added=KT):
            nm.wait(pe, "add", added)
            mm = nc.tensor.matmul(ps[:, bank, 0:min(n, S)], ones[:], sqsum[:, 0:min(n, S)], start=True, stop=True)
            if n > S:
                mm = nc.tensor.matmul(ps[:, bank + 1, 0:n - S], ones[:], sqsum[:, S:n], start=True, stop=True)
            mm.then_inc(nm.mm, 1)

        def make_rstd(act, nm, n, bank):
            nm.wait(act, "mm", 1)
            src = ps[:, bank:bank + 2].rearrange("p b c -> p (b c)")[:, 0:n]
            nc.scalar.activation(rstd[:, 0:n], src, ACT.Ln, bias=eps_t[:], scale=1.0 / D).then_inc(nm.ln, 1)
            nm.wait(act, "ln", 1)
            nc.scalar.activation(rstd[:, 0:n], rstd[:, 0:n], ACT.Exp, scale=-0.5).then_inc(nm.r, 1)

        none = dict(src=0, t=0, hi=0, lo=0)
        nm1 = Norm(src=0)
        nm2a = Norm(**none, sq=0, add=10)
        nm2b = Norm()
        nm3a = Norm(**none)
        nm3b = Norm()
        nm4 = Norm(src=0)
        nm5 = Norm(src=0, hi=0, lo=0)
        cvec = sem("cvec")
        res_free = sem("res_free")
        f_hi = sem("f_hi")
        f_lo = sem("f_lo")
        th_a = sem("th_a")
        gel = sem("gel")
        gel_t = sem("gel_t")
        pr_mm = sem("pr_mm")
        pr_ev = sem("pr_ev")
        up_free = sem("up_free")
        up_v = sem("up_v")
        f_zero = sem("f_zero")
        g_tanh = sem("g_tanh")
        g_out = [sem(f"g_out{i}") for i in range(3)]
        gate_in = [sem(f"gate_in{i}") for i in range(2)]
        up_y = sem("up_y")
        up_hi = sem("up_hi")
        wo_free = [sem(f"wo_free{i}") for i in range(3)]
        wo_f = [sem(f"wo_f{i}") for i in range(3)]
        ml_relu = sem("ml_relu")
        ml_sq = sem("ml_sq")
        ml_hi = sem("ml_hi")
        ml_lo = sem("ml_lo")
        ml_f = sem("ml_f")
        mod_in = [sem(f"mod_in{i}") for i in range(MRAW)]
        mod_mul = sem("mod_mul")
        crow_in = sem("crow_in")
        c_tanh = sem("c_tanh")
        mod_ev = sem("mod_ev")
        ha = {n: sem("ha_" + n) for n in
              ["q", "k", "v", "g", "gt", "rope", "ro", "vt", "ve", "s", "m", "e", "a", "t", "te", "pv", "sq", "st",
               "ln", "r", "o", "hi", "lo", "w", "c", "on"]}


        def wait_head(eng, name, head, per, k):
            i, c = head
            if i is not None:
                eng.wait_ge(ha[name], i * (2 * per) + (c * per + k))
            elif c * per + k > 0:
                eng.wait_ge(ha[name], c * per + k)

        def all_heads(eng, turn):
            turn((None, 0), True)
            with eng.Fori(0, 3) as i:
                turn((i, 1), True)
                turn((i, 2), True)
            turn((None, 7), False)

        hb = {n: sem("hb_" + n) for n in ["ev", "rope", "free", "gt", "vt", "ve"]}

        class Attn:
            def __init__(self, name, steps, slots, width, sbuf, ptbuf, sbn, finish):
                self.steps, self.slots, self.width, self.sb, self.pt, self.sbn, self.finish = \
                    steps, slots, width, sbuf, ptbuf, sbn, finish
                self.s, self.m, self.e, self.p, self.t, self.te, self.o, self.oh, self.ol, self.k = \
                    [sem(f"{name}_{n}") for n in ("s", "m", "e", "p", "t", "te", "o", "oh", "ol", "k")]
                self.tb = 2
                self.between_pe = self.between_act = self.between_dve = lambda eng, x: None
                self.blk = [sum(len(x["blocks"]) for x in steps[:n]) for n in range(len(steps) + 1)]
                self.grp = [sum(x["last"] for x in steps[:n]) for n in range(len(steps) + 1)]

            def sbank(self, m):
                if self.slots == 4:
                    return ps[:, m % 4]
                return pair(m % 2)

        def attn_scores(pe, A, n, heads=range(REP)):
            if n >= len(A.steps):
                return
            st = A.steps[n]
            for r in heads:
                m = n * REP + r
                if m >= A.slots:
                    pe.wait_ge(A.m, m - A.slots + 1)
                for c, (o, rhs) in enumerate(st["k"]):
                    mm = nc.tensor.matmul(A.sbank(m)[:, o:o + rhs.shape[-1]], st["q"](r), rhs,
                                          start=st["kstart"][c], stop=True, skip_group_check=True)
                mm.then_inc(A.s, 1)

        def attn_out(pe, A, n):
            st = A.steps[n]
            pe.wait_ge(A.p, n + 1)
            nb = len(st["blocks"])
            g = A.grp[n]
            ob = ps[0:HD, 6 + g % 2]

            def turn(b):
                x = A.blk[n] + b
                if x >= A.tb:
                    pe.wait_ge(A.te, x - A.tb + 1)
                o, w = st["blocks"][b]
                for r in range(REP):
                    mm = nc.tensor.transpose(ps[0:w, 4 + x % A.tb, r * P:(r + 1) * P],
                                             A.sb[n % A.sbn][:, r, o:o + w], ident[:])
                mm.then_inc(A.t, 1)

            def weigh(b):
                x = A.blk[n] + b
                pe.wait_ge(A.te, x + 1)
                o, w = st["blocks"][b]
                if b == 0 and st["first"] and g >= 2:
                    pe.wait_ge(A.ol, g - 1)
                mm = nc.tensor.matmul(ob, st["v"][b], A.pt[0:w, x % 4], start=(st["first"] and b == 0),
                                      stop=(st["last"] and b == nb - 1))
                if st["last"] and b == nb - 1:
                    mm.then_inc(A.o, 1)
                else:
                    mm.then_inc(A.k, 1)
            for b in range(nb):
                turn(b)
                A.between_pe(pe, A.blk[n] + b)
                if A.slots == 2 and b == 1:
                    attn_scores(pe, A, n + 2, (2, 3))
                if b:
                    weigh(b - 1)
            weigh(nb - 1)

        def attn_pe(pe, A):
            attn_scores(pe, A, 0)
            attn_scores(pe, A, 1)
            for n in range(len(A.steps)):
                attn_scores(pe, A, n + 2, range(REP) if A.slots == 4 else (0, 1))
                attn_out(pe, A, n)

        def attn_act(act, A):
            def turned(n):
                st = A.steps[n]
                for b, (o, w) in enumerate(st["blocks"]):
                    x = A.blk[n] + b
                    act.wait_ge(A.t, x + 1)
                    if x >= 4:
                        need = x - 3
                        gd = sum(1 for s in range(len(A.steps)) if A.steps[s]["last"] and A.blk[s + 1] <= need)
                        if gd:
                            act.wait_ge(A.o, gd)
                        if need - gd:
                            act.wait_ge(A.k, need - gd)
                    nc.scalar.activation(A.pt[0:w, x % 4], ps[0:w, 4 + x % A.tb], ACT.Copy).then_inc(A.te, 1)
                    A.between_act(act, x)

            def finished(n):
                if A.steps[n]["last"]:
                    A.finish["act"](act, A, n, A.grp[n])

            for n, st in enumerate(A.steps):
                for r in range(REP):
                    m = n * REP + r
                    act.wait_ge(A.m, m + 1)
                    if st["sink"] is not None or st["clamp"]:
                        act.wait_ge(A.m, (n + 1) * REP)
                        act.wait_ge(mfix[A], fixn(A, n) + 1)
                    buf = A.sb[n % A.sbn][:, r, 0:st["keys"]]
                    c = (n % 2) * REP + r
                    nc.scalar.activation(buf, buf, ACT.Exp, bias=negm[:, c:c + 1], scale=-1.0,
                                         accum_out=sums[:, c:c + 1]).then_inc(A.e, 1)
                if st["sink"] is not None:
                    c = (n % 2) * REP
                    nc.scalar.activation(esk[:, c:c + REP], esk[:, c:c + REP], ACT.Exp).then_inc(A.e, 1)
                else:
                    act.wait_ge(A.e, 5 * n + 4)
                    nc.scalar.activation(spare, eps_t[:], ACT.Copy).then_inc(A.e, 1)
                if n:
                    turned(n - 1)
                if n >= 2:
                    finished(n - 2)
            turned(len(A.steps) - 1)
            finished(len(A.steps) - 2)
            finished(len(A.steps) - 1)

        mfix = {}

        def fixn(A, n):
            return sum(1 for s in A.steps[:n] if s["sink"] is not None or s["clamp"])

        def attn_dve(v, A):
            def finished(n):
                if A.steps[n]["last"]:
                    A.finish["dve"](v, A, n, A.grp[n])

            def minima(n):
                st = A.steps[n]
                c = (n % 2) * REP
                if n >= A.sbn:
                    v.wait_ge(A.t, A.blk[n - A.sbn + 1])
                for r in range(REP):
                    m = n * REP + r
                    v.wait_ge(A.s, m + 1)
                    nc.vector.tensor_tensor_reduce(
                        out=A.sb[n % A.sbn][:, r, 0:st["keys"]], in0=A.sbank(m)[:, st["off"]:st["off"] + st["keys"]],
                        in1=st["bias"](r), scale=1.0, scalar=3e38, op0=ALU.add, op1=ALU.min,
                        accum_out=negm[:, c + r:c + r + 1]).then_inc(A.m, 1)
                nm_ = negm[:, c:c + REP]
                if st["clamp"]:
                    v.wait_ge(A.m, (n + 1) * REP)
                    nc.vector.tensor_scalar(nm_, nm_, BIG / 10, None, ALU.min).then_inc(mfix[A], 1)
                if st["sink"] is not None:
                    v.wait_ge(A.m, (n + 1) * REP)
                    k = st["sink"]
                    done(nc.vector.tensor_tensor(nm_, nm_, nsinks[:, k:k + REP], ALU.min))
                    settle(v)
                    nc.vector.tensor_tensor(esk[:, c:c + REP], sinks[:, k:k + REP], nm_, ALU.add).then_inc(mfix[A], 1)

            minima(0)
            for n, st in enumerate(A.steps):
                c = (n % 2) * REP
                if n + 1 < len(A.steps):
                    minima(n + 1)
                if n >= 2:
                    finished(n - 2)
                v.wait_ge(A.e, 5 * (n + 1))
                su = sums[:, c:c + REP]
                if st["sink"] is not None:
                    done(nc.vector.tensor_tensor(rs[:, c:c + REP], su, esk[:, c:c + REP], ALU.add))
                else:
                    done(nc.vector.tensor_scalar(rs[:, c:c + REP], su, 1e-30, None, ALU.max))
                settle(v)
                done(nc.vector.reciprocal(wgt[:, c:c + REP], rs[:, c:c + REP]))
                if st["gate"] is not None:
                    settle(v)
                    done(nc.vector.tensor_tensor(wgt[:, c:c + REP], wgt[:, c:c + REP], st["gate"], ALU.mult))
                settle(v)
                for r in range(REP):
                    buf = A.sb[n % A.sbn][:, r, 0:st["keys"]]
                    ins = nc.vector.tensor_scalar(buf, buf, wgt[:, c + r:c + r + 1], None, ALU.mult)
                ins.then_inc(A.p, 1)
                A.between_dve(v, n)
            finished(len(A.steps) - 2)
            finished(len(A.steps) - 1)

        def o_view(x):
            return x.rearrange("p (r q) -> p r q", r=REP)

        def fin1_act(act, A, n, g):
            act.wait_ge(A.o, g + 1)
            h, l = A.steps[n]["dst"]
            nc.scalar.activation(h, o_view(ps[0:HD, 6 + g % 2]), ACT.Copy).then_inc(A.oh, 1)

        def fin1_dve(v, A, n, g):
            h, l = A.steps[n]["dst"]
            v.wait_ge(A.oh, g + 1)
            nc.vector.tensor_tensor(l, o_view(ps[0:HD, 6 + g % 2]), h.bitcast(F32), ALU.subtract).then_inc(A.ol, 1)

        def fin2_act(act, A, n, g):
            act.wait_ge(A.oh, g + 1)
            h, l, gg, tmp = A.steps[n]["dst"]
            nc.scalar.activation(h, tmp, ACT.Copy).then_inc(A.k2, 1)

        def fin2_dve(v, A, n, g):
            h, l, gg, tmp = A.steps[n]["dst"]
            v.wait_ge(A.o, g + 1)
            if g:
                v.wait_ge(A.k2, g)
                v.wait_ge(A.ol, g)
            nc.vector.scalar_tensor_tensor(out=tmp, in0=o_view(ps[0:HD, 6 + g % 2]), scalar=0.5, in1=gg,
                                           op0=ALU.mult, op1=ALU.mult).then_inc(A.oh, 1)
            v.wait_ge(A.k2, g + 1)
            nc.vector.tensor_tensor(l, tmp, h.bitcast(F32), ALU.subtract).then_inc(A.ol, 1)

        def steps1():
            out = []
            for g in range(2):
                gs = slice(g * HD, (g + 1) * HD)
                for i in range(QT):
                    qs = slice(i * P, (i + 1) * P)
                    n = (i + 1) * P
                    dst = (o1h[gs, 0:REP, qs], o1l[gs, 0:REP, qs])
                    gcol = lambda b, g=g, i=i: gate[:, i, g * 12 + b:g * 12 + b + 12:3]
                    q = lambda r, gs=gs, qs=qs: q_n[gs, r, qs]
                    for kind in (0, 1):
                        out.append(dict(q=q, k=[(0, k_all[gs, kind, 0:n])], kstart=[True], off=0, keys=n,
                                        bias=lambda r, g=g, n=n: strip_n[:, g * REP + r, S - n:S],
                                        blocks=[(j * P, P) for j in range(i + 1)],
                                        v=[v_all[:, kind, j, gs] for j in range(i + 1)],
                                        first=(kind == 0), last=False, dst=dst, gate=gcol(1 + kind), sink=None,
                                        clamp=False))
                    out.append(dict(q=q, k=[(0, kcmp[gs, 0:NCMP + 1])], kstart=[True], off=0, keys=NCMP,
                                    bias=lambda r, i=i: cmask[:, i, :], blocks=[(0, NCMP)],
                                    v=[vcmp[0:NCMP, g, :]], first=False, last=True, dst=dst, gate=gcol(0), sink=None,
                                    clamp=True))
            for g in range(2):
                gs = slice(g * HD, (g + 1) * HD)
                for i in range(QT):
                    qs = slice(i * P, (i + 1) * P)
                    lo = max(i - 1, 0)
                    n = (i + 1 - lo) * P
                    out.append(dict(q=lambda r, gs=gs, qs=qs: q_s[gs, r, qs],
                                    k=[(0, k_all[gs, 2, lo * P:lo * P + n])], kstart=[True], off=0, keys=n,
                                    bias=lambda r, g=g, n=n: strip_s[:, g * REP + r, 256 - n:256],
                                    blocks=[(j * P, P) for j in range(n // P)],
                                    v=[v_all[:, 2, lo + j, gs] for j in range(n // P)],
                                    first=True, last=True, dst=(o1h[gs, REP:8, qs], o1l[gs, REP:8, qs]), gate=None,
                                    sink=g * REP, clamp=False))
            return out

        def steps2():
            out = []
            for kh in range(4):
                pb = (kh % 2) * HD
                gs = slice(pb, pb + HD)
                kt = kh // 2
                for i in range(QT):
                    qs = slice(i * P, (i + 1) * P)
                    lo, hi = max(i - 1, 0), min(i + 2, QT)
                    n = (hi - lo) * P
                    mask = bm0[:, 0:C + n] if i == 0 else bm1[:, 0:C + n]
                    ts = slice(kt * REP, (kt + 1) * REP)
                    out.append(dict(q=lambda r, gs=gs, qs=qs, kt=kt: b_q[gs, kt * REP + r, qs],
                                    k=[(C, b_k[gs, kt, S:SC]), (S, b_k[gs, kt, lo * P:hi * P])], kstart=[True, True],
                                    off=C, keys=C + n, bias=lambda r, mask=mask: mask,
                                    blocks=[(j * P, P) for j in range(2 + hi - lo)],
                                    v=[b_v[:, QT + j, kh * HD:(kh + 1) * HD] for j in range(2)]
                                    + [b_v[:, j, kh * HD:(kh + 1) * HD] for j in range(lo, hi)],
                                    first=True, last=True,
                                    dst=(x1h[gs, ts, qs], x1l[gs, ts, qs], b_g[gs, ts, qs], o_view(ot[gs, :])),
                                    gate=None, sink=8 + kh * REP, clamp=False))
            return out

        A1 = Attn("at1", steps1(), 4, 512, sb1, pt1, 3, dict(act=fin1_act, dve=fin1_dve))
        A2 = Attn("at2", steps2(), 2, 1024, b_sb, b_pt, 3, dict(act=fin2_act, dve=fin2_dve))
        A2.k2 = sem("at2_hi")

        def gate_tiles(pe, x):
            for y in (2 * x, 2 * x + 1):
                j, k = divmod(y, KT)
                u = U_G + j
                if k == 0:
                    split_ready(pe, u)
                    if j:
                        pe.wait_ge(g_tanh, j)
                mm = products(u, [(ps[:, 5], lambda k: x1h[:, k, :], lambda k: x1l[:, k, :])], k, k + 1,
                              first=(k == 0), last=(k == KT - 1))
                if k == KT - 1:
                    mm.then_inc(unit, 1)

        def gate_out(act, x):
            if x % 4 != 3:
                return
            j = x // 4
            unit_done(act, U_G + j)
            if j >= 3:
                act.wait_ge(g_out[j % 3], 16 * (j // 3))
            nc.scalar.activation(g_stage[:, j % 3, :], ps[:, 5], ACT.Tanh, scale=0.5).then_inc(g_tanh, 1)
            split_high(act, U_G + j + 2)
            act.wait_ge(g_tanh, j + 1)
            act.dma_start(gates[j // 2, :, j % 2, :], g_stage[:, j % 3, :]).then_inc(g_out[j % 3], 16)
        A1.tb = 1
        A1.between_pe, A1.between_act = gate_tiles, gate_out
        mfix[A1] = sem("at1_fix")
        mfix[A2] = sem("at2_fix")

        @block.sync
        def _(sp):
            for dst, name in ((ident[:], "ident"), (gains, "gains"), (bmod, "bmod"), (lamv[0:HD], "lamv"),
                              (subg, "subg"), (w2[:], "w2"), (pos[:], "pos"), (onehot[:], "onehot"),
                              (blhs[0:BUCKETS], "rel_bias"), (blhs[BUCKETS:34], "selrows"), (cmask[:], "cmask")):
                sp.dma_start(dst, t[name]).then_inc(const_in, 16)
            sp.dma_start(sinks, bass.AP(t["sinks"].tensor, 0, [[0, P], [1, 24]])).then_inc(const_in, 16)
            for u in range(RAW):
                load_unit(sp, u, t["w_att"][u])
            sp.wait_ge(brow_ok, 2)
            sp.dma_start(dbias, brow[:].unsqueeze(1).to_broadcast([16, P, TBL])).then_inc(dbias_in, 16)
            sp.wait_ge(dbias_in, 16)
            sp.dma_start(strip_n[:], bass.AP(dbias.tensor, 127, [[TBL - 1, P], [P * TBL, 8], [1, 512]])).then_inc(strips_in, 16)
            sp.dma_start(strip_s[:], bass.AP(dbias.tensor, 8 * P * TBL + 383, [[TBL - 1, P], [P * TBL, 8], [1, 256]])).then_inc(strips_in, 16)
            for u in range(RAW, N_ATT):
                load_unit(sp, u, t["w_att"][u])
            with sp.Fori(0, 4) as i:
                for j in range(4):
                    load_unit(sp, U_G + j, t["w_g"][bass.ds(i * 4 + j, 1)].rearrange("o p k m -> p (o k) m"), i, 4)
            for j in range(RAW):
                load_unit(sp, U_UP + j, t["w_up"][j])
            begin_after(sp, "nsa")
            for i in range(3):
                sp.wait_ge(g_out[i], 16 * len(range(i, N_G, 3)))
            sp.dma_start(tg_parts[0][:, 0:2], gates[0:2].rearrange("m p h s -> p m h s")).then_inc(gate_in[0], 16)
            sp.dma_start(tg_parts[0][:, 2:4], gates[2:4].rearrange("m p h s -> p m h s")).then_inc(gate_in[1], 16)
            for i in (1, 2):
                sp.dma_start(tg_parts[i][:], gates[2 * i + 2:2 * i + 4].rearrange("m p h s -> p m h s")).then_inc(gate_in[1], 16)
            for j in range(RAW, N_UP):
                load_unit(sp, U_UP + j, t["w_up"][j])
            sp.dma_start(hc[:, :, 0:S], t["xT"]).then_inc(x_in[0], 16)
            sp.dma_start(hc[:, :, S:SC], t["ctxT"]).then_inc(ctx_in, 16)
            with sp.Fori(0, 2) as i:
                for j in range(4):
                    load_unit(sp, U_OUT + j, t["w_out"][bass.ds(i * 4 + j, 1)].rearrange("o p k m -> p (o k) m"), i, 4)
            with sp.Fori(0, 4) as i:
                for j in range(16):
                    load_unit(sp, U_MLP + j, t["w_mlp"][bass.ds(i * 16 + j, 1)].rearrange("o p k m -> p (o k) m"), i, 16)
            with sp.Fori(0, 8) as i:
                for j in range(4):
                    load_unit(sp, U_A + j, t["w_a"][bass.ds(i * 4 + j, 1)].rearrange("o p k m -> p (o k) m"), i, 4)
            with sp.Fori(0, 2) as i:
                for j in range(4):
                    load_unit(sp, U_AO + j, t["w_ao"][bass.ds(i * 4 + j, 1)].rearrange("o p k m -> p (o k) m"), i, 4)
            with sp.Fori(0, 5) as i:
                for j in range(4):
                    load_unit(sp, U_B + j, t["w_b"][bass.ds(i * 4 + j, 1)].rearrange("o p k m -> p (o k) m"), i, 4)
            with sp.Fori(0, 2) as i:
                for j in range(4):
                    load_unit(sp, U_BO + j, t["w_bo"][bass.ds(i * 4 + j, 1)].rearrange("o p k m -> p (o k) m"), i, 4)
            for k in range(KT):
                nm5.wait(sp, "t", k + 1)
                sp.dma_start(out[:, k], xo[:, k]).then_inc(out_done, 16)
            sp.wait_ge(out_done, 16 * KT)

        @block.gpsimd
        def _(g):
            def low(u, i=None):
                g.wait_ge(w_hi, u + 1 if i is None else i * 4 + (u + 1))
                nc.gpsimd.tensor_tensor(w_l[:, u % SPL], raw[:, u % RAW], w_h[:, u % SPL].bitcast(F32),
                                        ALU.subtract).then_inc(w_lo, 1)
            head = U_END % 4
            for u in range(head):
                low(u)
            with g.Fori(0, (U_END - head) // 4) as i:
                for j in range(4):
                    low(head + j, i)

        CONSTS = 16 * 12

        @block.tensor
        def _(pe):
            pe.wait_ge(const_in, CONSTS)
            pe.wait_ge(boot, 1)
            nc.tensor.matmul(ps[0:16, 6, :], blhs[:], onehot[:, 0:512], start=True, stop=True)
            nc.tensor.matmul(ps[0:16, 7, 0:128], blhs[:], onehot[:, 512:640], start=True, stop=True)
            pe.wait_ge(boot, 3)
            nc.tensor.matmul(ps[:, 5, 0:2], ones[0:HD, :], lamp[0:HD, :], start=True, stop=True).then_inc(cvec, 1)
            sum_features(pe, nm1, S, 4)
            plain = [(lambda k: x1h[:, k, :], lambda k: x1l[:, k, :])]
            r = 0
            for u in range(N_ATT):
                cmp_u = 2 <= u < 10
                first = not (cmp_u and u % 2 == 1)
                split_ready(pe, u)
                if first and r >= 2:
                    pe.wait_ge(res_free, r - 1)
                if not cmp_u:
                    if u == 0:
                        for k in range(KT):
                            nm1.wait(pe, "lo", k + 1)
                            mm = products(u, [(ps[:, 0], lambda k: x1h[:, k, :], lambda k: x1l[:, k, :])], k, k + 1,
                                          first=(k == 0), last=(k == KT - 1))
                    else:
                        mm = products(u, [(ps[:, r % 2], lambda k: x1h[:, k, :], lambda k: x1l[:, k, :])])
                    r += 1
                else:
                    kv = (u - 2) // 4
                    kk = u % 2
                    pe.wait_ge(f_lo, kv + 1)

                    def fr(f, kv=kv, kk=kk):
                        return lambda k: bass.AP(f, kv * FW + kk * 8 + k, [[2 * FW, P], [256, 3], [8, 32]])
                    mm = products(u, [(ps[:, r % 2, 0:96], fr(fh), fr(fl))], first=(kk == 0), last=(kk == 1))
                    if kk == 1:
                        r += 1
                mm.then_inc(unit, 1)
            pe.wait_ge(gel, 1)
            glv = gl3[:, :, :].rearrange("p c (g n) -> p c g n", g=2)
            for g in range(2):
                for mt in range(2):
                    nc.tensor.matmul(ps[g * HD:(g + 1) * HD, 2, 0:NCMP], w2[:, 0, mt, :], glv[:, mt, g, :],
                                     start=(mt == 0), stop=(mt == 1))
            for g in range(2):
                for mt in range(2):
                    mm = nc.tensor.matmul(ps[0:NCMP, 3, g * HD:(g + 1) * HD], glv[:, 2 + mt, g, :], w2[:, 1, mt, :],
                                          start=(mt == 0), stop=(mt == 1))
            mm.then_inc(pr_mm, 1)
            pe.wait_ge(res_free, 21)
            for n in range(4):
                for tt in range(QT):
                    mm = nc.tensor.transpose(ps[:, 4 + n, tt * P:(tt + 1) * P], vT[:, n, tt * P:(tt + 1) * P], ident[:])
                mm.then_inc(pr_mm, 1)
            end_phase(pe, "prep")
            begin_after(pe, "prep")
            attn_pe(pe, A1)
            for x in range(A1.blk[-1], N_G * KT // 2):
                gate_tiles(pe, x)
            end_phase(pe, "nsa")
            begin_after(pe, "nsa")
            for m in range(N_UP):
                b = 2 * (m % 2)
                if m >= 2:
                    pe.wait_ge(up_free, m - 1)
                split_ready(pe, U_UP + m)
                products(U_UP + m, [(ps[:, b], lambda k: o1h[:, k, :], lambda k: o1l[:, k, :])], 0, 4)
                products(U_UP + m, [(ps[:, b + 1], lambda k: o1h[:, k, :], lambda k: o1l[:, k, :])], 4, 8).then_inc(unit, 1)
            end_phase(pe, "up")
            begin_after(pe, "up")

            def out_products(n, u0, yh, yl, wide):
                with pe.Fori(0, 2) as i:
                    for j in range(4):
                        split_ready(pe, u0 + j, i, 4)
                        pe.wait_ge(wo_free[n], i * 4 + (j + 1))
                        if wide:
                            parts = [(ps[:, 2 * (j % 2)], lambda k: yh[:, k, 0:S], lambda k: yl[:, k, 0:S]),
                                     (ps[:, 2 * (j % 2) + 1, 0:C], lambda k: yh[:, k, S:SC], lambda k: yl[:, k, S:SC])]
                        else:
                            parts = [(ps[:, j % 2], lambda k: yh[:, k, :], lambda k: yl[:, k, :])]
                        if n == 1 and j == 0:
                            for k in range(KT):
                                pe.wait_ge(ha["lo"], k + 1)
                                mm = products(u0, parts, k, k + 1, first=(k == 0), last=(k == KT - 1))
                            mm.then_inc(unit, 1)
                        else:
                            products(u0 + j, parts).then_inc(unit, 1)
            out_products(0, U_OUT, y1h, y1l, False)
            sum_features(pe, nm2a, S, 4, KT + 2)
            end_phase(pe, "wout")
            begin_after(pe, "wout")
            sum_features(pe, nm2b, S, 6)
            end_phase(pe, "norm2")
            with pe.Fori(0, 4) as i:
                for j in range(16):
                    u = U_MLP + j
                    split_ready(pe, u, i, 16)
                    pe.wait_ge(ml_f, i * 16 + (j + 1))
                    if j == 0:
                        for k in range(KT):
                            nm2b.wait(pe, "lo", k + 1)
                            mm = products(u, [(ps[:, 0], lambda k: x1h[:, k, :], lambda k: x1l[:, k, :])], k, k + 1,
                                          first=(k == 0), last=(k == KT - 1))
                    elif j < 8:
                        mm = products(u, [(ps[:, j % 4], lambda k: x1h[:, k, :], lambda k: x1l[:, k, :])])
                    else:
                        if j == 8:
                            pe.wait_ge(ml_lo, i * 8 + 7)
                            products(u, [(ps[:, j % 4], lambda k: m_h[:, k, :], lambda k: m_l[:, k, :])], 0, 7, last=False)
                            pe.wait_ge(ml_lo, i * 8 + 8)
                            mm = products(u, [(ps[:, j % 4], lambda k: m_h[:, k, :], lambda k: m_l[:, k, :])], 7, 8, first=False)
                        else:
                            mm = products(u, [(ps[:, j % 4], lambda k: m_h[:, k, :], lambda k: m_l[:, k, :])])
                    mm.then_inc(unit, 1)
            sum_features(pe, nm3a, S, 4)
            end_phase(pe, "mlp")
            begin_after(pe, "mlp")
            sum_features(pe, nm3b, SC, 6)
            end_phase(pe, "norm3")
            def project(head, pos, n):
                i, c = head
                for x in range(pos, pos + n):
                    j, k = divmod(x, KT)
                    u = U_A + 4 * c + j
                    if k == 0:
                        split_ready(pe, u, i, 8)
                        wait_head(pe, "gqkv"[j], head, 1, 1 if j else 0)
                    if i is None and c == 0 and j == 0:
                        nm3b.wait(pe, "lo", k + 1)
                    mm = products(u, [(ps[:, 0], lambda k: x2h[:, k, 0:S], lambda k: x2l[:, k, 0:S]),
                                      (ps[:, 1, 0:C], lambda k: x2h[:, k, S:SC], lambda k: x2l[:, k, S:SC])],
                                  k, k + 1, first=(k == 0), last=(k == KT - 1))
                    if k == KT - 1:
                        mm.then_inc(unit, 1)

            def attend(head, more):
                i, c = head
                pos = [0]
                aq, ak = a_q[c % 2], a_k[c % 2]

                def dense(n):
                    if more:
                        project((i, c + 1), pos[0], n)
                        pos[0] += n

                def score(qt, m):
                    wait_head(pe, "m", head, 12, 2 * qt + m)
                    ms = slice(m * HD, (m + 1) * HD)
                    q = aq[ms, qt * P:(qt + 1) * P]
                    if qt < QT:
                        nc.tensor.matmul(ps[:, 2], q, ak[ms, 0:S], start=True, stop=True)
                        mm = nc.tensor.matmul(ps[:, 3, 0:C], q, ak[ms, S:SC], start=True, stop=True)
                    else:
                        mm = nc.tensor.matmul(ps[:, 2, 0:C], q, ak[ms, S:SC], start=True, stop=True)
                    mm.then_inc(ha["s"], 1)

                def turns(qt):
                    wait_head(pe, "a", head, 6, qt + 1)
                    if qt == 0:
                        wait_head(pe, "ve", head, 1, 1)
                    else:
                        wait_head(pe, "te", head, 6, qt)
                    for b in range(6 if qt < QT else 2):
                        mm = nc.tensor.transpose(ps[:, 4 + b // 4, (b % 4) * P:(b % 4 + 1) * P],
                                                 a_p[qt % 3][0][:, b * P:(b + 1) * P], ident[:])
                    mm.then_inc(ha["t"], 1)

                wait_head(pe, "ro", head, 2, 2)
                score(0, 0)
                dense(2)
                score(0, 1)
                dense(2)
                wait_head(pe, "v", head, 1, 1)
                wait_head(pe, "ln", head, 1, 0)
                for b in range(6):
                    mm = nc.tensor.transpose(ps[:, 4 + b // 4, (b % 4) * P:(b % 4 + 1) * P], a_vT[:, b * P:(b + 1) * P], ident[:])
                mm.then_inc(ha["vt"], 1)
                score(1, 0)
                dense(2)
                score(1, 1)
                dense(2)
                for qt, (n0, n1, n2) in enumerate(((1, 1, 1), (1, 1, 2), (1, 0, 2), (1, 1, 1))):
                    score(qt + 2, 0)
                    dense(n0)
                    score(qt + 2, 1)
                    dense(n1)
                    turns(qt)
                    dense(n2)
                turns(4)
                dense(1)
                wait_head(pe, "on", head, 1, 0)
                wait_head(pe, "te", head, 6, 4)
                for b in range(6):
                    mm = nc.tensor.matmul(ps[:, 6], a_v[:, b, :], a_pt[:, b, :], start=(b == 0), stop=(b == 5))
                dense(2)
                turns(5)
                dense(2)
                wait_head(pe, "te", head, 6, 6)
                for b in range(2):
                    mm = nc.tensor.matmul(ps[:, 7, 0:C], a_v[:, 4 + b, :], a_pt2[:, b, :], start=(b == 0), stop=(b == 1))
                mm.then_inc(ha["pv"], 1)
                dense(6)
                wait_head(pe, "sq", head, 1, 1)
                nc.tensor.matmul(ps[:, 4], ones[:], a_sq[:, 0:S], start=True, stop=True)
                nc.tensor.matmul(ps[:, 5, 0:C], ones[:], a_sq[:, S:SC], start=True, stop=True).then_inc(ha["st"], 1)

            project((None, 0), 0, 4 * KT)
            all_heads(pe, attend)
            end_phase(pe, "heads")
            begin_after(pe, "heads")
            out_products(1, U_AO, x2h, x2l, True)
            end_phase(pe, "ao")
            begin_after(pe, "ao")
            sum_features(pe, nm4, SC, 6)
            end_phase(pe, "norm4")
            for u in range(N_B):
                split_ready(pe, U_B + u)
                if u >= 2:
                    pe.wait_ge(hb["free"], u - 1)
                parts = [(ps[:, 2 * (u % 2)], lambda k: x2h[:, k, 0:S], lambda k: x2l[:, k, 0:S])]
                if 8 <= u < 12:
                    parts.append((ps[:, 2 * (u % 2) + 1, 0:C], lambda k: x2h[:, k, S:SC], lambda k: x2l[:, k, S:SC]))
                if u == 0:
                    for k in range(KT):
                        nm4.wait(pe, "lo", k + 1)
                        mm = products(U_B, parts, k, k + 1, first=(k == 0), last=(k == KT - 1))
                    mm.then_inc(unit, 1)
                else:
                    products(U_B + u, parts).then_inc(unit, 1)
                if u == 13:
                    for n in range(2):
                        if n:
                            pe.wait_ge(hb["ve"], 1)
                        for b in range(6):
                            mm = nc.tensor.transpose(ps[:, 4 + b // 4, (b % 4) * P:(b % 4 + 1) * P],
                                                     b_vT[:, n, b * P:(b + 1) * P], ident[:])
                        mm.then_inc(hb["vt"], 1)
            end_phase(pe, "bqkv")
            begin_after(pe, "bqkv")
            attn_pe(pe, A2)
            end_phase(pe, "battn")
            begin_after(pe, "battn")
            out_products(2, U_BO, x1h, x1l, False)
            sum_features(pe, nm5, S, 4)

        @block.scalar
        def _(act):
            for h in range(2):
                hs = slice(h * KT // 2, (h + 1) * KT // 2)
                act.dma_start(xin[:, hs], t["xT"][:, hs]).then_inc(x_in[h], 16)
            for k in range(KT):
                if k % (KT // 2) == 0:
                    act.wait_ge(x_in[k // (KT // 2)], 16)
                square_tile(act, nm1, k, xin[:, k, :], S)
            split_high(act, 0)
            act.wait_ge(const_in, CONSTS)
            act.wait_ge(boot, 4)
            nc.scalar.activation(lame, lame, ACT.Exp).then_inc(cvec, 1)
            make_rstd(act, nm1, S, 4)
            for k in range(KT):
                nm1.wait(act, "t", k + 1)
                nc.scalar.activation(x1h[:, k, :], xn[:, k % 2, 0:S], ACT.Copy).then_inc(nm1.hi, 1)
                if k == 2:
                    split_high(act, 1)
            r = 0
            for u in range(N_ATT):
                unit_done(act, u)
                split_high(act, u + 2)
                if u in (0, 1):
                    if u == 0:
                        nm1.wait(act, "lo", KT)
                    for g in range(2):
                        for op in range(2):
                            src = ps[g * HD:(g + 1) * HD, u % 2].rearrange("p (t o) -> p t o", o=2)[:, :, op]
                            ins = nc.scalar.activation(fh[op * HD:(op + 1) * HD, u, g * 256:(g + 1) * 256], src, ACT.Copy)
                            ins.then_inc(f_hi, 1)
                    nc.scalar.activation(fh[:, u, 512:520 + 0], pos[:, u, 0:8], ACT.Copy).then_inc(f_hi, 1)
                    nc.scalar.activation(fh[:, u, 520:528], pos[:, u, 8:16], ACT.Copy).then_inc(f_hi, 1)
                if u == 10:
                    act.wait_ge(gel_t, 1)
                    nc.scalar.activation(gl2[:], gl1[:], ACT.Tanh, scale=GELU_C).then_inc(th_a, 1)
                if u == 18:
                    nc.scalar.activation(vT[:, 3, :], ps[:, 0], ACT.Tanh, scale=0.5).then_inc(th_a, 1)
            end_phase(act, "prep")
            begin_after(act, "prep")
            act.wait_ge(strips_in, 32)
            attn_act(act, A1)
            gate_out(act, 4 * N_G - 1)
            end_phase(act, "nsa")
            begin_after(act, "nsa")
            for m in range(N_UP):
                unit_done(act, U_UP + m)
                split_high(act, U_UP + m + 2)
                act.wait_ge(up_y, m + 1)
                nc.scalar.activation(y1h[:, m, :], ty[:, m % 2, :], ACT.Copy).then_inc(up_hi, 1)
            end_phase(act, "up")
            begin_after(act, "up")
            act.dma_start(crow[:].rearrange("p v k -> p (v k)"), bass.AP(t["crow"].tensor, 0, [[0, P], [1, 2 * D]])
                          ).then_inc(crow_in, 16)
            with act.Fori(0, 2) as i:
                for j in range(4):
                    unit_done(act, U_OUT + j, i, 4)
                    split_high(act, U_OUT + j + 2, i, 4)
                    nc.scalar.activation(f_t[:, bass.ds(i * 4 + j, 1), :].rearrange("p a s -> p (a s)"), ps[:, j % 2],
                                         ACT.Copy).then_inc(wo_f[0], 1)
                    nm2a.wait(act, "add", i * 4 + (j + 1))
                    nc.scalar.activation(sq[:, j % 2, 0:S], ps[:, j % 2], ACT.Square).then_inc(wo_free[0], 1)
            make_rstd(act, nm2a, S, 4)
            end_phase(act, "wout")
            begin_after(act, "wout")
            for c in range(MRAW - 1):
                act.dma_start(mraw[:, c], t["w_mod"][c].rearrange("p (k m) -> p k m", k=KT)).then_inc(mod_in[c], 16)
            act.wait_ge(crow_in, 16)
            nc.scalar.activation(ctanh[:], crow[:], ACT.Tanh, scale=0.5).then_inc(c_tanh, 1)
            for k in range(KT):
                nm2b.wait(act, "src", k + 1)
                square_tile(act, nm2b, k, hc[:, k, 0:S], S)
            make_rstd(act, nm2b, S, 6)
            for k in range(KT):
                nm2b.wait(act, "t", k + 1)
                nc.scalar.activation(x1h[:, k, :], xn2[:, k % 2, 0:S], ACT.Copy).then_inc(nm2b.hi, 1)
            end_phase(act, "norm2")
            begin_after(act, "norm2")
            act.wait_ge(mod_ev, 1)
            with act.Fori(0, 4) as i:
                for j in range(16):
                    unit_done(act, U_MLP + j, i, 16)
                    split_high(act, U_MLP + j + 2, i, 16)
                    if j < 8:
                        nc.scalar.activation(relu[:, j % 2, :], ps[:, j % 4], ACT.Relu).then_inc(ml_relu, 1)
                        act.wait_ge(ml_sq, i * 8 + (j + 1))
                        nc.scalar.activation(m_h[:, j, :], msq[:, j % 2, :], ACT.Copy).then_inc(ml_hi, 1)
                    if j % 4 != 3:
                        c = j // 4 * 3 + j % 4 + MRAW - 1
                        act.wait_ge(mod_mul, i * 24 + 2 * (c - MRAW + 1) + 2)
                        act.dma_start(mraw[:, c % MRAW], t["w_mod"][bass.ds(i * 12 + c, 1)].rearrange("o p (k m) -> p (o k) m", k=KT)
                                      ).then_inc(mod_in[c % MRAW], 16)
            for c in range(MRAW - 1):
                act.wait_ge(mod_in[c], 16 * (N_MOD // MRAW + 1))
            for k in range(KT):
                square_tile(act, nm3a, k, f_t[:, k, :], S)
            make_rstd(act, nm3a, S, 4)
            end_phase(act, "mlp")
            begin_after(act, "mlp")
            for k in range(KT):
                nm3b.wait(act, "src", k + 1)
                square_tile(act, nm3b, k, hc[:, k, :], SC)
            make_rstd(act, nm3b, SC, 6)

            def shifted(nm, l):
                for k in range(KT):
                    nm.wait(act, "t", k + 1)
                    for w, a, b in ((0, 0, S), (1, S, SC)):
                        ins = nc.scalar.activation(x2h[:, k, a:b], xn2[:, k % 2, a:b], ACT.Identity,
                                                   bias=mod[:, l * 24 + k, w:w + 1])
                    ins.then_inc(nm.hi, 1)
            shifted(nm3b, 0)
            end_phase(act, "norm3")
            begin_after(act, "norm3")
            act.dma_start(cos_t[:], t["cos"]).then_inc(tab_in, 16)
            act.dma_start(sin_t[:], t["sin"]).then_inc(tab_in, 16)
            def take(head, j, ahead):
                i, c = head
                unit_done(act, U_A + 4 * c + j, i, 8)
                src = pair(0)[:, 0:SC]
                if j == 0:
                    nc.scalar.activation(a_q[c % 2][:], src, ACT.Copy, scale=-0.125).then_inc(ha["q"], 1)
                elif j == 1:
                    nc.scalar.activation(a_k[c % 2][:], src, ACT.Copy).then_inc(ha["k"], 1)
                elif j == 2:
                    nc.scalar.activation(a_vT[:], src, ACT.Copy).then_inc(ha["v"], 1)
                else:
                    nc.scalar.activation(a_g[c % 2][:], src, ACT.Tanh, scale=0.5).then_inc(ha["gt"], 1)
                if ahead:
                    split_high(act, U_A + 4 * c + j + 2, i, 8)

            def attend(head, more):
                i, c = head

                def exps(qt, m):
                    n = SC if qt < QT else C
                    cc = 2 * (qt % 3) + m
                    wait_head(act, "m", head, 12, 2 * qt + m + 1)
                    buf = a_p[qt % 3][m][:, 0:n]
                    nc.scalar.activation(buf, buf, ACT.Exp, bias=negm[:, cc:cc + 1], scale=-1.0,
                                         accum_out=sums[:, cc:cc + 1]).then_inc(ha["e"], 1)

                def turned(qt):
                    wait_head(act, "t", head, 6, qt + 1)
                    if qt < QT:
                        nc.scalar.activation(a_pt[:, :, qt * P:(qt + 1) * P],
                                             pair(2)[:, 0:SC].rearrange("p (b q) -> p b q", b=6), ACT.Copy).then_inc(ha["te"], 1)
                    else:
                        nc.scalar.activation(a_pt2[:, :, (qt - QT) * P:(qt - QT + 1) * P],
                                             pair(2)[:, 0:C].rearrange("p (b q) -> p b q", b=2), ACT.Copy).then_inc(ha["te"], 1)
                exps(0, 0)
                exps(0, 1)
                wait_head(act, "vt", head, 1, 1)
                nc.scalar.activation(a_v[:].rearrange("p b e -> p (b e)"), pair(2)[:, 0:SC], ACT.Copy).then_inc(ha["ve"], 1)
                exps(1, 0)
                exps(1, 1)
                if more:
                    take((i, c + 1), 0, True)
                for qt in range(6):
                    if qt < 4:
                        exps(qt + 2, 0)
                        if qt == 2 and more:
                            take((i, c + 1), 1, True)
                        exps(qt + 2, 1)
                    if qt == 5 and more:
                        take((i, c + 1), 2, True)
                    turned(qt)
                wait_head(act, "pv", head, 1, 1)
                wait_head(act, "on", head, 1, 0)
                nc.scalar.activation(a_sq[:], pair(3)[:, 0:SC], ACT.Square).then_inc(ha["sq"], 1)
                if more:
                    take((i, c + 1), 3, True)
                wait_head(act, "st", head, 1, 1)
                nc.scalar.activation(rstd[:], pair(2)[:, 0:SC], ACT.Ln, bias=seps_t[:], scale=1.0 / P).then_inc(ha["ln"], 1)
                wait_head(act, "ln", head, 1, 1)
                nc.scalar.activation(rstd[:], rstd[:], ACT.Exp, scale=-0.5).then_inc(ha["r"], 1)

            for j in range(4):
                take((None, 0), j, True)
            all_heads(act, attend)
            end_phase(act, "heads")
            begin_after(act, "heads")
            for k in range(KT):
                nc.scalar.activation(x2h[:, k, :], o2[:, k, :], ACT.Copy).then_inc(ha["hi"], 1)
            for j in range(N_OUT):
                unit_done(act, U_AO + j)
                split_high(act, U_AO + j + 2)
                act.wait_ge(wo_free[1], 2 + j + 1)
                square_tile(act, nm4, j, hc[:, j, :], SC)
            end_phase(act, "ao")
            begin_after(act, "ao")
            make_rstd(act, nm4, SC, 6)
            shifted(nm4, 1)
            end_phase(act, "norm4")
            begin_after(act, "norm4")
            act.dma_start(bm0[:], t["bm0"]).then_inc(tab_in, 16)
            act.dma_start(bm1[:], t["bm1"]).then_inc(tab_in, 16)
            for u in range(N_B):
                unit_done(act, U_B + u)
                split_high(act, U_B + u + 2)
                b = u % 2
                if u < 8:
                    nc.scalar.activation(b_q[:, u, :], ps[:, 2 * b], ACT.Copy, scale=-0.125).then_inc(hb["free"], 1)
                elif u < 10:
                    nc.scalar.activation(b_k[:, u - 8, :], pair(b)[:, 0:SC], ACT.Copy).then_inc(hb["free"], 1)
                elif u < 12:
                    nc.scalar.activation(b_vT[:, u - 10, :], pair(b)[:, 0:SC], ACT.Copy).then_inc(hb["free"], 1)
                else:
                    nc.scalar.activation(b_g[:, u - 12, :], ps[:, 2 * b], ACT.Tanh, scale=0.5).then_inc(hb["gt"], 1)
                    if u == 14:
                        pass
            end_phase(act, "bqkv")
            begin_after(act, "bqkv")
            attn_act(act, A2)
            end_phase(act, "battn")
            begin_after(act, "battn")
            for j in range(N_OUT):
                if j < N_OUT - 2:
                    unit_done(act, U_BO + j)
                    split_high(act, U_BO + j + 2)
                act.wait_ge(wo_free[2], 2 + j + 1)
                square_tile(act, nm5, j, hc[:, j, 0:S], S)
            make_rstd(act, nm5, S, 4)

        @block.vector
        def _(v):
            nc.vector.memset(ones[:], 1.0)
            nc.vector.memset(eps_t, EPS)
            nc.vector.memset(seps_t, SUB_EPS)
            nc.vector.memset(zero, 0.0)
            nc.vector.memset(fh[:].bitcast(F32), 0.0)
            nc.vector.memset(fl[:].bitcast(F32), 0.0)
            nc.vector.memset(kcmp[:], 0.0).then_inc(boot, 1)
            for k in range(KT // 2):
                add_square(v, nm1, k, S)
            v.wait_ge(const_in, CONSTS)
            done(nc.vector.tensor_scalar(nsinks, sinks, -1.0, None, ALU.mult))
            done(nc.vector.tensor_scalar(subs, subg, 0.5 * (1.0 - LAM_INIT), None, ALU.mult))
            lv = lamv[0:HD].rearrange("p (a b) -> p a b", b=2)
            nc.vector.tensor_tensor(lamp[0:HD], lv[:, :, 0], lv[:, :, 1], ALU.mult).then_inc(boot, 2)
            for k in range(KT // 2, KT):
                add_square(v, nm1, k, S)
            v.wait_ge(cvec, 1)
            nc.vector.tensor_copy(brow[:, 0:512], ps[0:16, 6, :]).then_inc(brow_ok, 1)
            nc.vector.tensor_copy(brow[:, 512:640], ps[0:16, 7, 0:128]).then_inc(brow_ok, 1)
            nc.vector.tensor_copy(lame, ps[:, 5, 0:2]).then_inc(boot, 1)
            v.wait_ge(cvec, 2)
            done(nc.vector.tensor_scalar(lam, lame[:, 0:1], lame[:, 1:2], LAM_INIT, ALU.subtract, ALU.add))

            def normed(nm, k, src, gain, dst_t, n):
                if k >= 2:
                    nm.wait(v, "lo", k - 1)
                nc.vector.scalar_tensor_tensor(out=dst_t(k), in0=src, scalar=gain, in1=rstd[:, 0:n],
                                               op0=ALU.mult, op1=ALU.mult).then_inc(nm.t, 1)

            def lowed(nm, k, dst_t, lo_dst, hi_src):
                nm.wait(v, "hi", k + 1)
                nc.vector.tensor_tensor(lo_dst(k), dst_t(k), hi_src(k).bitcast(F32), ALU.subtract).then_inc(nm.lo, 1)

            def norm_tiles(nm, src, gain, dst_t, lo_dst, hi_src, n):
                nm.wait(v, "r", 1)
                for k in range(KT):
                    normed(nm, k, src(k), gain(k), dst_t, n)
                    if k:
                        lowed(nm, k - 1, dst_t, lo_dst, hi_src)
                lowed(nm, KT - 1, dst_t, lo_dst, hi_src)

            norm_tiles(nm1, lambda k: xin[:, k, :], lambda k: gains[:, G_MIX_PRE, k:k + 1], lambda k: xn[:, k % 2, 0:S],
                       lambda k: x1l[:, k, :], lambda k: x1h[:, k, :], S)
            r = 0
            for u in range(N_ATT):
                if 2 <= u < 10:
                    if u % 2 == 1:
                        unit_done(v, u)
                        c = (u - 2) // 2
                        done(nc.vector.tensor_copy(hbias[:, c:c + 1], ps[:, r % 2, 64:65]))
                        settle(v)
                        src = ps[:, r % 2, 0:64].rearrange("p (g n) -> p g n", g=2)[:, :, 0:NCMP]
                        nc.vector.tensor_scalar(hid[:, c, :].rearrange("p (g n) -> p g n", g=2), src, hbias[:, c:c + 1], None,
                                                ALU.add).then_inc(res_free, 1)
                        r += 1
                    if u == 9:
                        v.wait_ge(res_free, 6)
                        done(nc.vector.tensor_tensor(gl1[:], hid[:], hid[:], ALU.mult))
                        settle(v)
                        done(nc.vector.tensor_scalar(gl1[:], gl1[:], 0.044715, 1.0, ALU.mult, ALU.add))
                        settle(v)
                        nc.vector.tensor_tensor(gl1[:], gl1[:], hid[:], ALU.mult).then_inc(gel_t, 1)
                    continue
                if u in (0, 1):
                    for g in range(2):
                        for op in range(2):
                            v.wait_ge(f_hi, 6 * u + 4)
                            src = ps[g * HD:(g + 1) * HD, u % 2].rearrange("p (t o) -> p t o", o=2)[:, :, op]
                            dsl = (slice(op * HD, (op + 1) * HD), u, slice(g * 256, (g + 1) * 256))
                            ins = nc.vector.tensor_tensor(fl[dsl], src, fh[dsl].bitcast(F32), ALU.subtract)
                    ins.then_inc(res_free, 1)
                    v.wait_ge(f_hi, 6 * u + 6)
                    for a, b in ((0, 8), (8, 16)):
                        ins = nc.vector.tensor_tensor(fl[:, u, 512 + a:512 + b], pos[:, u, a:b],
                                                      fh[:, u, 512 + a:512 + b].bitcast(F32), ALU.subtract)
                    ins.then_inc(f_lo, 1)
                elif u < 14:
                    unit_done(v, u)
                    nc.vector.tensor_scalar(q_n[:, u - 10, :], ps[:, r % 2], -0.125, None, ALU.mult).then_inc(res_free, 1)
                elif u < 16:
                    unit_done(v, u)
                    nc.vector.tensor_copy(k_all[:, u - 14, :], ps[:, r % 2]).then_inc(res_free, 1)
                elif u < 18:
                    unit_done(v, u)
                    nc.vector.tensor_copy(vT[:, u - 16, :], ps[:, r % 2]).then_inc(res_free, 1)
                elif u == 18:
                    v.wait_ge(th_a, 2)
                    done(nc.vector.tensor_scalar(hbias[:, 0:1], lam, 1.0, None, ALU.mult))
                    settle(v)
                    nc.vector.tensor_copy(hbias[:, 1:2], hbias[:, 0:1]).then_inc(res_free, 1)
                elif u < 23:
                    unit_done(v, u)
                    nc.vector.tensor_scalar(q_s[:, u - 19, :], ps[:, r % 2], -0.125, None, ALU.mult).then_inc(res_free, 1)
                elif u == 23:
                    unit_done(v, u)
                    nc.vector.tensor_copy(k_all[:, 2, :], ps[:, r % 2]).then_inc(res_free, 1)
                else:
                    unit_done(v, u)
                    nc.vector.tensor_copy(vT[:, 2, :], ps[:, r % 2]).then_inc(res_free, 1)
                r += 1
                if u == 10:
                    v.wait_ge(th_a, 1)
                    done(nc.vector.scalar_tensor_tensor(out=gl3[:], in0=gl2[:], scalar=1.0, in1=hid[:], op0=ALU.add,
                                                        op1=ALU.mult))
                    settle(v)
                    nc.vector.tensor_scalar(gl3[:], gl3[:], 0.5, None, ALU.mult).then_inc(gel, 1)
            v.wait_ge(pr_mm, 1)
            nc.vector.tensor_copy(kcmp[:, 0:NCMP], ps[:, 2, 0:NCMP])
            nc.vector.tensor_copy(vcmp[0:NCMP].rearrange("p g d -> p (g d)"), ps[0:NCMP, 3, 0:P])
            for n in range(4):
                v.wait_ge(pr_mm, n + 2)
                if n < 3:
                    nc.vector.tensor_copy(v_all[:, n].rearrange("p t d -> p (t d)"), ps[:, 4 + n])
                else:
                    nc.vector.tensor_scalar(gate[:].rearrange("p t d -> p (t d)"), ps[:, 4 + n], 0.5, 0.5, ALU.mult, ALU.add)
            end_phase(v, "prep")
            begin_after(v, "prep")
            v.wait_ge(strips_in, 32)
            attn_dve(v, A1)
            end_phase(v, "nsa")
            begin_after(v, "nsa")
            for m in range(N_UP):
                b = m % 2
                if m == 0:
                    v.wait_ge(gate_in[0], 16)
                if m == 2:
                    v.wait_ge(gate_in[1], 48)
                unit_done(v, U_UP + m)
                for h in range(2):
                    ins = nc.vector.scalar_tensor_tensor(out=tg[m][:, h, :], in0=tg[m][:, h, :], scalar=1.0,
                                                         in1=ps[:, 2 * b + h], op0=ALU.add, op1=ALU.mult)
                    ins.then_inc(up_v, 1)
                v.wait_ge(up_v, 3 * m + 2)
                nc.vector.tensor_tensor(tg[m][:, 0, :], tg[m][:, 0, :], tg[m][:, 1, :], ALU.add).then_inc(up_v, 1)
                v.wait_ge(up_v, 3 * m + 3)
                nc.vector.tensor_scalar(ty[:, b, :], tg[m][:, 0, :], 0.5, None, ALU.mult).then_inc(up_y, 1)
                v.wait_ge(up_hi, m + 1)
                nc.vector.tensor_tensor(y1l[:, m, :], ty[:, b, :], y1h[:, m, :].bitcast(F32), ALU.subtract).then_inc(up_free, 1)
            end_phase(v, "up")
            begin_after(v, "up")
            nc.vector.memset(sqsum[:, 0:S], 0.0).then_inc(nm2a.add, 2)
            nm2a.wait(v, "add", 2)
            v.drain().then_inc(wo_free[0], 2)
            with v.Fori(0, 2) as i:
                for j in range(4):
                    v.wait_ge(wo_free[0], i * 4 + (j + 3))
                    nm2a.wait(v, "add", i * 4 + (j + 2))
                    nc.vector.tensor_tensor(sqsum[:, 0:S], sqsum[:, 0:S], sq[:, j % 2, 0:S], ALU.add).then_inc(nm2a.add, 1)
            nm2a.wait(v, "r", 1)
            end_phase(v, "wout")
            begin_after(v, "wout")
            v.wait_ge(x_in[0], 32)

            def post_norm(nmb, gain_row, n2):
                for k in range(KT):
                    done(nc.vector.scalar_tensor_tensor(out=f_t[:, k, :], in0=f_t[:, k, :], scalar=gains[:, gain_row, k:k + 1],
                                                        in1=rstd[:, 0:S], op0=ALU.mult, op1=ALU.mult))
                for k in range(KT):
                    settle(v)
                    nc.vector.tensor_tensor(hc[:, k, 0:S], hc[:, k, 0:S], f_t[:, k, :], ALU.add).then_inc(nmb.src, 1)
                    if k:
                        add_square(v, nmb, k - 1, n2)
                add_square(v, nmb, KT - 1, n2)
            post_norm(nm2b, G_MIX_POST, S)
            norm_tiles(nm2b, lambda k: hc[:, k, 0:S], lambda k: gains[:, G_MLP_PRE, k:k + 1], lambda k: xn2[:, k % 2, 0:S],
                       lambda k: x1l[:, k, :], lambda k: x1h[:, k, :], S)
            nc.vector.memset(f_t[:], 0.0).then_inc(f_zero, 1)
            end_phase(v, "norm2")
            begin_after(v, "norm2")
            v.drain().then_inc(ml_f, 4)
            v.wait_ge(c_tanh, 1)
            done(nc.vector.scalar_tensor_tensor(out=crow[:], in0=ctanh[:], scalar=1.0, in1=crow[:], op0=ALU.add, op1=ALU.mult))
            settle(v)
            v.drain().then_inc(mod_mul, 2)
            v.drain().then_inc(mod_ev, 1)
            v.wait_ge(f_zero, 1)
            with v.Fori(0, 4) as i:
                for j in range(16):
                    unit_done(v, U_MLP + j, i, 16)
                    if j < 8:
                        v.wait_ge(ml_relu, i * 8 + (j + 1))
                        nc.vector.scalar_tensor_tensor(out=msq[:, j % 2, :], in0=ps[:, j % 4], scalar=0.0, in1=relu[:, j % 2, :],
                                                       op0=ALU.max, op1=ALU.mult).then_inc(ml_sq, 1)
                        v.wait_ge(ml_hi, i * 8 + (j + 1))
                        nc.vector.tensor_tensor(m_l[:, j, :], msq[:, j % 2, :], m_h[:, j, :].bitcast(F32),
                                                ALU.subtract).then_inc(ml_lo, 1)
                        v.wait_ge(ml_lo, i * 8 + (j + 1))
                        nc.vector.memset(esk[:, 0:1], 0.0).then_inc(ml_f, 1)
                    else:
                        nc.vector.tensor_tensor(f_t[:, j - 8, :], ps[:, j % 4], f_t[:, j - 8, :], ALU.add).then_inc(ml_f, 1)
                    if j % 4 != 3:
                        c = j // 4 * 3 + j % 4
                        v.wait_ge(mod_in[c % MRAW], i * (16 * 12 // MRAW) + 16 * (c // MRAW + 1))
                        nc.vector.memset(tick[:, 2:3], 0.0)
                        for w in range(2):
                            v.wait_ge(mod_mul, i * 24 + (2 * c + w + 2))
                            nc.vector.memset(tick[:, w:w + 1], 0.0)
                            nc.vector.tensor_tensor_reduce(
                                out=terms[:], in0=mraw[:, c % MRAW].rearrange("p k m -> p (k m)"), in1=crow[:, w, :],
                                scale=0.5, scalar=0.0, op0=ALU.mult, op1=ALU.add,
                                accum_out=mcol[:, c, w:w + 1]).then_inc(mod_mul, 1)
                v.wait_ge(mod_mul, i * 24 + 26)
                nc.vector.tensor_tensor(mod[:, bass.ds(i * 12, 12), :], mcol,
                                        bmod[:, bass.ds(i * 12, 12)].unsqueeze(2).to_broadcast([P, 12, 2]),
                                        ALU.add).then_inc(mod_ev, 1)
            for k in range(KT):
                add_square(v, nm3a, k, S)
            v.wait_ge(mod_ev, 5)
            for l in range(2):
                for w in range(2):
                    done(nc.vector.scalar_tensor_tensor(out=mulx[:, l, w, :], in0=mod[:, l * 24 + 8:l * 24 + 16, w], scalar=1.0,
                                                        in1=gains[:, G_A + l, :], op0=ALU.add, op1=ALU.mult))
            settle(v)
            nm3a.wait(v, "r", 1)
            end_phase(v, "mlp")
            begin_after(v, "mlp")
            v.wait_ge(ctx_in, 16)
            post_norm(nm3b, G_MLP_POST, SC)

            def modulated(nm, l):
                parts = lambda k: ((0, S, mulx[:, l, 0, k:k + 1], mod[:, l * 24 + k, 0:1]),
                                   (S, SC, mulx[:, l, 1, k:k + 1], mod[:, l * 24 + k, 1:2]))

                def low(k):
                    nm.wait(v, "hi", k + 1)
                    for a, b, mul, shift in parts(k):
                        ins = nc.vector.scalar_tensor_tensor(out=x2l[:, k, a:b], in0=xn2[:, k % 2, a:b], scalar=shift,
                                                             in1=x2h[:, k, a:b].bitcast(F32), op0=ALU.add, op1=ALU.subtract)
                    ins.then_inc(nm.lo, 1)
                nm.wait(v, "r", 1)
                for k in range(KT):
                    if k >= 2:
                        nm.wait(v, "lo", k - 1)
                    for a, b, mul, shift in parts(k):
                        ins = nc.vector.scalar_tensor_tensor(out=xn2[:, k % 2, a:b], in0=hc[:, k, a:b], scalar=mul,
                                                             in1=rstd[:, a:b], op0=ALU.mult, op1=ALU.mult)
                    ins.then_inc(nm.t, 1)
                    if k:
                        low(k - 1)
                low(KT - 1)
            modulated(nm3b, 0)
            end_phase(v, "norm3")
            begin_after(v, "norm3")
            v.wait_ge(tab_in, 32)
            def rotate(head, n, ready):
                x = (a_q, a_k)[n][head[1] % 2]
                wait_head(v, ready, head, 1, 1)
                wait_head(v, "ro", head, 2, n)
                nc.vector.tensor_tensor(ropea[:, 2, :], x[:, 0:S], cos_t[:], ALU.mult).then_inc(ha["c"], 1)
                nc.vector.stream_shuffle(ropea[:, 0, :], x[:, 0:S], SHUFFLE).then_inc(ha["c"], 1)
                wait_head(v, "c", head, 6, 3 * n + 2)
                nc.vector.tensor_tensor(ropea[:, 1, :], ropea[:, 0, :], sin_t[:], ALU.mult).then_inc(ha["c"], 1)
                wait_head(v, "c", head, 6, 3 * n + 3)
                nc.vector.tensor_tensor(x[:, 0:S], ropea[:, 1, :], ropea[:, 2, :], ALU.add).then_inc(ha["ro"], 1)

            def gate_up(head):
                g = a_g[head[1] % 2]
                wait_head(v, "gt", head, 1, 1)
                nc.vector.scalar_tensor_tensor(out=g[:], in0=g[:], scalar=1.0, in1=pair(0)[:, 0:SC], op0=ALU.add,
                                               op1=ALU.mult).then_inc(ha["g"], 1)

            def output(head):
                i, c = head
                wait_head(v, "r", head, 1, 1)
                nc.vector.scalar_tensor_tensor(out=a_sq[:], in0=pair(3)[:, 0:SC], scalar=subs, in1=rstd[:], op0=ALU.mult,
                                               op1=ALU.mult).then_inc(ha["on"], 1)
                wait_head(v, "on", head, 1, 1)
                dst = o2[:, c, :] if i is None else o2[:, bass.ds(i * 2 + c, 1), :].rearrange("p a s -> p (a s)")
                nc.vector.tensor_tensor(dst, a_sq[:], a_g[c % 2][:], ALU.mult).then_inc(ha["o"], 1)

            def attend(head, more):
                i, c = head

                def mins(qt):
                    n = SC if qt < QT else C
                    wait_head(v, "t", head, 6, qt - 2)
                    for m in range(2):
                        wait_head(v, "s", head, 12, 2 * qt + m + 1)
                        cc = 2 * (qt % 3) + m
                        nc.vector.memset(tick[:, 0:1], 0.0)
                        nc.vector.tensor_tensor_reduce(
                            out=a_p[qt % 3][m][:, 0:n], in0=pair(1)[:, 0:n], in1=zero.to_broadcast([P, n]), scale=1.0,
                            scalar=3e38, op0=ALU.add, op1=ALU.min, accum_out=negm[:, cc:cc + 1]).then_inc(ha["m"], 1)

                def combine(qt):
                    n = SC if qt < QT else C
                    cc = 2 * (qt % 3)
                    wait_head(v, "e", head, 12, 2 * qt + 2)
                    nc.vector.reciprocal(rs[:, cc:cc + 2], sums[:, cc:cc + 2]).then_inc(ha["w"], 1)
                    wait_head(v, "w", head, 18, 3 * qt + 1)
                    nc.vector.tensor_tensor(wgt[:, cc:cc + 1], rs[:, cc + 1:cc + 2], lam, ALU.mult).then_inc(ha["w"], 1)
                    wait_head(v, "w", head, 18, 3 * qt + 2)
                    p0, p1 = [x[:, 0:n] for x in a_p[qt % 3]]
                    nc.vector.tensor_scalar(p1, p1, wgt[:, cc:cc + 1], None, ALU.mult).then_inc(ha["w"], 1)
                    wait_head(v, "w", head, 18, 3 * qt + 3)
                    nc.vector.scalar_tensor_tensor(out=p0, in0=p0, scalar=rs[:, cc:cc + 1],
                                                   in1=p1, op0=ALU.mult, op1=ALU.subtract).then_inc(ha["a"], 1)
                mins(0)
                mins(1)
                for qt in range(6):
                    combine(qt)
                    if qt == 0 and c > 0:
                        output((i, c - 1))
                    if qt < 4:
                        mins(qt + 2)
                if more:
                    rotate((i, c + 1), 0, "q")
                    rotate((i, c + 1), 1, "k")
                    gate_up((i, c + 1))

            rotate((None, 0), 0, "q")
            rotate((None, 0), 1, "k")
            gate_up((None, 0))
            all_heads(v, attend)
            output((None, 7))
            end_phase(v, "heads")
            begin_after(v, "heads")

            def residual(n, l, u0, wide, nm):
                v.drain().then_inc(wo_free[n], 2)
                for j in range(KT):
                    unit_done(v, u0 + j)
                    gcol = mod[:, l * 24 + 16 + j, :]
                    for w, a, b in ((0, 0, S), (1, S, SC))[0:1 + wide]:
                        src = (pair(j % 2) if wide else ps[:, j % 2])[:, a:b]
                        ins = nc.vector.scalar_tensor_tensor(out=hc[:, j, a:b], in0=src, scalar=gcol[:, w:w + 1],
                                                             in1=hc[:, j, a:b], op0=ALU.mult, op1=ALU.add)
                    ins.then_inc(wo_free[n], 1)
                    if j:
                        add_square(v, nm, j - 1, SC if wide else S)
                add_square(v, nm, KT - 1, SC if wide else S)
            for k in range(KT):
                v.wait_ge(ha["hi"], k + 1)
                nc.vector.tensor_tensor(x2l[:, k, :], o2[:, k, :], x2h[:, k, :].bitcast(F32), ALU.subtract).then_inc(ha["lo"], 1)
            residual(1, 0, U_AO, 1, nm4)
            end_phase(v, "ao")
            begin_after(v, "ao")
            modulated(nm4, 1)
            end_phase(v, "norm4")
            begin_after(v, "norm4")
            for u in range(N_B):
                if u < 10:
                    x = b_q[:, u, :] if u < 8 else b_k[:, u - 8, 0:S]
                    v.wait_ge(hb["free"], u + 1)
                    nc.vector.stream_shuffle(ropeb[:, 0, :], x, SHUFFLE)
                    done(nc.vector.tensor_tensor(ropeb[:, 2, :], x, cos_t[:], ALU.mult))
                    settle(v)
                    done(nc.vector.tensor_tensor(ropeb[:, 1, :], ropeb[:, 0, :], sin_t[:], ALU.mult))
                    settle(v)
                    done(nc.vector.tensor_tensor(x, ropeb[:, 1, :], ropeb[:, 2, :], ALU.add))
                    settle(v)
                elif u >= 12:
                    v.wait_ge(hb["gt"], u - 11)
                    nc.vector.scalar_tensor_tensor(out=b_g[:, u - 12, :], in0=b_g[:, u - 12, :], scalar=1.0, in1=ps[:, 2 * (u % 2)],
                                                   op0=ALU.add, op1=ALU.mult).then_inc(hb["free"], 1)
                if u == 13:
                    for n in range(2):
                        v.wait_ge(hb["vt"], n + 1)
                        nc.vector.tensor_copy(b_v[:, :, n * P:(n + 1) * P],
                                              pair(2)[:, 0:SC].rearrange("p (b d) -> p b d", b=6)).then_inc(hb["ve"], 1)
            v.wait_ge(tab_in, 64)
            end_phase(v, "bqkv")
            begin_after(v, "bqkv")
            attn_dve(v, A2)
            end_phase(v, "battn")
            begin_after(v, "battn")
            residual(2, 1, U_BO, 0, nm5)
            nm5.wait(v, "r", 1)
            for k in range(KT):
                nc.vector.scalar_tensor_tensor(out=xo[:, k, :], in0=hc[:, k, 0:S], scalar=gains[:, G_FINAL, k:k + 1],
                                               in1=rstd[:, 0:S], op0=ALU.mult, op1=ALU.mult).then_inc(nm5.t, 1)


def _units(w):
    import numpy as np
    k, m = w.shape
    return np.ascontiguousarray(w.reshape(k // 1024, 8, 128, m // 128, 128).transpose(3, 0, 2, 1, 4))


def _tables():
    import math
    import numpy as np
    f = np.float32
    dist = 511 - np.arange(TBL)
    d = np.maximum(dist, 0)
    df = np.maximum(d, 1).astype(f)
    large = 16 + (np.log(df / f(16)) / f(math.log(1024 / 16)) * f(16)).astype(np.int32)
    bucket = np.where(d < 16, d, np.minimum(large, BUCKETS - 1))
    onehot = np.zeros((34, TBL), f)
    onehot[bucket, np.arange(TBL)] = -1.0
    onehot[32] = np.where(dist >= 0, 0.0, BIG)
    onehot[33] = np.where((dist >= 0) & (dist < 128), 0.0, BIG)
    selrows = np.zeros((2, 16), f)
    selrows[0, 0:8] = 1.0
    selrows[1, 8:16] = 1.0
    p = np.arange(P)
    tq = np.arange(QT)[None, :] * P + p[:, None]
    cmask = np.where(np.arange(NCMP)[None, None, :] * 16 + 31 <= tq[:, :, None], 0.0, BIG).astype(f)
    band = np.where(np.abs(p[:, None] - np.arange(384)[None, :] + 128) <= 128, 0.0, BIG).astype(f)
    bm1 = np.concatenate([np.zeros((P, C), f), band], 1)
    bm0 = np.concatenate([np.zeros((P, C), f), band[:, 128:384]], 1)
    tok = np.arange(S)
    inv = f(10000.0) ** (-np.arange(0, 32, 2, dtype=f) / f(32))
    row, col = (tok // 64).astype(f), (tok % 64).astype(f)
    feat = np.arange(64)
    ang = np.where((feat < 32)[:, None], row[None, :], col[None, :]).astype(f) * inv[feat % 16][:, None]
    cos, sin = np.cos(ang).astype(f), np.sin(ang).astype(f)
    sin = np.where((feat % 32 < 16)[:, None], -sin, sin)
    return dict(ident=np.eye(P, dtype=f), onehot=onehot, selrows=selrows, cmask=cmask, bm0=bm0, bm1=bm1,
                cos=np.concatenate([cos, cos], 0), sin=np.concatenate([sin, sin], 0))


def kernel(x, norm_mix_pre, norm_mix_post, norm_mlp_pre, norm_mlp_post, w_in, cmp_pos_k, cmp_w1_k, cmp_w2_k, cmp_pos_v,
           cmp_w1_v, cmp_w2_v, attn_sinks, rel_bias, w_up_nsa, w_up_swa, w_out, w_mlp_in, w_mlp_out, c_2, ctx_2, c_ctx_2,
           w_mod_2, b_mod_2, norm_g_2, w_o_2, a_w_in_2, a_lambda_q1_2, a_lambda_k1_2, a_lambda_q2_2, a_lambda_k2_2,
           a_subln_g_2, b_w_in_2, b_sink_2, final_g_2):
    import numpy as np
    import concourse.bacc as bacc
    from concourse import mybir as mb
    from concourse.bass_utils import run_bass_kernel_spmd

    def cols(a):
        a = np.asarray(a)
        return np.moveaxis(a.reshape(a.shape[:-1] + (-1, P)), -1, 0)

    def tmajor(a):
        a = np.asarray(a)
        return a.reshape(a.shape[0], KT, P).transpose(2, 1, 0)

    def pair_heads(n_kv, rep, w):
        i = np.arange(n_kv * rep * HD).reshape(n_kv // 2, 2, rep, HD)
        return w + i.transpose(0, 2, 1, 3).reshape(-1)

    w_in = np.asarray(w_in)[0]
    qn = pair_heads(2, 4, 0)
    w_att = [_units(w_in[:, 512:768])[:, 0]]
    for w in (cmp_w1_k, cmp_w1_v):
        w_att.append(_units(np.asarray(w)[0]).reshape(4, P, KT, P))
    gcols = np.zeros((D, P), np.float32)
    gcols[:, 0:24] = w_in[:, 1280:1304]
    att_cols = np.concatenate([w_in[:, qn], w_in[:, 768:896], w_in[:, 1024:1152], w_in[:, 896:1024], w_in[:, 1152:1280],
                               gcols, w_in[:, 1304 + qn], w_in[:, 1816:1944], w_in[:, 1944:2072]], 1)
    w_att.append(_units(att_cols)[:, 0])
    ga, gb = _units(w_in[:, 2072:3096])[:, 0], _units(w_in[:, 3096:4120])[:, 0]
    up = np.concatenate([np.asarray(w_up_nsa)[0][qn], np.asarray(w_up_swa)[0][qn]], 0)
    w_g = np.stack([ga, gb], 1).reshape(N_G, P, KT, P)
    m_in = _units(np.asarray(w_mlp_in)[0])[:, 0].reshape(4, 8, P, KT, P)
    m_out = _units(np.asarray(w_mlp_out)[0]).transpose(1, 0, 2, 3, 4)
    w_mlp = np.concatenate([m_in, m_out], 1).reshape(64, P, KT, P)
    w_mod = np.asarray(w_mod_2).transpose(0, 2, 1).reshape(N_MOD, P, D)
    w_mod = np.concatenate([w_mod, w_mod[0:3]], 0)
    w_a = _units(np.asarray(a_w_in_2)[0])[:, 0].reshape(4, 8, P, KT, P).transpose(1, 0, 2, 3, 4).reshape(32, P, KT, P)
    wo = np.asarray(w_o_2)
    bw = np.asarray(b_w_in_2)[0]
    bq = pair_heads(4, 4, 0)
    w_b = _units(np.concatenate([bw[:, bq], bw[:, 1024:1536], bw[:, 1536 + bq]], 1))[:, 0]
    w2 = np.stack([np.asarray(w)[0].reshape(2, P, HD) for w in (cmp_w2_k, cmp_w2_v)], 0).transpose(2, 0, 1, 3)
    pos = np.stack([np.asarray(w)[0].reshape(16, P).T for w in (cmp_pos_k, cmp_pos_v)], 1)
    gains = np.stack([np.asarray(norm_mix_pre)[0], np.asarray(norm_mix_post)[0], np.asarray(norm_mlp_pre)[0],
                      np.asarray(norm_mlp_post)[0], np.asarray(norm_g_2)[0], np.asarray(norm_g_2)[1],
                      np.asarray(final_g_2)], 0)
    ins = dict(_tables())
    ins.update(
        xT=tmajor(np.asarray(x)[0]), ctxT=tmajor(np.asarray(ctx_2)[0]), gains=cols(gains),
        bmod=cols(np.asarray(b_mod_2)).reshape(P, 48),
        crow=np.stack([np.asarray(c_2)[0], np.asarray(c_ctx_2)], 0),
        lamv=np.stack([np.asarray(a)[0] for a in (a_lambda_q1_2, a_lambda_k1_2, a_lambda_q2_2, a_lambda_k2_2)], 1),
        subg=np.asarray(a_subln_g_2)[0].reshape(P, 1), w2=w2, pos=pos, rel_bias=np.asarray(rel_bias),
        sinks=np.concatenate([np.asarray(attn_sinks)[0], np.asarray(b_sink_2)[0]]).reshape(1, 24),
        w_att=np.concatenate(w_att, 0), w_g=w_g, w_up=_units(up)[:, 0], w_out=_units(np.asarray(w_out)[0])[:, 0], w_mlp=w_mlp, w_mod=w_mod,
        w_a=w_a, w_ao=_units(wo[0])[:, 0], w_b=w_b, w_bo=_units(wo[1][bq])[:, 0])
    nc = bacc.Bacc("TRN2", target_bir_lowering=False, num_devices=1)
    arrays, t = {}, {}
    for name, a in ins.items():
        a = np.ascontiguousarray(a)
        arrays["in_" + name] = a
        t[name] = nc.dram_tensor("in_" + name, a.shape, mb.dt.from_np(a.dtype), kind="ExternalInput").ap()
    out = nc.dram_tensor("out", (P, KT, S), mb.dt.float32, kind="ExternalOutput").ap()
    build(nc, t, out)
    r = run_bass_kernel_spmd(nc, [arrays], core_ids=[0])
    y = r.results[0]["out"]
    return np.ascontiguousarray(y.transpose(2, 1, 0).reshape(1, S, D))
```
